# Optimizing a Trainium2 kernel written in Bass

```python
import jax
import jax.numpy as jnp
from jax import lax
import numpy as np
import math
import jax, jax.numpy as jnp

D_MODEL = 2048
BATCH = 1
SEQ = 256
DEPTH = 2

N_GROUPS = 4
GROUP_WIDTH = D_MODEL // N_GROUPS
HEAD_DIM = 64
N_HEADS = GROUP_WIDTH // HEAD_DIM
D_FF = ((8 * D_MODEL + 3 * 256 - 1) // (3 * 256)) * 256

RET_CHUNK = 128
HGRN_CHUNK = 32
MLSTM_CHUNK = 64
CONV_WIDTH = 4
ROPE_BASE = 10000.0
RWKV_W_LORA = 64
RWKV_A_LORA = 64
RWKV_V_LORA = 32
RWKV_G_LORA = 128
RWKV_DECAY_SCALE = 0.6065306597126334
RWKV_LN_EPS = 64e-5
NORM_EPS = 1e-6

RET_SPLIT = (GROUP_WIDTH,) * 4
HGRN_SPLIT = (GROUP_WIDTH,) * 4
MLSTM_SPLIT = (GROUP_WIDTH,) * 4 + (N_HEADS, N_HEADS)
RWKV_SPLIT = (GROUP_WIDTH,) * 3 + (RWKV_W_LORA, RWKV_A_LORA, RWKV_G_LORA)
GROUP_COLS = (sum(RET_SPLIT), sum(HGRN_SPLIT), sum(MLSTM_SPLIT), sum(RWKV_SPLIT))
N_IN = sum(GROUP_COLS)


def split_cols(t, sizes):
    return jnp.split(t, [int(i) for i in np.cumsum(sizes)[:-1]], axis=-1)

def rms_norm(x, w):
    xf = x.astype(jnp.float32)
    y = xf * lax.rsqrt(jnp.mean(xf * xf, axis=-1, keepdims=True) + NORM_EPS)
    return (y * w.astype(jnp.float32)).astype(x.dtype)

def to_heads(t):
    return t.reshape(t.shape[0], t.shape[1], N_HEADS, HEAD_DIM).transpose(0, 2, 1, 3)

def from_heads(t):
    return t.transpose(0, 2, 1, 3)

def head_rms(t, w=None):
    y = t * lax.rsqrt(jnp.mean(t * t, axis=-1, keepdims=True) + NORM_EPS)
    if w is not None:
        y = y * w.reshape(N_HEADS, HEAD_DIM)
    return y.reshape(t.shape[0], t.shape[1], -1)

def to_chunks(t, c):
    b, h, s = t.shape[:3]
    return jnp.moveaxis(t.reshape(b, h, s // c, c, *t.shape[3:]), 2, 0)

def from_chunks(t):
    t = jnp.moveaxis(t, 0, 2)
    return t.reshape(t.shape[0], t.shape[1], -1, t.shape[-1])

def rotary(t, pos):
    half = HEAD_DIM // 2
    inv_freq = ROPE_BASE ** (-jnp.arange(half, dtype=jnp.float32) / half)
    ang = pos[:, None] * inv_freq[None, :]
    cos, sin = jnp.cos(ang), jnp.sin(ang)
    t1, t2 = t[..., :half], t[..., half:]
    return jnp.concatenate([t1 * cos - t2 * sin, t1 * sin + t2 * cos], axis=-1)

def token_shift(t):
    return jnp.pad(t, ((0, 0), (1, 0), (0, 0)))[:, :-1]

def causal_dwconv(t, w, b):
    seq = t.shape[1]
    tp = jnp.pad(t, ((0, 0), (CONV_WIDTH - 1, 0), (0, 0)))
    out = b + tp[:, 0:seq] * w[0]
    for j in range(1, CONV_WIDTH):
        out = out + tp[:, j:j + seq] * w[j]
    return out

def chunked_retention(q, k, v):
    c = RET_CHUNK
    b, h, s, d = q.shape
    log_gamma = jnp.log1p(-jnp.exp2(-5.0 - jnp.arange(h, dtype=jnp.float32)))
    idx = jnp.arange(c, dtype=jnp.float32)
    rel = idx[:, None] - idx[None, :]
    intra = jnp.where(rel >= 0, jnp.exp(log_gamma[:, None, None] * jnp.maximum(rel, 0.0)), 0.0)
    q_dec = jnp.exp(log_gamma[:, None] * (idx + 1.0))[:, :, None]
    k_dec = jnp.exp(log_gamma[:, None] * (c - 1.0 - idx))[:, :, None]
    chunk_dec = jnp.exp(log_gamma * c)[:, None, None]

    def step(state, inp):
        qc, kc, vc = inp
        scores = jnp.einsum('bhtd,bhsd->bhts', qc, kc) * intra
        out = (jnp.einsum('bhts,bhse->bhte', scores, vc)
               + jnp.einsum('bhtd,bhde->bhte', qc * q_dec, state))
        state = chunk_dec * state + jnp.einsum('bhsd,bhse->bhde', kc * k_dec, vc)
        return state, out

    _, o = lax.scan(step, jnp.zeros((b, h, d, d), q.dtype),
                    (to_chunks(q, c), to_chunks(k, c), to_chunks(v, c)))
    return from_chunks(o)

def retention_group(p):
    q, k, v, g = split_cols(p, RET_SPLIT)
    pos = jnp.arange(p.shape[1], dtype=jnp.float32)
    qh = rotary(to_heads(q), pos)
    kh = rotary(to_heads(k), pos) * HEAD_DIM ** -0.5
    o = chunked_retention(qh, kh, to_heads(v))
    return head_rms(from_heads(o)) * jax.nn.silu(g)

def chunked_hgrn2(q, k, v, log_f):
    c = HGRN_CHUNK
    b, h, s, dk = q.shape
    dv = v.shape[-1]
    causal = jnp.tril(jnp.ones((c, c), dtype=bool))[:, :, None]

    def step(state, inp):
        qc, kc, vc, gc = inp
        cum = jnp.cumsum(gc, axis=2)
        pair = jnp.where(causal,
                         jnp.exp(jnp.minimum(cum[:, :, :, None, :] - cum[:, :, None, :, :], 0.0)), 0.0)
        scores = jnp.einsum('bhtd,bhsd,bhtsd->bhts', qc, kc, pair)
        out = (jnp.einsum('bhts,bhse->bhte', scores, vc)
               + jnp.einsum('bhtd,bhde->bhte', qc * jnp.exp(cum), state))
        cum_end = cum[:, :, -1:, :]
        state = (jnp.exp(cum_end)[:, :, 0, :, None] * state
                 + jnp.einsum('bhsd,bhse->bhde', kc * jnp.exp(cum_end - cum), vc))
        return state, out

    _, o = lax.scan(step, jnp.zeros((b, h, dk, dv), q.dtype),
                    (to_chunks(q, c), to_chunks(k, c), to_chunks(v, c), to_chunks(log_f, c)))
    return from_chunks(o)

def hgrn2_group(p, lb, norm_w):
    q, f, i, g = split_cols(p, HGRN_SPLIT)
    log_f = jnp.logaddexp(jnp.log(lb), jnp.log1p(-lb) + jax.nn.log_sigmoid(f))
    k = (1.0 - lb) * jax.nn.sigmoid(-f)
    o = chunked_hgrn2(to_heads(jax.nn.silu(q)) * HEAD_DIM ** -0.5, to_heads(k), to_heads(i), to_heads(log_f))
    return head_rms(from_heads(o), norm_w) * jax.nn.sigmoid(g)

def chunked_mlstm(q, k, v, log_i, log_f):
    c = MLSTM_CHUNK
    b, h, s, dk = q.shape
    dv = v.shape[-1]
    causal = jnp.tril(jnp.ones((c, c), dtype=bool))

    def step(carry, inp):
        cmem, nvec, m = carry
        qc, kc, vc, ic, fc = inp
        cum = jnp.cumsum(fc, axis=-1)
        logd = jnp.where(causal, cum[..., :, None] - cum[..., None, :] + ic[..., None, :], -jnp.inf)
        log_inter = cum + m[..., None]
        m_t = jnp.maximum(jnp.max(logd, axis=-1), log_inter)
        scores = jnp.einsum('bhtd,bhsd->bhts', qc, kc) * jnp.exp(logd - m_t[..., None])
        w_inter = jnp.exp(log_inter - m_t)
        num = (jnp.einsum('bhts,bhse->bhte', scores, vc)
               + w_inter[..., None] * jnp.einsum('bhtd,bhde->bhte', qc, cmem))
        den = jnp.sum(scores, axis=-1) + w_inter * jnp.einsum('bhtd,bhd->bht', qc, nvec)
        h_out = num / jnp.maximum(jnp.abs(den), jnp.exp(-m_t))[..., None]
        cum_end = cum[..., -1]
        log_w = cum_end[..., None] - cum + ic
        m_new = jnp.maximum(cum_end + m, jnp.max(log_w, axis=-1))
        decay = jnp.exp(cum_end + m - m_new)
        kw = kc * jnp.exp(log_w - m_new[..., None])[..., None]
        cmem = decay[..., None, None] * cmem + jnp.einsum('bhsd,bhse->bhde', kw, vc)
        nvec = decay[..., None] * nvec + jnp.sum(kw, axis=2)
        return (cmem, nvec, m_new), h_out

    init = (jnp.zeros((b, h, dk, dv), q.dtype), jnp.zeros((b, h, dk), q.dtype), jnp.zeros((b, h), q.dtype))
    _, o = lax.scan(step, init, (to_chunks(q, c), to_chunks(k, c), to_chunks(v, c),
                                 to_chunks(log_i, c), to_chunks(log_f, c)))
    return from_chunks(o)

def mlstm_group(p, conv_w, conv_b, i_bias, f_bias, norm_w):
    q, k, v, o, ig, fg = split_cols(p, MLSTM_SPLIT)
    qk = jax.nn.silu(causal_dwconv(jnp.concatenate([q, k], axis=-1), conv_w, conv_b))
    q, k = jnp.split(qk, 2, axis=-1)
    log_i = jnp.swapaxes(ig + i_bias, 1, 2)
    log_f = jnp.swapaxes(jax.nn.log_sigmoid(fg + f_bias), 1, 2)
    hm = chunked_mlstm(to_heads(q), to_heads(k) * HEAD_DIM ** -0.5, to_heads(v), log_i, log_f)
    return jax.nn.sigmoid(o) * head_rms(from_heads(hm), norm_w)

def rwkv7_scan(r, log_w, k, v, kk, a):
    b, s, h, d = r.shape
    xs = tuple(jnp.swapaxes(t, 0, 1) for t in (r, log_w, k, v, kk, a))

    def step(state, inp):
        rt, lwt, kt, vt, kkt, at = inp
        state = (state * jnp.exp(lwt)[:, :, None, :]
                 - jnp.einsum('bhvk,bhk->bhv', state, kkt)[..., None] * (at * kkt)[:, :, None, :]
                 + vt[..., None] * kt[:, :, None, :])
        return state, jnp.einsum('bhvk,bhk->bhv', state, rt)

    _, y = lax.scan(step, jnp.zeros((b, h, d, d), r.dtype), xs)
    return jnp.swapaxes(y, 0, 1)

def rwkv7_group(p, v_first, mu, w0, w_up, a0, a_up, g_up, k_k, k_a, r_k, ln_w, ln_b, vmix):
    b, s, _ = p.shape
    p = p + (token_shift(p) - p) * mu
    r, k, v, wd, ad, gd = split_cols(p, RWKV_SPLIT)
    log_w = -RWKV_DECAY_SCALE * jax.nn.sigmoid(w0 + jnp.tanh(wd) @ w_up)
    a = jax.nn.sigmoid(a0 + ad @ a_up)
    g = jax.nn.sigmoid(gd) @ g_up
    if vmix is None:
        v_first = v
    else:
        v0, v_down, v_up = vmix
        v = v + (v_first - v) * jax.nn.sigmoid(v0 + (v @ v_down) @ v_up)

    def hs(t):
        return t.reshape(b, s, N_HEADS, HEAD_DIM)

    kk = hs(k * k_k)
    kk = kk / jnp.maximum(jnp.sqrt(jnp.sum(kk * kk, axis=-1, keepdims=True)), 1e-12)
    k = k * (1.0 + (a - 1.0) * k_a)
    y = rwkv7_scan(hs(r), hs(log_w), hs(k), hs(v), kk, hs(a))
    mean = jnp.mean(y, axis=-1, keepdims=True)
    var = jnp.mean(jnp.square(y - mean), axis=-1, keepdims=True)
    y = ((y - mean) * lax.rsqrt(var + RWKV_LN_EPS)).reshape(b, s, -1) * ln_w + ln_b
    bonus = (jnp.sum(hs(r * k * r_k), axis=-1, keepdims=True) * hs(v)).reshape(b, s, -1)
    return (y + bonus) * g, v_first

def first_inputs(seed: int = 0) -> dict:
    key = jax.random.key(seed)
    keys = jax.random.split(key, 31)
    counter = iter(range(31))
    G, H, L = GROUP_WIDTH, N_HEADS, DEPTH

    def nrm(shape, scale):
        return scale * jax.random.normal(keys[next(counter)], shape, jnp.float32)

    def gain(shape):
        return 1.0 + nrm(shape, 0.05)

    return {
        'x': nrm((BATCH, SEQ, D_MODEL), 1.0),
        'w_in': nrm((L, D_MODEL, N_IN), D_MODEL ** -0.5),
        'w_out': nrm((L, D_MODEL, D_MODEL), D_MODEL ** -0.5),
        'norm_pre_mix': gain((L, D_MODEL)),
        'norm_post_mix': gain((L, D_MODEL)),
        'norm_pre_ffn': gain((L, D_MODEL)),
        'norm_post_ffn': gain((L, D_MODEL)),
        'w_ffn_gate': nrm((L, D_MODEL, D_FF), D_MODEL ** -0.5),
        'w_ffn_up': nrm((L, D_MODEL, D_FF), D_MODEL ** -0.5),
        'w_ffn_down': nrm((L, D_FF, D_MODEL), D_FF ** -0.5),
        'hgrn_lb_logits': nrm((L, G), 0.5),
        'hgrn_norm_w': gain((L, G)),
        'mlstm_conv_w': nrm((L, CONV_WIDTH, 2 * G), CONV_WIDTH ** -0.5),
        'mlstm_conv_b': nrm((L, 2 * G), 0.02),
        'mlstm_i_bias': nrm((L, H), 0.1) - 1.0,
        'mlstm_f_bias': nrm((L, H), 0.5) + 3.0,
        'mlstm_norm_w': gain((L, G)),
        'rwkv_mu': jax.random.uniform(keys[next(counter)], (L, GROUP_COLS[3]), jnp.float32),
        'rwkv_w0': nrm((L, G), 0.5),
        'rwkv_w_up': nrm((L, RWKV_W_LORA, G), 0.5 * RWKV_W_LORA ** -0.5),
        'rwkv_a0': nrm((L, G), 0.5),
        'rwkv_a_up': nrm((L, RWKV_A_LORA, G), 0.5 * RWKV_A_LORA ** -0.5),
        'rwkv_g_up': nrm((L, RWKV_G_LORA, G), RWKV_G_LORA ** -0.5),
        'rwkv_k_k': gain((L, G)),
        'rwkv_k_a': gain((L, G)),
        'rwkv_r_k': nrm((L, G), 0.1),
        'rwkv_ln_w': gain((L, G)),
        'rwkv_ln_b': nrm((L, G), 0.02),
        'rwkv_v0': nrm((L - 1, G), 0.5),
        'rwkv_v_down': nrm((L - 1, G, RWKV_V_LORA), G ** -0.5),
        'rwkv_v_up': nrm((L - 1, RWKV_V_LORA, G), 0.5 * RWKV_V_LORA ** -0.5),
    }

def first_block(x, w_in, w_out, norm_pre_mix, norm_post_mix, norm_pre_ffn, norm_post_ffn,
              w_ffn_gate, w_ffn_up, w_ffn_down, hgrn_lb_logits, hgrn_norm_w,
              mlstm_conv_w, mlstm_conv_b, mlstm_i_bias, mlstm_f_bias, mlstm_norm_w,
              rwkv_mu, rwkv_w0, rwkv_w_up, rwkv_a0, rwkv_a_up, rwkv_g_up,
              rwkv_k_k, rwkv_k_a, rwkv_r_k, rwkv_ln_w, rwkv_ln_b,
              rwkv_v0, rwkv_v_down, rwkv_v_up):
    lb_cum = jnp.cumsum(jax.nn.softmax(hgrn_lb_logits.astype(jnp.float32), axis=0), axis=0)
    lower_bounds = lb_cum - lb_cum[0]
    v_first = None
    h = x
    for l in range(DEPTH):
        u = rms_norm(h, norm_pre_mix[l])
        p = (u @ w_in[l]).astype(jnp.float32)
        p_ret, p_hgrn, p_ml, p_rw = split_cols(p, GROUP_COLS)
        o_ret = retention_group(p_ret)
        o_hgrn = hgrn2_group(p_hgrn, lower_bounds[l], hgrn_norm_w[l])
        o_ml = mlstm_group(p_ml, mlstm_conv_w[l], mlstm_conv_b[l], mlstm_i_bias[l],
                           mlstm_f_bias[l], mlstm_norm_w[l])
        vmix = None if l == 0 else (rwkv_v0[l - 1], rwkv_v_down[l - 1], rwkv_v_up[l - 1])
        o_rw, v_first = rwkv7_group(p_rw, v_first, rwkv_mu[l], rwkv_w0[l], rwkv_w_up[l],
                                    rwkv_a0[l], rwkv_a_up[l], rwkv_g_up[l], rwkv_k_k[l],
                                    rwkv_k_a[l], rwkv_r_k[l], rwkv_ln_w[l], rwkv_ln_b[l], vmix)
        mixed = jnp.concatenate([o_ret, o_hgrn, o_ml, o_rw], axis=-1).astype(h.dtype) @ w_out[l]
        h = h + rms_norm(mixed, norm_post_mix[l])
        u = rms_norm(h, norm_pre_ffn[l])
        ffn = (jax.nn.silu(u @ w_ffn_gate[l]) * (u @ w_ffn_up[l])) @ w_ffn_down[l]
        h = h + rms_norm(ffn, norm_post_ffn[l])
    return h


DEPTH_2 = 1

A_HEADS = 16
A_HEAD_DIM = 64
A_KV_GROUPS = 4
A_REP = A_HEADS // A_KV_GROUPS
A_WIDTH = A_HEADS * A_HEAD_DIM
A_KV_WIDTH = A_KV_GROUPS * A_HEAD_DIM
CMP_BLOCK = 32
CMP_STRIDE = 16
CMP_HIDDEN = 4 * A_HEAD_DIM
SEL_BLOCK = 64
SEL_TOPK = 16
SEL_QCHUNK = 32
WIN_SIZE = 512
FORCE_BONUS = 1.0e4
B_HEADS = 8
B_HEAD_DIM = 128
B_WIDTH = B_HEADS * B_HEAD_DIM
DILATION_PATTERNS = ((128, 1), (512, 4), (2048, 16))
BAND_BLOCK = 128
ROPE_THETA = 500000.0
ROPE_FRACTION = 4
EPS = 1e-6
NEG = -1e30
IN_SIZES = (A_WIDTH,) + (A_KV_WIDTH,) * 6 + (A_HEADS * 3, A_WIDTH) + (B_WIDTH,) * 4 + (D_MODEL, D_MODEL)
N_IN_2 = sum(IN_SIZES)
IN_SPLITS = [int(s) for s in np.cumsum(IN_SIZES)[:-1]]


F32 = jnp.float32

def rms_norm_2(x, g):
    xf = x.astype(F32)
    y = xf * lax.rsqrt(jnp.mean(xf * xf, axis=-1, keepdims=True) + EPS)
    return (y * g.astype(F32)).astype(x.dtype)

def partial_rope(x, pos):
    dh = x.shape[-1]
    rot = dh // ROPE_FRACTION
    half = rot // 2
    inv = (ROPE_THETA ** (-np.arange(0, rot, 2) / rot)).astype(np.float32)
    ang = pos.astype(F32)[..., None] * inv
    ang = ang.reshape(ang.shape[:2] + (1,) * (x.ndim - 3) + (half,))
    cos, sin = jnp.cos(ang), jnp.sin(ang)
    x1 = x[..., :half].astype(F32)
    x2 = x[..., half:rot].astype(F32)
    out = jnp.concatenate([x1 * cos - x2 * sin, x2 * cos + x1 * sin, x[..., rot:].astype(F32)], axis=-1)
    return out.astype(x.dtype)

def banded_attention(q, k, v, max_dist):
    N, L, G, R, dh = q.shape
    bs = math.gcd(L, BAND_BLOCK)
    nb = L // bs
    span = max_dist + bs
    kp = jnp.pad(k, ((0, 0), (max_dist, 0), (0, 0), (0, 0)))
    vp = jnp.pad(v, ((0, 0), (max_dist, 0), (0, 0), (0, 0)))
    idx = np.arange(nb)[:, None] * bs + np.arange(span)[None, :]
    kb = kp[:, idx]
    vb = vp[:, idx]
    qb = q.reshape(N, nb, bs, G, R, dh)
    s = jnp.einsum('nbqgrd,nbkgd->nbgrqk', qb, kb, preferred_element_type=F32) * (dh ** -0.5)
    qpos = np.arange(nb)[:, None] * bs + np.arange(bs)[None, :]
    kpos = idx - max_dist
    diff = qpos[:, :, None] - kpos[:, None, :]
    mask = (diff >= 0) & (diff <= max_dist) & (kpos[:, None, :] >= 0)
    s = jnp.where(mask[None, :, None, None], s, NEG)
    lse = jax.nn.logsumexp(s, axis=-1)
    p = jnp.exp(s - lse[..., None])
    o = jnp.einsum('nbgrqk,nbkgd->nbqgrd', p.astype(vb.dtype), vb, preferred_element_type=F32)
    o = o.reshape(N, L, G, R, dh)
    lse = lse.transpose(0, 1, 4, 2, 3).reshape(N, L, G, R)
    return o, lse

def dilated_mixture(q, k, v):
    B, S, H, dh = q.shape
    outs, lses = [], []
    for w, r in DILATION_PATTERNS:
        L = S // r
        def to_cls(t):
            return t.reshape(B, L, r, H, dh).transpose(0, 2, 1, 3, 4).reshape(B * r, L, H, dh)
        o, lse = banded_attention(to_cls(q)[:, :, :, None], to_cls(k), to_cls(v), w // r)
        outs.append(o.reshape(B, r, L, H, dh).transpose(0, 2, 1, 3, 4).reshape(B, S, H, dh))
        lses.append(lse.reshape(B, r, L, H).transpose(0, 2, 1, 3).reshape(B, S, H))
    wts = jax.nn.softmax(jnp.stack(lses, axis=0), axis=0)
    return jnp.sum(wts[..., None] * jnp.stack(outs, axis=0), axis=0)

def nsa_attention(q, k_cmp, v_cmp, k_sel, v_sel, k_win, v_win, gate_logits, pos,
                  pe_ck, pe_cv, w_ck1, w_ck2, w_cv1, w_cv2):
    B, S, G, R, dh = q.shape
    scale = dh ** -0.5
    tq = np.arange(S)
    n_c = (S - CMP_BLOCK) // CMP_STRIDE + 1
    cidx = np.arange(n_c)[:, None] * CMP_STRIDE + np.arange(CMP_BLOCK)[None, :]
    cmp_end = cidx[:, -1]
    def compress(t, pe, w1, w2):
        blk = t[:, cidx] + pe[None, None, :, None, :]
        blk = blk.transpose(0, 1, 3, 2, 4).reshape(B, n_c, G, CMP_BLOCK * dh)
        return jax.nn.gelu(blk @ w1) @ w2
    kc = partial_rope(compress(k_cmp, pe_ck, w_ck1, w_ck2), pos[:, cmp_end])
    vc = compress(v_cmp, pe_cv, w_cv1, w_cv2)
    cmask = (cmp_end[None, :] <= tq[:, None])[None, :, None, None, :]
    s = jnp.einsum('bsgrd,bcgd->bsgrc', q, kc, preferred_element_type=F32) * scale
    s = jnp.where(cmask, s, NEG)
    e = jnp.exp(s - jnp.max(s, axis=-1, keepdims=True)) * cmask
    p_cmp = e / jnp.maximum(jnp.sum(e, axis=-1, keepdims=True), 1.0)
    o_cmp = jnp.einsum('bsgrc,bcgd->bsgrd', p_cmp.astype(vc.dtype), vc, preferred_element_type=F32)
    n_s = S // SEL_BLOCK
    cs = cidx[:, 0]
    ss = np.arange(n_s) * SEL_BLOCK
    overlap = np.clip(np.minimum(cs[:, None] + CMP_BLOCK, ss[None, :] + SEL_BLOCK)
                      - np.maximum(cs[:, None], ss[None, :]), 0, None).astype(np.float32) / CMP_BLOCK
    imp = jnp.einsum('bsgc,cj->bsgj', jnp.sum(p_cmp, axis=3), overlap)
    jb = np.arange(n_s)[None, :]
    cur = (tq // SEL_BLOCK)[:, None]
    valid = ss[None, :] <= tq[:, None]
    forced = (valid & ((jb == 0) | (jb == cur) | (jb == cur - 1))).astype(np.float32)
    score = jnp.where(valid[None, :, None, :], imp + FORCE_BONUS * forced[None, :, None, :], NEG)
    n_sel = min(SEL_TOPK, n_s)
    _, sel_idx = lax.top_k(score, n_sel)
    K = n_sel * SEL_BLOCK
    Qc = SEL_QCHUNK
    nq = S // Qc
    ksT = k_sel.transpose(0, 2, 1, 3)
    vsT = v_sel.transpose(0, 2, 1, 3)
    gather = jax.vmap(jax.vmap(lambda a, i: jnp.take(a, i, axis=0)))
    def sel_chunk(args):
        qb, ib, tb = args
        tok = ib[..., None] * SEL_BLOCK + jnp.arange(SEL_BLOCK, dtype=jnp.int32)
        tok = tok.reshape(B, Qc, G, K).transpose(0, 2, 1, 3)
        flat = tok.reshape(B, G, Qc * K)
        kg = gather(ksT, flat).reshape(B, G, Qc, K, dh)
        vg = gather(vsT, flat).reshape(B, G, Qc, K, dh)
        sc = jnp.einsum('bqgrd,bgqkd->bgrqk', qb, kg, preferred_element_type=F32) * scale
        m = (tok <= tb[None, None, :, None])[:, :, None]
        pr = jax.nn.softmax(jnp.where(m, sc, NEG), axis=-1)
        return jnp.einsum('bgrqk,bgqkd->bqgrd', pr.astype(vg.dtype), vg, preferred_element_type=F32)
    qc = q.reshape(B, nq, Qc, G, R, dh).transpose(1, 0, 2, 3, 4, 5)
    ic = sel_idx.reshape(B, nq, Qc, G, n_sel).transpose(1, 0, 2, 3, 4)
    tc = jnp.asarray(tq.reshape(nq, Qc), dtype=jnp.int32)
    o_sel = lax.map(sel_chunk, (qc, ic, tc)).transpose(1, 0, 2, 3, 4, 5).reshape(B, S, G, R, dh)
    o_win, _ = banded_attention(q, k_win, v_win, WIN_SIZE - 1)
    g = jax.nn.sigmoid(gate_logits.astype(F32)).reshape(B, S, G, R, 3)
    o = g[..., 0:1] * o_cmp + g[..., 1:2] * o_sel + g[..., 2:3] * o_win
    return o.reshape(B, S, G * R * dh)

def hybrid_layer(x, c, pos, w_ada, b_ada, g_pre, g_post, w_in, pe_ck, pe_cv, w_ck1, w_ck2,
                 w_cv1, w_cv2, w_br_a, w_br_b, w_out):
    B, S, D = x.shape
    ada = c @ w_ada + b_ada
    shift, scale, gate = jnp.split(ada, 3, axis=-1)
    h = rms_norm_2(x, g_pre) * (1.0 + scale[:, None, :]) + shift[:, None, :]
    proj = h @ w_in
    (qa, kc, vc, ks, vs, kw, vw, ga, za, qb, kb, vb, zb, ma, mb) = jnp.split(proj, IN_SPLITS, axis=-1)
    kv = lambda t: t.reshape(B, S, A_KV_GROUPS, A_HEAD_DIM)
    qa = partial_rope(qa.reshape(B, S, A_KV_GROUPS, A_REP, A_HEAD_DIM), pos)
    oa = nsa_attention(qa, kv(kc), kv(vc), partial_rope(kv(ks), pos), kv(vs),
                       partial_rope(kv(kw), pos), kv(vw), ga, pos,
                       pe_ck, pe_cv, w_ck1, w_ck2, w_cv1, w_cv2)
    ya = (oa * jax.nn.silu(za.astype(F32))).astype(x.dtype) @ w_br_a
    hd = lambda t: t.reshape(B, S, B_HEADS, B_HEAD_DIM)
    ob = dilated_mixture(partial_rope(hd(qb), pos), partial_rope(hd(kb), pos), hd(vb))
    ob = ob.reshape(B, S, B_WIDTH)
    yb = (ob * jax.nn.silu(zb.astype(F32))).astype(x.dtype) @ w_br_b
    merged = jax.nn.sigmoid(ma) * ya + jax.nn.sigmoid(mb) * yb
    out = merged @ w_out
    return x + (gate[:, None, :] * rms_norm_2(out, g_post)).astype(x.dtype)

def second_inputs(seed: int = 0) -> dict:
    key = jax.random.key(seed)
    ks = jax.random.split(key, 20)
    nrm = lambda k, shape, s: jax.random.normal(k, shape, dtype=F32) * s
    D = D_MODEL
    x = nrm(ks[0], (BATCH, SEQ, D), 1.0)
    c = nrm(ks[1], (BATCH, D), 1.0)
    positions = (jnp.arange(SEQ, dtype=jnp.int32)[None, :]
                 + jax.random.randint(ks[2], (BATCH, 1), 0, 4096, dtype=jnp.int32))
    return {
        'x': x,
        'c': c,
        'positions': positions,
        'w_ada': nrm(ks[3], (DEPTH_2, D, 3 * D), 0.5 * D ** -0.5),
        'b_ada': nrm(ks[4], (DEPTH_2, 3 * D), 0.01),
        'g_pre': 1.0 + nrm(ks[5], (DEPTH_2, D), 0.02),
        'g_post': 1.0 + nrm(ks[6], (DEPTH_2, D), 0.02),
        'w_in': nrm(ks[7], (DEPTH_2, D, N_IN_2), D ** -0.5),
        'pe_ck': nrm(ks[8], (DEPTH_2, CMP_BLOCK, A_HEAD_DIM), 0.02),
        'pe_cv': nrm(ks[9], (DEPTH_2, CMP_BLOCK, A_HEAD_DIM), 0.02),
        'w_ck1': nrm(ks[10], (DEPTH_2, CMP_BLOCK * A_HEAD_DIM, CMP_HIDDEN), (CMP_BLOCK * A_HEAD_DIM) ** -0.5),
        'w_ck2': nrm(ks[11], (DEPTH_2, CMP_HIDDEN, A_HEAD_DIM), CMP_HIDDEN ** -0.5),
        'w_cv1': nrm(ks[12], (DEPTH_2, CMP_BLOCK * A_HEAD_DIM, CMP_HIDDEN), (CMP_BLOCK * A_HEAD_DIM) ** -0.5),
        'w_cv2': nrm(ks[13], (DEPTH_2, CMP_HIDDEN, A_HEAD_DIM), CMP_HIDDEN ** -0.5),
        'w_br_a': nrm(ks[14], (DEPTH_2, A_WIDTH, D), A_WIDTH ** -0.5),
        'w_br_b': nrm(ks[15], (DEPTH_2, B_WIDTH, D), B_WIDTH ** -0.5),
        'w_out': nrm(ks[16], (DEPTH_2, D, D), D ** -0.5),
    }

def second_block(x, c, positions, w_ada, b_ada, g_pre, g_post, w_in, pe_ck, pe_cv, w_ck1, w_ck2,
              w_cv1, w_cv2, w_br_a, w_br_b, w_out):
    h = x
    for layer in range(DEPTH_2):
        h = hybrid_layer(h, c, positions, w_ada[layer], b_ada[layer], g_pre[layer], g_post[layer],
                         w_in[layer], pe_ck[layer], pe_cv[layer], w_ck1[layer], w_ck2[layer],
                         w_cv1[layer], w_cv2[layer], w_br_a[layer], w_br_b[layer], w_out[layer])
    return h


def setup_inputs(seed=0):
    out = dict(first_inputs(seed))
    for name, value in second_inputs(seed + 1).items():
        if name != "x":
            out[name + "_2"] = value
    return out


def reference(
    x, w_in, w_out, norm_pre_mix, norm_post_mix, norm_pre_ffn, norm_post_ffn, w_ffn_gate,
    w_ffn_up, w_ffn_down, hgrn_lb_logits, hgrn_norm_w, mlstm_conv_w, mlstm_conv_b, mlstm_i_bias,
    mlstm_f_bias, mlstm_norm_w, rwkv_mu, rwkv_w0, rwkv_w_up, rwkv_a0, rwkv_a_up, rwkv_g_up,
    rwkv_k_k, rwkv_k_a, rwkv_r_k, rwkv_ln_w, rwkv_ln_b, rwkv_v0, rwkv_v_down, rwkv_v_up, c_2,
    positions_2, w_ada_2, b_ada_2, g_pre_2, g_post_2, w_in_2, pe_ck_2, pe_cv_2, w_ck1_2,
    w_ck2_2, w_cv1_2, w_cv2_2, w_br_a_2, w_br_b_2, w_out_2,
):
    x = first_block(
        x, w_in, w_out, norm_pre_mix, norm_post_mix, norm_pre_ffn, norm_post_ffn, w_ffn_gate,
        w_ffn_up, w_ffn_down, hgrn_lb_logits, hgrn_norm_w, mlstm_conv_w, mlstm_conv_b,
        mlstm_i_bias, mlstm_f_bias, mlstm_norm_w, rwkv_mu, rwkv_w0, rwkv_w_up, rwkv_a0,
        rwkv_a_up, rwkv_g_up, rwkv_k_k, rwkv_k_a, rwkv_r_k, rwkv_ln_w, rwkv_ln_b, rwkv_v0,
        rwkv_v_down, rwkv_v_up,
    )
    return second_block(
        x, c_2, positions_2, w_ada_2, b_ada_2, g_pre_2, g_post_2, w_in_2, pe_ck_2, pe_cv_2,
        w_ck1_2, w_ck2_2, w_cv1_2, w_cv2_2, w_br_a_2, w_br_b_2, w_out_2,
    )


_drawn_inputs = setup_inputs


def setup_inputs(seed=0):
    import zlib

    import numpy as np

    out = dict(_drawn_inputs(seed))
    spreads = {}
    factors = {'mlstm_conv_b': 3.406,
     'mlstm_i_bias': 8.0,
     'rwkv_k_k': 8.0,
     'rwkv_ln_b': 4.562,
     'b_ada_2': 8.0,
     'g_pre_2': 8.0,
     'g_post_2': 25.586,
     'pe_ck_2': 32.959,
     'pe_cv_2': 64.0}
    for name, (base, spread) in spreads.items():
        noise = np.random.default_rng([zlib.crc32(name.encode()), seed]).standard_normal(out[name].shape)
        drawn = base * np.exp(spread * noise) if base else spread * noise
        out[name] = jnp.asarray(drawn.astype(out[name].dtype))
    for name, factor in factors.items():
        out[name] = (out[name] * factor).astype(out[name].dtype)
    return out
```

```python
from contextlib import ExitStack

import numpy as np
import concourse.bass as bass
from concourse import mybir

F32 = mybir.dt.float32
I32 = mybir.dt.int32
ALU = mybir.AluOpType
ACT = mybir.ActivationFunctionType
AX = mybir.AxisListType

P = 128
T = 256
D = 2048
KT = D // P
GW = 512
GT = GW // P
HD = 64
NH = GW // HD
DFF = 5632
FT = DFF // P
CW = 512
CB = CW // P
SK = 4
SLOTS = 11
NEG = -1e30
EPS = 1e-6


class Signal:

    def __init__(self, ctx, nc, name):
        self.sem = ctx.enter_context(nc.semaphore(name))
        self.base = 0
        self.seen = 0

    def up(self, times=1):
        self.seen += times
        return self.sem, 1

    def at(self, k):
        return self.sem, self.base + k

    def now(self):
        return self.sem, self.base + self.seen

    def close(self):
        self.base += self.seen
        self.seen = 0


def done(eng, ins, sig):
    ins.then_inc(*sig.up())
    eng.wait_ge(*sig.now())


class Core:

    def __init__(self, nc, ctx):
        self.nc, self.ctx = nc, ctx
        self.signals = {}
        self.loads = {}
        self.uses = [0] * SLOTS
        self.ring = self.sb("weight_ring", [P, SLOTS, SK, CW])
        self.ps = ctx.enter_context(nc.psum_tensor("ps", [P, 8, 512], F32))
        self.free = [self.sig("psum_free_0"), self.sig("psum_free_1")]
        self.landed = [ctx.enter_context(nc.semaphore(f"slab_landed_{i}")) for i in range(SLOTS)]
        self.slab_used = self.sig("slab_used")
        self.factor_ready = self.sig("factor_ready")
        self.tmp = self.sb("tmp", [P, 2, CW // P, T])
        self.act_step = self.sig("act_step")
        self.dve_step = self.sig("dve_step")
        self.pool_step = self.sig("pool_step")

    def sb(self, name, shape, dt=F32):
        return self.ctx.enter_context(self.nc.sbuf_tensor(name, shape, dt))

    def sig(self, name):
        if name not in self.signals:
            self.signals[name] = Signal(self.ctx, self.nc, name)
        return self.signals[name]

    def end(self):
        for s in self.signals.values():
            s.close()


class Load:

    def __init__(self, core, name):
        if name not in core.loads:
            core.loads[name] = [core.ctx.enter_context(core.nc.semaphore(name)), 0]
        self.rec = core.loads[name]

    def start(self, eng, dst, src):
        self.rec[1] += 16
        eng.dma_start(dst, src).then_inc(self.rec[0], 16)

    def all(self):
        return self.rec[0], self.rec[1]


class Linear:

    def __init__(self, core, mats, k, col0, cols, rhs, dst, kind="copy", func=None, src=None):
        self.core, self.mats, self.rhs, self.dst, self.kind, self.func, self.src_tiles = \
            core, mats, rhs, dst, kind, func, src
        self.kt = k // P
        self.slabs = self.kt // SK
        self.body = {16: 2, 44: 1, 8: 4}[self.kt]
        self.slots = self.body * self.slabs
        assert self.slots <= SLOTS
        self.col0 = col0
        self.m = len(mats)
        full, self.last = divmod(cols, CW)
        self.n_chunks = full * self.m
        assert not (self.m == 2 and self.last)
        self.trips = self.n_chunks // self.body
        if self.trips < 2:
            self.trips = 0
        self.looped = self.trips * self.body
        self.total = self.n_chunks + (1 if self.last else 0)
        self.prefetched = False

    def width(self, q):
        return CW if q < self.n_chunks else self.last

    def src(self, q, s, i=None):
        rows = self.mats[q % self.m][s * SK * P:(s + 1) * SK * P, :].rearrange("(k p) n -> p k n", p=P)
        col = self.col0 + q // self.m * CW
        n = self.width(q)
        if i is None:
            return rows[:, :, col:col + n]
        return rows[:, :, bass.ds(i * (self.body // self.m * CW) + col, n)]

    def load(self, sp, q, s, i=None):
        slot = (q * self.slabs + s) % self.slots
        n = self.width(q)
        sp.dma_start(self.core.ring[:, slot, :, 0:n], self.src(q, s, i)).then_inc(self.core.landed[slot], 16)

    def prefetch(self, sp):
        for g in range(min(self.slots, self.total * self.slabs)):
            self.load(sp, g // self.slabs, g % self.slabs)
        self.prefetched = True

    def run(self, after=None):
        core, nc = self.core, self.core.nc
        body, slabs, slots, trips = self.body, self.slabs, self.slots, self.trips
        used = core.slab_used
        nb = CW // P

        with nc.Block() as block:
            @block.sync
            def _(sp):
                if not self.prefetched:
                    self.prefetch(sp)
                if trips:
                    with sp.Fori(0, trips - 1) as i:
                        for g in range(slots):
                            sp.wait_ge(used.sem, i * slots + (used.base + g + 1))
                            self.load(sp, body + g // slabs, g % slabs, i)
                for g in range(max(self.looped, body) * slabs, self.total * slabs):
                    sp.wait_ge(*used.at(g - slots + 1))
                    self.load(sp, g // slabs, g % slabs)
                if after is not None:
                    for g in range(min(after.slots, after.total * after.slabs)):
                        sp.wait_ge(*used.at(self.total * slabs))
                        after.load(sp, g // after.slabs, g % after.slabs)
                    after.prefetched = True

            @block.tensor
            def _(pe):
                def chunk(q, n, i):
                    par = q % 2 if body > 1 else 0
                    turn = q // 2 if body > 1 else q
                    free = core.free[par]
                    per = max(body // 2, 1)
                    pe.wait_ge(free.sem, free.base + turn + 1 + (0 if i is None else i * per))
                    for s in range(slabs):
                        slot = (q * slabs + s) % slots
                        uses = core.uses[slot] + 1 + (q * slabs + s) // slots
                        pe.wait_ge(core.landed[slot], 16 * uses + (0 if i is None else i * 16))
                        for k in range(SK):
                            kk = s * SK + k
                            if self.kind == "row":
                                mm = nc.tensor.matmul(core.ps[0:1, nb * par, 0:n], self.rhs(kk), core.ring[:, slot, k, 0:n],
                                                      start=(kk == 0), stop=(kk == self.kt - 1))
                                continue
                            for m in range(n // P):
                                mm = nc.tensor.matmul(core.ps[:, nb * par + m, 0:T],
                                                      core.ring[:, slot, k, m * P:(m + 1) * P],
                                                      self.rhs(kk), start=(kk == 0), stop=(kk == self.kt - 1))
                        mm.then_inc(used.sem, 1)

                if trips:
                    with pe.Fori(0, trips) as i:
                        for q in range(body):
                            chunk(q, CW, i)
                for q in range(self.looped, self.total):
                    chunk(q, self.width(q), None)

            @block.scalar
            def _(act):
                act.sem_inc(core.free[0].sem, 1)
                act.sem_inc(core.free[1].sem, 1)

                def chunk(q, i):
                    par = q % 2 if body > 1 else 0
                    n = self.width(q) // P
                    ready = used.base + (q + 1) * slabs + (0 if i is None else i * slots)
                    at = q // self.m * nb + (0 if i is None else i * (body // self.m * nb))
                    ps = core.ps[:, nb * par:nb * par + n, 0:T]
                    tmp = core.tmp[:, par if self.kind == "mul" else 0, 0:n, :]
                    if self.kind == "row":
                        act.wait_ge(used.sem, ready)
                        nc.scalar.activation(self.dst[:, bass.ds(at * P, CW)], core.ps[0:1, nb * par, :], ACT.Copy)\
                            .then_inc(core.free[par].sem, 1)
                    elif self.kind == "copy":
                        act.wait_ge(used.sem, ready)
                        nc.scalar.activation(self.dst[:, bass.ds(at, n), :], ps, ACT.Copy).then_inc(core.free[par].sem, 1)
                    elif self.kind == "mul":
                        turn = q // 2 + (0 if i is None else i * max(body // 2, 1))
                        act.wait_ge(used.sem, ready)
                        act.wait_ge(core.free[par].sem, core.free[par].base + 1 + turn)
                        nc.scalar.activation(tmp, ps, self.func).then_inc(core.factor_ready.sem, 1)
                    elif q % 2 == 0:
                        turn = q // 2 + (0 if i is None else i)
                        act.wait_ge(used.sem, ready)
                        act.wait_ge(core.free[1].sem, core.free[1].base + 1 + turn)
                        nc.scalar.activation(tmp, ps, ACT.Silu).then_inc(core.free[0].sem, 1)

                if trips:
                    with act.Fori(0, trips) as i:
                        for q in range(body):
                            chunk(q, i)
                for q in range(self.looped, self.total):
                    chunk(q, None)

            @block.vector
            def _(dve):
                if self.kind in ("copy", "row"):
                    return

                def chunk(q, i):
                    par = q % 2 if body > 1 else 0
                    n = self.width(q) // P
                    at = q // self.m * nb + (0 if i is None else i * (body // self.m * nb))
                    dst = self.dst[:, bass.ds(at, n), :]
                    if self.kind == "mul":
                        dve.wait_ge(core.factor_ready.sem,
                                    core.factor_ready.base + q + 1 + (0 if i is None else i * body))
                        nc.vector.tensor_tensor(dst, self.src_tiles[:, bass.ds(at, n), :],
                                                core.tmp[:, par, 0:n, :], ALU.mult).then_inc(core.free[par].sem, 1)
                    elif q % 2 == 1:
                        dve.wait_ge(core.free[0].sem, core.free[0].base + q // 2 + 2 + (0 if i is None else i))
                        dve.wait_ge(used.sem, used.base + (q + 1) * slabs + (0 if i is None else i * slots))
                        nc.vector.tensor_tensor(dst, core.tmp[:, 0, 0:n, :], core.ps[:, nb:nb + n, 0:T], ALU.mult)\
                            .then_inc(core.free[1].sem, 1)

                if trips:
                    with dve.Fori(0, trips) as i:
                        for q in range(body):
                            chunk(q, i)
                for q in range(self.looped, self.total):
                    chunk(q, None)

        per_par = [0, 0]
        for q in range(self.total):
            per_par[q % 2 if body > 1 else 0] += 1
        core.free[0].base += per_par[0] + 1
        core.free[1].base += per_par[1] + 1
        used.base += self.total * slabs
        if self.kind == "mul":
            core.factor_ready.base += self.total
        for g in range(self.total * slabs):
            core.uses[g % slots] += 1


LEVELS = 8


def constants():
    i = np.arange(P)
    t = np.arange(T)
    head = i // HD
    c = {}
    c["ident"] = np.eye(P)
    c["head_ones"] = (head[:, None] == head[None, :])
    c["ones"] = np.ones((P, P))

    def rotation(width, rot):
        r = np.zeros((P, P))
        for o in range(P):
            d, half = o % width, rot // 2
            if d < half:
                r[o + half, o] = -1
            elif d < rot:
                r[o - half, o] = 1
        return r

    c["rot_ret"] = rotation(HD, HD)
    c["rot_a"] = rotation(HD, 16)
    c["rot_b"] = rotation(P, 32)
    for g in range(2):
        dup = (i[:, None] == g * HD + i[None, :] % HD).astype(np.float64)
        c[f"dup{g}"] = dup
        c[f"rot_dup{g}"] = dup @ rotation(HD, 16)
    c["eye_pair"] = (i[:, None] % HD == np.arange(HD)[None, :])
    small = list(c)
    inv = (10000.0 ** (-np.arange(HD // 2, dtype=np.float32) / np.float32(HD // 2))).astype(np.float32)
    ang = (t.astype(np.float32)[None, :] * inv[i % (HD // 2)][:, None]).astype(np.float32)
    c["ret_cos_sin"] = np.concatenate([np.cos(ang), np.sin(ang)], 1)
    lg = np.log1p(-np.exp2(-5.0 - np.arange(NH)))
    low = np.tile(t[None, :], (P, 1)) - i[:, None]
    causal = (low >= 0)
    dec = np.where(causal[None], np.exp(lg[:, None, None] * np.maximum(low, 0)[None]), 0) * HD ** -0.5
    c["ret_decay"] = np.concatenate([dec, dec[:, :, :P]], 2).transpose(1, 0, 2).reshape(P, -1)
    cm = causal * HD ** -0.5
    c["mlstm_mask"] = np.concatenate([cm, cm[:, :P]], 1)
    s, u = i[:, None], i[None, :]
    levels = [s == u]
    for l in range(LEVELS - 1):
        b = 1 << l
        levels.append((s // (2 * b) == u // (2 * b)) & (s // b % 2 == 0) & (u // b % 2 == 1))
    c["hgrn_levels"] = np.stack(levels, 1).reshape(P, -1)
    chunk = s // 64 == u // 64
    b8 = s // 8 == u // 8
    c["low8"] = chunk & b8 & (u < s)
    c["up8"] = chunk & b8 & (u > s)
    c["low_off"] = chunk & ~b8 & (u < s)
    c["up_strict"] = chunk & (u > s)
    c["up_incl"] = chunk & (u >= s)
    c["up_incl_neg"] = -1.0 * c["up_incl"]
    c["chunk_starts"] = np.tile((t % 64 != 0)[None, :], (P, 1))
    for tt in range(2):
        q = i[:, None] + tt * P
        k = t[None, :]
        c[f"causal{tt}"] = np.where(k <= q, 0, NEG)
        d = q - k
        n = ((d >= 0) & (d <= 128)) * 1.0 + ((d >= 0) & (d % 4 == 0)) + ((d >= 0) & (d % 16 == 0))
        c[f"dilated{tt}"] = np.where(n > 0, np.log(np.maximum(n, 1)), NEG)
        e = np.arange(15)[None, :] * 16 + 31
        c[f"cmp{tt}"] = np.concatenate([np.where(e <= q, 0, NEG), (e <= q) * 1.0], 1)

    def inv2(width):
        rot = width // 4
        v = (500000.0 ** (-np.arange(0, rot, 2) / rot)).astype(np.float32)
        out = np.zeros(P, np.float32)
        for o in range(P):
            if o % width < rot:
                out[o] = v[o % width % (rot // 2)]
        return out

    c["inv_freq"] = np.stack([inv2(HD), inv2(P)], 1)
    c = {k: np.ascontiguousarray(v, dtype=np.float32) for k, v in c.items()}
    at, n = {}, 0
    for k, v in c.items():
        at[k] = (n, v.shape[1])
        n += v.shape[1]
    return np.concatenate(list(c.values()), 1), at, sum(c[k].shape[1] for k in small), small


N_ARENA = 68
P_AT, MIX_AT, S_AT = 0, 16, 32


LAYER_VECTORS = dict(norm_pre_mix=16, norm_post_mix=16, norm_pre_ffn=16, norm_post_ffn=16, hgrn_norm_w=4, mlstm_conv_w=32,
                     mlstm_conv_b=8, mlstm_norm_w=4, rwkv_mu=14, rwkv_w0=4, rwkv_a0=4, rwkv_k_k=4, rwkv_k_a=4, rwkv_r_k=4,
                     rwkv_ln_w=4, rwkv_ln_b=4, rwkv_v0=4, mlstm_i_bias=1, mlstm_f_bias=1, hgrn_lb_logits=4)
LAYER_N = sum(LAYER_VECTORS.values()) + 1
SECOND_VECTORS = dict(b_ada_2=48, g_pre_2=16, g_post_2=16, c_2=16)


def vector_columns(names):
    at, out = 0, {}
    for name, n in names.items():
        out[name] = (at, n)
        at += n
    return out


class Model(Core):
    def __init__(self, nc, ctx, consts):
        super().__init__(nc, ctx)
        _, self.const_at, n_small, self.small = constants()
        self.consts = consts
        self.h = self.sb("h", [P, KT, T])
        self.u = self.sb("u", [P, KT, T])
        self.arena = self.sb("arena", [P, N_ARENA, T])
        self.v_first = self.sb("v_first", [P, GT, T])
        self.par = self.sb("vectors", [P, 2, LAYER_N])
        self.bounds = self.sb("bounds", [P, 3, GT])
        self.chunk_w = self.sb("chunk_w", [P, 4, 4])
        self.gates = self.tmp[0:NH, 1, 0:2, :]
        self.cs = self.sb("small_consts", [P, n_small])

    def const(self, name):
        o, n = self.const_at[name]
        return self.cs[:, o:o + n]

    def const_dram(self, name):
        o, n = self.const_at[name]
        return self.consts[:, o:o + n]

    def a(self, t0, n=1):
        return self.arena[:, t0:t0 + n, :]

    def flat(self, t0, n):
        assert n <= (N_ARENA - t0) * T
        return self.arena[:, :, :].rearrange("p a b -> p (a b)")[:, t0 * T:t0 * T + n]

    def banks(self, b, n):
        return self.ps[:, b:b + n, :].rearrange("p a b -> p (a b)")


def bcast(ap, n):
    return ap.unsqueeze(1).broadcast_to([ap.shape[0], n, ap.shape[-1]])


def rms_stage(m, src, weight, dst, add_to=None, prefetch=None, scratch=S_AT, shift=None):
    nc = m.nc
    sq = m.a(scratch, KT)
    inv = m.tmp[:, 1, 0, :]
    squares = m.sig("squares")
    sums = m.sig("mean_sums")
    var = m.sig("variance")
    root = m.sig("root")
    with nc.Block() as block:
        if prefetch is not None:
            @block.sync
            def _(sp):
                prefetch.prefetch(sp)

        @block.scalar
        def _(act):
            for q in range(4):
                nc.scalar.activation(sq[:, 4 * q:4 * q + 4, :], src[:, 4 * q:4 * q + 4, :], ACT.Square)\
                    .then_inc(*squares.up())
            act.wait_ge(*var.at(1))
            nc.scalar.activation(inv, inv, ACT.Sqrt).then_inc(*root.up())

        @block.tensor
        def _(pe):
            for k in range(KT):
                if k % 4 == 0:
                    pe.wait_ge(*squares.at(k // 4 + 1))
                mm = nc.tensor.matmul(m.ps[:, 0, 0:T], m.const("ones"), sq[:, k, :], start=(k == 0), stop=(k == KT - 1))
            mm.then_inc(*sums.up())

        @block.vector
        def _(dve):
            dve.wait_ge(*sums.at(1))
            nc.vector.tensor_scalar(inv, m.ps[:, 0, 0:T], 1.0 / D, EPS, ALU.mult, ALU.add).then_inc(*var.up())
            dve.wait_ge(*root.at(1))
            done(dve, nc.vector.reciprocal(inv, inv), m.dve_step)
            for k in range(KT):
                to = dst if add_to is None else sq
                last = nc.vector.scalar_tensor_tensor(to[:, k, :], src[:, k, :], weight[:, k:k + 1], inv, ALU.mult, ALU.mult)
            if add_to is not None:
                done(dve, last, m.dve_step)
                nc.vector.tensor_tensor(add_to[:, :, :], add_to[:, :, :], sq, ALU.add)
            if shift is not None:
                done(dve, last, m.dve_step)
                for k in range(KT):
                    nc.vector.tensor_scalar(dst[:, k, :], dst[:, k, :], shift[:, k:k + 1], None, ALU.add)
    m.end()


def head_norm_stage(m, o, dst, gate, weight=None, bias=None, bonus=None, eps=EPS, center=False):
    nc = m.nc
    sq = m.flat(S_AT, GT * T)
    inv = m.flat(S_AT + 4, GT * T)
    of = o.rearrange("p a b -> p (a b)")
    squares, sums, var, root = m.sig("squares"), m.sig("mean_sums"), m.sig("variance"), m.sig("root")
    centred, mean = m.sig("centred"), m.sig("head_mean")
    with nc.Block() as block:
        @block.tensor
        def _(pe):
            if center:
                for b in range(2):
                    mm = nc.tensor.matmul(m.ps[:, 2 + b, :], m.const("head_ones"), of[:, b * 512:(b + 1) * 512], start=True, stop=True)
                mm.then_inc(*mean.up())
            pe.wait_ge(*squares.at(1))
            for b in range(2):
                mm = nc.tensor.matmul(m.ps[:, b, :], m.const("head_ones"), sq[:, b * 512:(b + 1) * 512], start=True, stop=True)
            mm.then_inc(*sums.up())

        @block.scalar
        def _(act):
            if center:
                act.wait_ge(*centred.at(1))
            nc.scalar.activation(sq, of, ACT.Square).then_inc(*squares.up())
            act.wait_ge(*var.at(1))
            nc.scalar.activation(inv, inv, ACT.Sqrt).then_inc(*root.up())

        @block.vector
        def _(dve):
            if center:
                dve.wait_ge(*mean.at(1))
                nc.vector.scalar_tensor_tensor(of, m.banks(2, 2), -1.0 / HD, of, ALU.mult, ALU.add).then_inc(*centred.up())
            dve.wait_ge(*sums.at(1))
            nc.vector.tensor_scalar(inv, m.banks(0, 2), 1.0 / HD, eps, ALU.mult, ALU.add).then_inc(*var.up())
            dve.wait_ge(*root.at(1))
            done(dve, nc.vector.reciprocal(inv, inv), m.dve_step)
            done(dve, nc.vector.tensor_tensor(of, of, inv, ALU.mult), m.dve_step)
            if weight is not None:
                for j in range(GT):
                    if bias is None:
                        last = nc.vector.tensor_scalar(o[:, j, :], o[:, j, :], weight[:, j:j + 1], None, ALU.mult)
                    else:
                        last = nc.vector.tensor_scalar(o[:, j, :], o[:, j, :], weight[:, j:j + 1], bias[:, j:j + 1], ALU.mult, ALU.add)
                done(dve, last, m.dve_step)
            if bonus is not None:
                done(dve, nc.vector.tensor_tensor(o, o, bonus, ALU.add), m.dve_step)
            nc.vector.tensor_tensor(dst, o, gate, ALU.mult)
    m.end()


def decayed_product(pe, m, h, k, q, out):
    j, r = h // 2, slice(HD * (h % 2), HD * (h % 2) + HD)
    m.nc.tensor.matmul(out[:, 0:T], k[r, j, 0:P], q[r, j, :], start=True, stop=True)
    return m.nc.tensor.matmul(out[:, T:T + P], k[r, j, P:T], q[r, j, P:T], start=True, stop=True)


def weighted_values(pe, m, h, v, w, out, first=True):
    r = slice(HD * (h % 2), HD * (h % 2) + HD)
    m.nc.tensor.matmul(out[r, 0:T], v(0), w[:, 0:T], start=first, stop=False)
    return m.nc.tensor.matmul(out[r, P:T], v(1), w[:, T:T + P], start=False, stop=True)


def transpose_values(pe, m, v, bank):
    for tt in range(2):
        for j in range(GT):
            mm = m.nc.tensor.transpose(m.ps[:, bank + tt, j * P:(j + 1) * P], v[:, j, tt * P:(tt + 1) * P], m.const("ident"))
    return mm


def retention_stage(m):
    nc = m.nc
    q, k, v, g = (m.a(P_AT + 4 * n, GT) for n in range(4))
    qk = m.flat(P_AT, 8 * T)
    decay = m.flat(S_AT, NH * 384).rearrange("p (h n) -> p h n", h=NH)
    cs = m.flat(S_AT + 12, 2 * T)
    rot = m.flat(S_AT + 14, 8 * T)
    vt = m.flat(S_AT + 22, 2 * GW).rearrange("p (a b) -> p a b", a=2)
    pr = m.flat(S_AT + 26, 2 * 384).rearrange("p (a b) -> p a b", a=2)
    tables = Load(m, "tables_landed")
    rotated, scaled, qk_ready = m.sig("rotated"), m.sig("scaled"), m.sig("qk_ready")
    v_turned, v_ready = m.sig("v_turned"), m.sig("v_ready")
    scores, weights, o_done = m.sig("scores"), m.sig("weights"), m.sig("o_done")
    with nc.Block() as block:
        @block.sync
        def _(sp):
            tables.start(sp, cs, m.const_dram("ret_cos_sin"))
            tables.start(sp, decay, m.const_dram("ret_decay").rearrange("p (h n) -> p h n", h=NH))

        @block.tensor
        def _(pe):
            for b in range(4):
                mm = nc.tensor.matmul(m.ps[:, b, :], m.const("rot_ret"), qk[:, b * 512:(b + 1) * 512], start=True, stop=True)
            mm.then_inc(*rotated.up())
            transpose_values(pe, m, v, 4).then_inc(*v_turned.up())
            pe.wait_ge(*qk_ready.at(1))
            pe.wait_ge(*v_ready.at(1))
            for h in range(NH + 1):
                if h < NH:
                    if h >= 2:
                        pe.wait_ge(*weights.at(h - 1))
                    decayed_product(pe, m, h, k, q, m.ps[:, 6 + h % 2, :]).then_inc(*scores.up())
                if h >= 1:
                    g_ = h - 1
                    pe.wait_ge(*weights.at(h))
                    weighted_values(pe, m, g_, lambda st: vt[:, st, g_ * HD:(g_ + 1) * HD], pr[:, g_ % 2, :],
                                    m.ps[:, g_ // 4, (g_ // 2 % 2) * T:(g_ // 2 % 2) * T + T]).then_inc(*o_done.up())

        @block.gpsimd
        def _(pool):
            pool.wait_ge(*tables.all())
            pool.wait_ge(*rotated.at(1))
            nc.gpsimd.tensor_tensor(m.a(P_AT, 8), m.a(P_AT, 8), bcast(cs[:, 0:T], 8), ALU.mult).then_inc(*scaled.up())

        @block.scalar
        def _(act):
            nc.scalar.activation(g, g, ACT.Silu)
            act.wait_ge(*v_turned.at(1))
            nc.scalar.activation(vt, m.ps[:, 4:6, :], ACT.Copy).then_inc(*v_ready.up())
            act.wait_ge(*o_done.at(NH))
            nc.scalar.activation(q, m.banks(0, 2).rearrange("p (a b) -> p a b", b=T), ACT.Copy)

        @block.vector
        def _(dve):
            dve.wait_ge(*rotated.at(1))
            dve.wait_ge(*tables.all())
            done(dve, nc.vector.tensor_tensor(rot.rearrange("p (a b) -> p a b", b=T),
                                              m.banks(0, 4).rearrange("p (a b) -> p a b", b=T),
                                              bcast(cs[:, T:2 * T], 8), ALU.mult), m.dve_step)
            dve.wait_ge(*scaled.at(1))
            nc.vector.tensor_tensor(qk, qk, rot, ALU.add).then_inc(*qk_ready.up())
            for h in range(NH):
                dve.wait_ge(*scores.at(h + 1))
                if h >= 2:
                    dve.wait_ge(*o_done.at(h - 1))
                nc.vector.tensor_tensor(pr[:, h % 2, :], m.ps[:, 6 + h % 2, 0:384], decay[:, h, :], ALU.mult)\
                    .then_inc(*weights.up())
    m.end()


def log_one_plus_exp(act, m, x, out, log_part):
    done(act, m.nc.scalar.activation(out, x, ACT.Abs), m.act_step)
    done(act, m.nc.scalar.activation(out, out, ACT.Exp, scale=-1.0), m.act_step)
    m.nc.scalar.activation(out, out, ACT.Ln, bias=1.0).then_inc(*log_part.up())


def mlstm_stage(m, par, gates):
    nc = m.nc
    q, k, v, o = (m.a(P_AT + 4 * n, GT) for n in range(4))
    qk = m.a(P_AT, 8)
    acc = m.a(S_AT, 8)
    mask = m.flat(S_AT + 8, 384)
    vt = m.flat(S_AT + 10, 2 * GW).rearrange("p (a b) -> p a b", a=2)
    ex = m.flat(S_AT + 14, NH * 384).rearrange("p (h n) -> p h n", h=NH)
    exf = m.flat(S_AT + 14, NH * 384)
    pr = m.flat(S_AT + 26, 2 * 384).rearrange("p (a b) -> p a b", a=2)
    enm = m.flat(S_AT + 29, GT * T)
    rows = m.flat(S_AT + 33, 3 * T).rearrange("p (a b) -> p a b", b=T)
    log_i, log_f = gates[0:NH, 0, :], gates[0:NH, 1, :]
    lt, cum, gain = (rows[0:NH, n, :] for n in range(3))
    at = m.tmp[:, 0, 0, 0:2 * NH].rearrange("p (a b) -> p a b", a=2)
    run_m = m.tmp[0:NH, 0, 1, :]
    tables = Load(m, "tables_landed")
    conv, qk_ready = m.sig("conv_done"), m.sig("qk_ready")
    v_turned, v_ready = m.sig("v_turned"), m.sig("v_ready")
    biased, log_part, den_ready = m.sig("gates_biased"), m.sig("log_part"), m.sig("den_ready")
    gates_ready, gates_spread, gates_back = m.sig("gates_ready"), m.sig("gates_spread"), m.sig("gates_back")
    distance, decay, masked = m.sig("distance"), m.sig("decay_ready"), m.sig("decay_masked")
    scores, weights, o_done, least = m.sig("scores"), m.sig("weights"), m.sig("o_done"), m.sig("least_ready")
    ones = m.const("ones")
    with nc.Block() as block:
        @block.sync
        def _(sp):
            tables.start(sp, mask, m.const_dram("mlstm_mask"))

        @block.tensor
        def _(pe):
            transpose_values(pe, m, v, 6).then_inc(*v_turned.up())
            pe.wait_ge(*gates_ready.at(1))
            for tt in range(2):
                nc.tensor.transpose(m.ps[:, 4, tt * NH:tt * NH + NH], gain[:, tt * P:(tt + 1) * P], m.const("ident")[0:NH, 0:NH])\
                    .then_inc(*gates_spread.up())
            for h in range(NH):
                mm = nc.tensor.matmul(m.ps[:, h // 2, h % 2 * T:h % 2 * T + T],
                                      m.const("ident")[0:NH, h:h + 1].broadcast_to([NH, P]), run_m, start=True, stop=True)
            mm.then_inc(*gates_spread.up())
            pe.wait_ge(*gates_back.at(1))
            for h in range(NH):
                mm = nc.tensor.matmul(m.ps[HD * (h % 2):HD * (h % 2) + HD, 4 + h // 4, h // 2 % 2 * T:h // 2 % 2 * T + T],
                                      m.const("ident")[0:NH, h:h + 1].broadcast_to([NH, HD]), log_i, start=True, stop=True)
            mm.then_inc(*gates_spread.up())
            pe.wait_ge(*v_ready.at(1))
            pe.wait_ge(*qk_ready.at(1))
            for h in range(NH + 1):
                if h < NH:
                    if h >= 2:
                        pe.wait_ge(*weights.at(h - 1))
                    decayed_product(pe, m, h, k, q, m.ps[:, 6 + h % 2, :]).then_inc(*scores.up())
                if h >= 1:
                    g = h - 1
                    pe.wait_ge(*weights.at(h))
                    half = (g // 2 % 2) * T
                    weighted_values(pe, m, g, lambda st: vt[:, st, g * HD:(g + 1) * HD], pr[:, g % 2, :],
                                    m.ps[:, g // 4, half:half + T])
                    weighted_values(pe, m, g, lambda st: ones[:, 0:HD], pr[:, g % 2, :],
                                    m.ps[:, 2 + g // 4, half:half + T]).then_inc(*o_done.up())

        @block.gpsimd
        def _(pool):
            pool.wait_ge(*tables.all())
            pool.wait_ge(*decay.at(1))
            nc.gpsimd.tensor_tensor(ex, ex, bcast(mask, NH), ALU.mult).then_inc(*masked.up())

        @block.scalar
        def _(act):
            act.wait_ge(*v_turned.at(1))
            nc.scalar.activation(vt, m.ps[:, 6:8, :], ACT.Copy).then_inc(*v_ready.up())
            act.wait_ge(*biased.at(1))
            log_one_plus_exp(act, m, log_f, lt, log_part)
            act.wait_ge(*distance.at(1))
            nc.scalar.activation(exf, exf, ACT.Exp, scale=-1.0).then_inc(*decay.up())
            act.wait_ge(*gates_spread.at(4))
            nc.scalar.activation(enm, m.banks(4, 2), ACT.Exp, scale=-1.0).then_inc(*least.up())
            act.wait_ge(*conv.at(1))
            nc.scalar.activation(qk, acc, ACT.Silu).then_inc(*qk_ready.up())
            nc.scalar.activation(o, o, ACT.Sigmoid)
            act.wait_ge(*o_done.at(NH))
            nc.scalar.activation(acc[:, 0:GT, :], m.banks(2, 2).rearrange("p (a b) -> p a b", b=T), ACT.Abs).then_inc(*den_ready.up())

        @block.vector
        def _(dve):
            step = m.dve_step
            nc.vector.tensor_scalar(log_i, log_i, par["i_bias"][0:NH, :], None, ALU.add)
            done(dve, nc.vector.tensor_scalar(log_f, log_f, par["f_bias"][0:NH, :], None, ALU.add), biased)
            dve.wait_ge(*log_part.at(1))
            done(dve, nc.vector.scalar_tensor_tensor(log_f, log_f, 0.0, lt, ALU.min, ALU.subtract), step)
            done(dve, nc.vector.tensor_tensor_scan(cum, m.const("ones")[0:NH, 0:1].broadcast_to([NH, T]), log_f, 0.0,
                                                   ALU.mult, ALU.add), step)
            done(dve, nc.vector.tensor_tensor(gain, log_i, cum, ALU.subtract), step)
            done(dve, nc.vector.tensor_tensor_scan(run_m, gain, gain, 0.0, ALU.max, ALU.max), step)
            nc.vector.tensor_tensor(log_i, cum, run_m, ALU.add).then_inc(*gates_ready.up())
            dve.wait_ge(*gates_spread.at(2))
            done(dve, nc.vector.tensor_copy(at, m.ps[:, 4, 0:2 * NH].rearrange("p (a b) -> p a b", a=2)), gates_back)
            dve.wait_ge(*gates_spread.at(3))
            for h in range(NH):
                bank, half = h // 2, h % 2 * T
                nc.vector.tensor_scalar(ex[:, h, 0:T], m.ps[:, bank, half:half + T], at[:, 0, h:h + 1], 0.0, ALU.subtract, ALU.max)
                last = nc.vector.tensor_scalar(ex[:, h, T:T + P], m.ps[:, bank, half + P:half + T], at[:, 1, h:h + 1], 0.0,
                                               ALU.subtract, ALU.max)
            last.then_inc(*distance.up())
            cw, cb = par["conv_w"], par["conv_b"]
            for j in range(8):
                last = nc.vector.tensor_scalar(acc[:, j, :], qk[:, j, :], cw[:, 3 * 8 + j:3 * 8 + j + 1], cb[:, j:j + 1],
                                               ALU.mult, ALU.add)
            for back in range(1, 4):
                done(dve, last, step)
                for j in range(8):
                    w = cw[:, (3 - back) * 8 + j:(3 - back) * 8 + j + 1]
                    last = nc.vector.scalar_tensor_tensor(acc[:, j, back:T], qk[:, j, 0:T - back], w, acc[:, j, back:T],
                                                          ALU.mult, ALU.add)
            last.then_inc(*conv.up())
            dve.wait_ge(*masked.at(1))
            for h in range(NH):
                dve.wait_ge(*scores.at(h + 1))
                if h >= 2:
                    dve.wait_ge(*o_done.at(h - 1))
                nc.vector.tensor_tensor(pr[:, h % 2, :], m.ps[:, 6 + h % 2, 0:384], ex[:, h, :], ALU.mult)\
                    .then_inc(*weights.up())
            dve.wait_ge(*o_done.at(NH))
            dve.wait_ge(*least.at(1))
            dve.wait_ge(*den_ready.at(1))
            done(dve, nc.vector.tensor_tensor(enm, m.flat(S_AT, GT * T), enm, ALU.max), step)
            done(dve, nc.vector.reciprocal(enm, enm), step)
            nc.vector.tensor_tensor(m.flat(P_AT, GT * T), m.banks(0, 2), enm, ALU.mult)
    m.end()


def hgrn_stage(m, par, first):
    nc = m.nc
    q, f, v, g = (m.a(P_AT + 4 * n, GT) for n in range(4))
    k = m.a(S_AT, GT)
    levels = m.flat(S_AT + 4, LEVELS * P)
    vt = m.flat(P_AT + 8, 2 * GW).rearrange("p (a b) -> p a b", a=2)
    pr = m.flat(S_AT + 8, 2 * 384).rearrange("p (a b) -> p a b", a=2)
    prod = m.flat(S_AT + 11, LEVELS * T)
    dq, dk = m.a(S_AT + 19, LEVELS), m.a(S_AT + 27, LEVELS)
    lt = m.a(S_AT + 19, GT)
    ls = m.a(S_AT + 23, GT)
    tables = Load(m, "tables_landed")
    v_turned, v_ready, k_gate, log_ready = m.sig("v_turned"), m.sig("v_ready"), m.sig("k_gate"), m.sig("log_f_ready")
    log_part, odds_ready = m.sig("log_part"), m.sig("odds_ready")
    distance, decay, damped_q, damped_k = m.sig("distance"), m.sig("decay_ready"), m.sig("damped_q"), m.sig("damped_k")
    scores, summed, weights, off_done, o_done = (m.sig(n) for n in ("scores", "scores_masked", "weights", "off_diagonal", "o_done"))
    with nc.Block() as block:
        @block.sync
        def _(sp):
            tables.start(sp, levels, m.const_dram("hgrn_levels"))

        @block.tensor
        def _(pe):
            transpose_values(pe, m, v, 0).then_inc(*v_turned.up())
            pe.wait_ge(*v_ready.at(1))
            for h in range(NH + 1):
                if h < NH:
                    j, r = h // 2, slice(HD * (h % 2), HD * (h % 2) + HD)
                    if h % 2 == 0:
                        pe.wait_ge(*damped_q.at(j + 1))
                        pe.wait_ge(*damped_k.at(j + 1))
                    if h >= 1:
                        pe.wait_ge(*summed.at(h))
                    for l in range(LEVELS):
                        qq, kk = (q[r, j, :], k[r, j, :]) if l == 0 else (dq[r, l - 1, :], dk[r, l - 1, :])
                        for tt in range(2):
                            at = (2 * l + tt) * P
                            nc.tensor.matmul(m.ps[:, at // 512, at % 512:at % 512 + P], kk[:, tt * P:(tt + 1) * P],
                                             qq[:, tt * P:(tt + 1) * P], start=True, stop=True)
                    if h >= 2:
                        pe.wait_ge(*off_done.at(h - 1))
                    nc.tensor.matmul(m.ps[:, 4 + h % 2, 0:P], dk[r, LEVELS - 1, 0:P], dq[r, LEVELS - 1, P:T],
                                     start=True, stop=True).then_inc(*scores.up())
                if h >= 1:
                    g_ = h - 1
                    pe.wait_ge(*weights.at(h))
                    pe.wait_ge(*off_done.at(h))
                    weighted_values(pe, m, g_, lambda st: vt[:, st, g_ * HD:(g_ + 1) * HD], pr[:, g_ % 2, :],
                                    m.ps[:, 6 + g_ // 4, (g_ // 2 % 2) * T:(g_ // 2 % 2) * T + T]).then_inc(*o_done.up())

        @block.scalar
        def _(act):
            act.wait_ge(*v_turned.at(1))
            nc.scalar.activation(vt, m.ps[:, 0:2, :], ACT.Copy).then_inc(*v_ready.up())
            nc.scalar.activation(k, f, ACT.Sigmoid, scale=-1.0).then_inc(*k_gate.up())
            nc.scalar.activation(g, g, ACT.Sigmoid)
            nc.scalar.activation(q, q, ACT.Silu).then_inc(*k_gate.up())
            log_one_plus_exp(act, m, f, lt, log_part)
            if not first:
                act.wait_ge(*odds_ready.at(1))
                log_one_plus_exp(act, m, f, lt, log_part)

            def off(h):
                act.wait_ge(*scores.at(h + 1))
                if h >= 2:
                    act.wait_ge(*o_done.at(h - 1))
                nc.scalar.activation(pr[:, h % 2, P:T], m.ps[:, 4 + h % 2, 0:P], ACT.Copy).then_inc(*off_done.up())

            for j in range(GT):
                act.wait_ge(*distance.at(j + 1))
                nc.scalar.activation(dq, dq, ACT.Exp).then_inc(*decay.up())
                nc.scalar.activation(dk, dk, ACT.Exp, scale=-1.0).then_inc(*decay.up())
                off(2 * j)
                off(2 * j + 1)
            act.wait_ge(*o_done.at(NH))
            nc.scalar.activation(q, m.banks(6, 2).rearrange("p (a b) -> p a b", b=T), ACT.Copy)

        @block.gpsimd
        def _(pool):
            for j in range(GT):
                pool.wait_ge(*decay.at(2 * j + 1))
                nc.gpsimd.tensor_tensor(dq, dq, bcast(q[:, j, :], LEVELS), ALU.mult).then_inc(*damped_q.up())

        @block.vector
        def _(dve):
            step = m.dve_step
            dve.wait_ge(*k_gate.at(1))
            if not first:
                for j in range(GT):
                    nc.vector.tensor_scalar(k[:, j, :], k[:, j, :], par["one_less_lb"][:, j:j + 1], None, ALU.mult)
            dve.wait_ge(*log_part.at(1))
            done(dve, nc.vector.scalar_tensor_tensor(f, f, 0.0, lt, ALU.min, ALU.subtract), step)
            if not first:
                for j in range(GT):
                    last = nc.vector.tensor_scalar(f[:, j, :], f[:, j, :], par["log_odds"][:, j:j + 1], None, ALU.add)
                done(dve, last, odds_ready)
                dve.wait_ge(*log_part.at(2))
                done(dve, nc.vector.scalar_tensor_tensor(f, f, 0.0, lt, ALU.max, ALU.add), step)
                for j in range(GT):
                    last = nc.vector.tensor_scalar(f[:, j, :], f[:, j, :], par["log_lb"][:, j:j + 1], None, ALU.add)
                done(dve, last, step)
            for j in range(GT):
                last = nc.vector.tensor_tensor_scan(ls[:, j, :], m.const("ones")[:, 0:1].broadcast_to([P, T]), f[:, j, :], 0.0,
                                                    ALU.mult, ALU.add)
            done(dve, last, step)
            done(dve, nc.vector.tensor_copy(f, ls), step)
            dve.wait_ge(*k_gate.at(2))
            done(dve, nc.vector.tensor_scalar(q, q, HD ** -0.5, None, ALU.mult), step)
            dve.wait_ge(*tables.all())
            for j in range(GT):
                if j:
                    dve.wait_ge(*scores.at(2 * j))
                for l in range(LEVELS):
                    b = 1 << l
                    c = f[:, j, :].rearrange("p (n b) -> p n b", b=2 * b)
                    last = nc.vector.tensor_tensor(dk[:, l, :].rearrange("p (n b) -> p n b", b=2 * b), c,
                                                   c[:, :, b - 1:b].broadcast_to([P, T // (2 * b), 2 * b]), ALU.subtract)
                done(dve, last, step)
                done(dve, nc.vector.tensor_scalar(dq, dk, 0.0, None, ALU.min), step)
                nc.vector.tensor_scalar(dk, dk, 0.0, None, ALU.max).then_inc(*distance.up())
                dve.wait_ge(*decay.at(2 * j + 2))
                nc.vector.tensor_tensor(dk, dk, bcast(k[:, j, :], LEVELS), ALU.mult).then_inc(*damped_k.up())
                for h in (2 * j, 2 * j + 1):
                    dve.wait_ge(*scores.at(h + 1))
                    done(dve, nc.vector.tensor_tensor(prod.rearrange("p (l a t) -> p l a t", l=LEVELS, a=2),
                                                      m.banks(0, 4).rearrange("p (l a t) -> p l a t", l=LEVELS, a=2),
                                                      levels.rearrange("p (l t) -> p l t", l=LEVELS).unsqueeze(2).broadcast_to([P, LEVELS, 2, P]),
                                                      ALU.mult), summed)
                    if h >= 2:
                        dve.wait_ge(*o_done.at(h - 1))
                    w = pr[:, h % 2, :].rearrange("p (a t) -> p a t", t=P)[:, 0:3:2, :]
                    done(dve, nc.vector.tensor_reduce(w, prod.rearrange("p (l a t) -> p a t l", l=LEVELS, a=2), AX.X, ALU.add),
                         weights)
    m.end()


DECAY_SCALE = 0.6065306597126334
CHUNK = 64
NC = T // CHUNK


def rwkv_inputs_stage(m, par, w, first):
    nc = m.nc
    p = m.a(P_AT, 14)
    r, k, v = (m.a(P_AT + 4 * n, GT) for n in range(3))
    wa_in, g_in = m.arena[:, P_AT + 12, :], m.arena[:, P_AT + 13, :]
    starts = m.arena[:, P_AT + 15, :]
    wa_up, g_up = m.flat(S_AT, GW), m.flat(S_AT + 2, GW)
    v_down, v_up = m.flat(S_AT + 4, P).rearrange("p (a b) -> p a b", a=GT), m.flat(S_AT + 5, GW)
    v_low = m.arena[:, S_AT + 7, :]
    diff = m.a(S_AT + 8, 14)
    log_w, a, kk, sq, cum, big_w, g = (m.a(S_AT + n, GT) for n in (8, 12, 16, 20, 24, 28, 32))
    sig_v = m.tmp[:, 0, :, :]
    bonus = m.a(MIX_AT + 12, GT)
    weights = Load(m, "small_weights_landed")
    shifted, lora_in, lora_out, gates = m.sig("shifted"), m.sig("lora_in"), m.sig("lora_out"), m.sig("lora_gates")
    v_mix, kk_raw, squares, sums, root = m.sig("v_mix"), m.sig("kk_raw"), m.sig("squares"), m.sig("mean_sums"), m.sig("root")
    bonus_in, bonus_sum, cum_ready, exps = m.sig("bonus_in"), m.sig("bonus_sum"), m.sig("cum_ready"), m.sig("decay_ready")

    def tile(b, j):
        return m.ps[:, b + j // 2, j % 2 * T:j % 2 * T + T]

    with nc.Block() as block:
        @block.sync
        def _(sp):
            weights.start(sp, wa_up[0:HD, :], w["w_up"])
            weights.start(sp, wa_up[HD:P, :], w["a_up"])
            weights.start(sp, g_up, w["g_up"])
            weights.start(sp, starts, m.const_dram("chunk_starts"))
            if not first:
                weights.start(sp, v_down, w["v_down"].rearrange("(k p) n -> p k n", p=P))
                weights.start(sp, v_up[0:32, :], w["v_up"])

        @block.tensor
        def _(pe):
            pe.wait_ge(*weights.all())
            pe.wait_ge(*lora_in.at(1))
            for j in range(GT):
                nc.tensor.matmul(tile(0, j), wa_up[0:HD, j * P:(j + 1) * P], wa_in[0:HD, :], start=True, stop=True)
            for j in range(GT):
                nc.tensor.matmul(tile(2, j), wa_up[HD:P, j * P:(j + 1) * P], wa_in[HD:P, :], start=True, stop=True)
            for j in range(GT):
                mm = nc.tensor.matmul(tile(4, j), g_up[:, j * P:(j + 1) * P], g_in, start=True, stop=True)
            if not first:
                for j in range(GT):
                    mm = nc.tensor.matmul(m.ps[0:32, 6, 0:T], v_down[:, j, :], v[:, j, :], start=(j == 0), stop=(j == GT - 1))
            mm.then_inc(*lora_out.up())
            if not first:
                pe.wait_ge(*gates.at(2))
                for j in range(GT):
                    mm = nc.tensor.matmul(tile(6, j), v_up[0:32, j * P:(j + 1) * P], v_low[0:32, :], start=True, stop=True)
                mm.then_inc(*lora_out.up())
            pe.wait_ge(*gates.at(1 if first else 2))
            pe.wait_ge(*squares.at(1))
            for b in range(2):
                mm = nc.tensor.matmul(m.ps[:, b, :], m.const("head_ones"), sq[:, 2 * b:2 * b + 2, :], start=True, stop=True)
            mm.then_inc(*sums.up())
            pe.wait_ge(*bonus_in.at(1))
            for b in range(2):
                mm = nc.tensor.matmul(m.ps[:, 2 + b, :], m.const("head_ones"), sq[:, 2 * b:2 * b + 2, :], start=True, stop=True)
            mm.then_inc(*bonus_sum.up())

        @block.scalar
        def _(act):
            act.wait_ge(*shifted.at(1))
            nc.scalar.activation(wa_in[0:HD, :], wa_in[0:HD, :], ACT.Tanh)
            nc.scalar.activation(g_in, g_in, ACT.Sigmoid).then_inc(*lora_in.up())
            act.wait_ge(*lora_out.at(1))
            for j in range(GT):
                nc.scalar.activation(log_w[:, j, :], tile(0, j), ACT.Sigmoid, bias=par["w0"][:, j:j + 1])
            for j in range(GT):
                nc.scalar.activation(a[:, j, :], tile(2, j), ACT.Sigmoid, bias=par["a0"][:, j:j + 1])
            nc.scalar.activation(g, m.banks(4, 2).rearrange("p (a b) -> p a b", b=T), ACT.Copy).then_inc(*gates.up())
            if not first:
                nc.scalar.activation(v_low[0:32, :], m.ps[0:32, 6, 0:T], ACT.Copy).then_inc(*gates.up())
                act.wait_ge(*lora_out.at(2))
                for j in range(GT):
                    last = nc.scalar.activation(sig_v[:, j, :], tile(6, j), ACT.Sigmoid, bias=par["v0"][:, j:j + 1])
                last.then_inc(*v_mix.up())
            act.wait_ge(*kk_raw.at(1))
            nc.scalar.activation(sq, kk, ACT.Square).then_inc(*squares.up())
            act.wait_ge(*sums.at(1))
            nc.scalar.activation(sq, m.banks(0, 2).rearrange("p (a b) -> p a b", b=T), ACT.Sqrt).then_inc(*root.up())
            act.wait_ge(*cum_ready.at(1))
            nc.scalar.activation(big_w, cum, ACT.Exp).then_inc(*exps.up())
            act.wait_ge(*bonus_sum.at(1))
            nc.scalar.activation(sq, cum, ACT.Exp, scale=-1.0).then_inc(*exps.up())
            nc.scalar.activation(log_w, log_w, ACT.Exp).then_inc(*exps.up())

        @block.vector
        def _(dve):
            step = m.dve_step
            nc.vector.tensor_tensor(diff[:, :, 1:T], p[:, :, 0:T - 1], p[:, :, 1:T], ALU.subtract)
            done(dve, nc.vector.tensor_scalar(diff[:, :, 0:1], p[:, :, 0:1], -1.0, None, ALU.mult), step)
            for j in list(range(12, 14)) + list(range(12)):
                last = nc.vector.scalar_tensor_tensor(p[:, j, :], diff[:, j, :], par["mu"][:, j:j + 1], p[:, j, :], ALU.mult, ALU.add)
            done(dve, last, shifted)
            if first:
                nc.vector.tensor_copy(m.v_first[:, :, :], v)
            dve.wait_ge(*gates.at(1))
            for j in range(GT):
                last = nc.vector.tensor_scalar(kk[:, j, :], k[:, j, :], par["k_k"][:, j:j + 1], None, ALU.mult)
            done(dve, last, kk_raw)
            done(dve, nc.vector.tensor_scalar(log_w, log_w, -DECAY_SCALE, None, ALU.mult), step)
            dve.wait_ge(*weights.all())
            for j in range(GT):
                last = nc.vector.tensor_tensor_scan(cum[:, j, :], starts, log_w[:, j, :], 0.0, ALU.mult, ALU.add)
            done(dve, last, step)
            done(dve, nc.vector.tensor_tensor(log_w, cum, log_w, ALU.subtract), cum_ready)
            dve.wait_ge(*root.at(1))
            done(dve, nc.vector.tensor_scalar(sq, sq, 1e-12, None, ALU.max), step)
            done(dve, nc.vector.reciprocal(sq, sq), step)
            nc.vector.tensor_tensor(kk, kk, sq, ALU.mult)
            t = m.tmp[:, 1, :, :]
            for j in range(GT):
                last = nc.vector.tensor_scalar(t[:, j, :], a[:, j, :], -1.0, par["k_a"][:, j:j + 1], ALU.add, ALU.mult)
            done(dve, last, step)
            done(dve, nc.vector.scalar_tensor_tensor(k, t, 1.0, k, ALU.add, ALU.mult), step)
            for j in range(GT):
                last = nc.vector.scalar_tensor_tensor(sq[:, j, :], r[:, j, :], par["r_k"][:, j:j + 1], k[:, j, :], ALU.mult, ALU.mult)
            last.then_inc(*bonus_in.up())
            nc.vector.tensor_tensor(a, a, kk, ALU.mult)
            if not first:
                dve.wait_ge(*v_mix.at(1))
                done(dve, nc.vector.tensor_tensor(t, m.v_first[:, :, :], v, ALU.subtract), step)
                done(dve, nc.vector.tensor_tensor(t, t, sig_v, ALU.mult), step)
                done(dve, nc.vector.tensor_tensor(v, v, t, ALU.add), step)
            dve.wait_ge(*bonus_sum.at(1))
            done(dve, nc.vector.tensor_tensor(bonus, m.banks(2, 2).rearrange("p (a b) -> p a b", b=T), v, ALU.mult), step)
            dve.wait_ge(*exps.at(1))
            nc.vector.tensor_tensor(r, r, big_w, ALU.mult)
            nc.vector.tensor_copy(m.chunk_w[:, :, :], big_w[:, :, CHUNK - 1:T:CHUNK])
            dve.wait_ge(*exps.at(2))
            nc.vector.tensor_tensor(k, k, sq, ALU.mult)
            nc.vector.tensor_tensor(a, a, sq, ALU.mult)
            dve.wait_ge(*exps.at(3))
            nc.vector.tensor_tensor(kk, kk, log_w, ALU.mult)
    m.end()


def by_head(ap):
    return ap.rearrange("p (h t) n -> p h t n", h=2)


def mask4(ap):
    return ap.unsqueeze(1).unsqueeze(1).broadcast_to([P, 2, 2, P])


def rwkv_solve_stage(m):
    nc = m.nc
    kh, v, bh, kd = m.a(P_AT + 4, GT), m.a(P_AT + 8, GT), m.a(S_AT + 12, GT), m.a(S_AT + 16, GT)
    vt, kht, nbt, kdt = (m.u[:, 4 * n:4 * n + 4, :].rearrange("p (a b) c -> p a (b c)", a=2) for n in range(4))
    masks = m.flat(S_AT, 6 * P).rearrange("p (a b) -> p a b", b=P)
    low8, up8, low_off, up_strict = (masks[:, n, :] for n in range(4))

    def mat(t0):
        return m.flat(t0, 512).rearrange("p (x n) -> p x n", n=P)

    ad, adt, off, akt, a2, a2t = (mat(S_AT + n) for n in (20, 22, 24, 26, 28, 30))
    y, a4 = mat(P_AT + 12), mat(P_AT + 14)
    bt, b_, b2t, b2, b4t, t1 = ad, adt, akt, a2, a2t, y
    x1 = m.tmp[:, 0, 2:4, :].rearrange("p a (x n) -> p (a x) n", n=P)
    rhs = m.tmp[:, 0, 0:2, :].rearrange("p a b -> p (a b)")
    tables = Load(m, "tables_landed")
    turned, token_major, products, evacuated = m.sig("v_turned"), m.sig("v_ready"), m.sig("products"), m.sig("evacuated")

    def item(flat, x):
        hh, tt = divmod(x, 2)
        return flat.rearrange("p (q t h d) -> p q t h d", q=2, t=2, h=2)[:, :, tt, hh, :]

    with nc.Block() as block:
        @block.sync
        def _(sp):
            for n, name in enumerate(("low8", "up8", "low_off", "up_strict", "up_incl", "up_incl_neg")):
                tables.start(sp, masks[:, n, :], m.const_dram(name))

        @block.tensor
        def _(pe):
            for n, x in enumerate((v, kh, bh, kd)):
                transpose_values(pe, m, x, 2 * n).then_inc(*turned.up())
            pe.wait_ge(*token_major.at(4))

            def mats(bank, lhs, right, x, out=None):
                at = m.ps[:, bank, x * P:(x + 1) * P] if out is None else out
                return nc.tensor.matmul(at, lhs, right, start=True, stop=True)

            for j in range(GT):
                n = 10 * j
                if j:
                    pe.wait_ge(*evacuated.at(n))
                for hh in range(2):
                    r = slice(HD * hh, HD * hh + HD)
                    for tt in range(2):
                        x, tk = 2 * hh + tt, slice(tt * P, (tt + 1) * P)
                        for bank, l, rr in ((0, kd, bh), (1, bh, kd), (2, kh, kd)):
                            mm = mats(0, l[r, j, tk], rr[r, j, tk], x, m.ps[:, bank + 3 * hh, tk])
                mm.then_inc(*products.up())
                pe.wait_ge(*evacuated.at(n + 1))
                for x in range(4):
                    hh, tt = divmod(x, 2)
                    mats(0, adt[:, x, :], ad[:, x, :], x)
                    mats(1, ad[:, x, :], adt[:, x, :], x)
                    col = (tt * 2 + hh) * HD
                    head = (2 * j + hh) * HD
                    mm = mats(2, akt[:, x, :], vt[:, tt, head:head + HD], x, m.ps[:, 2, col:col + HD])
                mm.then_inc(*products.up())
                pe.wait_ge(*evacuated.at(n + 2))
                for x in range(4):
                    mats(0, a2t[:, x, :], a2[:, x, :], x)
                    mm = mats(1, a2[:, x, :], y[:, x, :], x)
                mm.then_inc(*products.up())
                pe.wait_ge(*evacuated.at(n + 3))
                for x in range(4):
                    mm = mats(0, a4[:, x, :], x1[:, x, :], x)
                mm.then_inc(*products.up())
                pe.wait_ge(*evacuated.at(n + 4))
                for x in range(4):
                    mats(0, off[:, x, :], t1[:, x, :], x)
                    mats(1, t1[:, x, :], off[:, x, :], x)
                    mm = mats(2, t1[:, x, :], item(rhs, x), x, item(m.ps[:, 2, :], x))
                mm.then_inc(*products.up())
                pe.wait_ge(*evacuated.at(n + 5))
                for x in range(4):
                    mats(0, b_[:, x, :], bt[:, x, :], x)
                    mm = mats(1, bt[:, x, :], b_[:, x, :], x)
                mm.then_inc(*products.up())
                pe.wait_ge(*evacuated.at(n + 6))
                for x in range(4):
                    mm = mats(0, b2[:, x, :], b2t[:, x, :], x)
                mm.then_inc(*products.up())
                z = m.flat(S_AT + 3 + 2 * j, 512)
                for q, l in enumerate((b4t, b2t, bt)):
                    pe.wait_ge(*evacuated.at(n + 7 + q))
                    for x in range(4):
                        mm = mats(0, l[:, x, :], item(z, x), x, item(m.ps[:, 0, :], x))
                    mm.then_inc(*products.up())

        @block.scalar
        def _(act):
            for n, x in enumerate((vt, kht, nbt, kdt)):
                act.wait_ge(*turned.at(n + 1))
                nc.scalar.activation(x, m.ps[:, 2 * n:2 * n + 2, :], ACT.Copy, scale=-1.0 if n == 2 else 1.0)\
                    .then_inc(*token_major.up())

        @block.vector
        def _(dve):
            ps = [m.ps[:, b, :].rearrange("p (x n) -> p x n", n=P) for b in range(3)]
            tt_, cp = nc.vector.tensor_tensor, nc.vector.tensor_copy
            dve.wait_ge(*tables.all())
            dve.wait_ge(*token_major.at(4))
            for j in range(GT):
                n = 10 * j
                z = m.flat(S_AT + 3 + 2 * j, 512)
                dve.wait_ge(*products.at(n + 1))
                for out, bank, mask in ((ad, 0, low8), (off, 0, low_off), (adt, 1, up8), (akt, 2, up_strict)):
                    last = tt_(by_head(out), m.ps[:, bank:bank + 4:3, 0:T].rearrange("p h (t n) -> p h t n", n=P),
                               mask4(mask), ALU.mult)
                done(dve, last, evacuated)
                nc.vector.scalar_tensor_tensor(y, adt, -1.0, bcast(m.const("ident"), 4), ALU.mult, ALU.add)
                cp(rhs[:, 0:T].rearrange("p (t h) -> p t h", t=2), kdt[:, :, j * P:(j + 1) * P])
                dve.wait_ge(*products.at(n + 2))
                cp(a2, ps[0])
                cp(a2t, ps[1])
                done(dve, cp(rhs[:, T:2 * T], m.ps[:, 2, 0:T]), evacuated)
                dve.wait_ge(*products.at(n + 3))
                cp(a4, ps[0])
                done(dve, tt_(x1, y, ps[1], ALU.add), evacuated)
                dve.wait_ge(*products.at(n + 4))
                tt_(t1, x1, ps[0], ALU.add).then_inc(*evacuated.up())
                dve.wait_ge(*products.at(n + 5))
                cp(bt, ps[0])
                cp(b_, ps[1])
                done(dve, cp(z, m.ps[:, 2, :]), evacuated)
                dve.wait_ge(*products.at(n + 6))
                cp(b2t, ps[0])
                done(dve, cp(b2, ps[1]), evacuated)
                dve.wait_ge(*products.at(n + 7))
                cp(b4t, ps[0]).then_inc(*evacuated.up())
                for q in range(3):
                    dve.wait_ge(*products.at(n + 8 + q))
                    done(dve, tt_(z, z, m.ps[:, 0, :], ALU.subtract if q == 2 else ALU.add), evacuated)
    m.end()


def rwkv_output_stage(m):
    nc = m.nc
    rd, kh, bh = m.a(P_AT, GT), m.a(P_AT + 4, GT), m.a(S_AT + 12, GT)
    vt, kht, nbt = (m.u[:, 4 * n:4 * n + 4, :].rearrange("p (a b) c -> p a (b c)", a=2) for n in range(3))
    incl = [m.flat(S_AT, 6 * P)[:, n * P:(n + 1) * P] for n in (4, 5)]
    trans = m.flat(S_AT + 20, 512).rearrange("p (c j n) -> p c j n", c=2, n=HD)
    state = m.flat(S_AT + 22, NC * T).rearrange("p (c j n) -> p c j n", c=NC, n=HD)
    gain = m.tmp[:, 1, 0:3, :].rearrange("p c (j n) -> p c j n", n=HD)
    xt = m.tmp[:, 0, :, :]
    un = m.flat(S_AT + 28, GT * T).rearrange("p (t j h n) -> p t j h n", t=2, j=GT, h=2)
    unf = m.flat(S_AT + 28, GT * T).rearrange("p (t n) -> p t n", t=2)
    low = m.flat(P_AT + 12, 1024).rearrange("p (q x n) -> p q x n", q=2, n=P)
    z = [m.flat(S_AT + 3 + 2 * j, 512).rearrange("p (q t h d) -> p q t h d", q=2, t=2, h=2) for j in range(GT)]
    zt = [m.flat(S_AT + 3 + 2 * j, 512).rearrange("p (q t n) -> p q t n", q=2, t=2) for j in range(GT)]
    chunk_maps, maps_ready, carried, states = m.sig("chunk_maps"), m.sig("maps_ready"), m.sig("carried"), m.sig("states")
    turned, x_ready, u_done, u_ready = m.sig("v_turned"), m.sig("v_ready"), m.sig("u_done"), m.sig("u_ready")
    products, evacuated, o_done = m.sig("products"), m.sig("evacuated"), m.sig("o_done")
    with nc.Block() as block:
        @block.tensor
        def _(pe):
            for c, bank in ((0, 1), (1, 2), (2, 3)):
                tt, rr = c // 2, slice(CHUNK * (c % 2), CHUNK * (c % 2) + CHUNK)
                for h in range(NH):
                    j, hh = divmod(h, 2)
                    o, cols = slice(HD * hh, HD * hh + HD), slice(h * HD, (h + 1) * HD)
                    out = m.ps[o, bank, j * HD:(j + 1) * HD]
                    nc.tensor.matmul(out, kht[rr, tt, cols], vt[rr, tt, cols], start=True, stop=False)
                    mm = nc.tensor.matmul(out, nbt[rr, tt, cols], z[j][rr, 1, tt, hh, :], start=False, stop=True)
                if c:
                    for h in range(NH):
                        j, hh = divmod(h, 2)
                        o, cols = slice(HD * hh, HD * hh + HD), slice(h * HD, (h + 1) * HD)
                        mm = nc.tensor.matmul(m.ps[o, 3 + c, j * HD:(j + 1) * HD], z[j][rr, 0, tt, hh, :], nbt[rr, tt, cols],
                                              start=True, stop=True)
            mm.then_inc(*chunk_maps.up())
            for j in range(GT):
                for tt in range(2):
                    mm = nc.tensor.transpose(m.ps[:, 6 + j // 2, (j % 2 * 2 + tt) * P:(j % 2 * 2 + tt + 1) * P],
                                             zt[j][:, 0, tt, :], m.const("ident"))
            mm.then_inc(*turned.up())
            for c in (1, 2):
                pe.wait_ge(*maps_ready.at(1))
                pe.wait_ge(*states.at(c))
                for hh in range(2):
                    r = slice(HD * hh, HD * hh + HD)
                    for j in range(GT):
                        mm = nc.tensor.matmul(m.ps[r, hh, j * HD:(j + 1) * HD], trans[r, c - 1, j, :], state[r, c, j, :],
                                              start=True, stop=True)
                mm.then_inc(*carried.up())
            pe.wait_ge(*states.at(3))
            pe.wait_ge(*x_ready.at(1))
            for hh in range(2):
                r = slice(HD * hh, HD * hh + HD)
                for c in range(NC):
                    tt, rr = c // 2, slice(CHUNK * (c % 2), CHUNK * (c % 2) + CHUNK)
                    for j in range(GT):
                        mm = nc.tensor.matmul(m.ps[rr, 2 + hh, (j * 2 + tt) * HD:(j * 2 + tt + 1) * HD],
                                              xt[r, j, c * CHUNK:(c + 1) * CHUNK], state[r, c, j, :], start=True, stop=True)
            mm.then_inc(*u_done.up())
            for j in range(GT):
                if j:
                    pe.wait_ge(*evacuated.at(j))
                else:
                    pe.wait_ge(*u_ready.at(1))
                for hh in range(2):
                    r = slice(HD * hh, HD * hh + HD)
                    for tt in range(2):
                        tk = slice(tt * P, (tt + 1) * P)
                        for q, l in enumerate((kh, bh)):
                            mm = nc.tensor.matmul(m.ps[:, 2 * q + hh, tk], l[r, j, tk], rd[r, j, tk], start=True, stop=True)
                mm.then_inc(*products.up())
                pe.wait_ge(*evacuated.at(j + 1))
                for hh in range(2):
                    r, cols = slice(HD * hh, HD * hh + HD), slice((2 * j + hh) * HD, (2 * j + hh + 1) * HD)
                    for tt in range(2):
                        x = 2 * hh + tt
                        at = j % 2 * T + tt * P
                        out = m.ps[r, 6 + j // 2, :]
                        nc.tensor.matmul(out[:, at:at + P], vt[:, tt, cols], low[:, 0, x, :], start=True, stop=False)
                        nc.tensor.matmul(out[:, at:at + P], unf[:, tt, cols], low[:, 1, x, :], start=False, stop=False)
                        for cc in range(2):
                            c = 2 * tt + cc
                            mm = nc.tensor.matmul(out[:, at + cc * CHUNK:at + (cc + 1) * CHUNK], state[r, c, j, :],
                                                  rd[r, j, c * CHUNK:(c + 1) * CHUNK], start=False, stop=(cc == 1))
                mm.then_inc(*o_done.up())

        @block.scalar
        def _(act):
            act.wait_ge(*turned.at(1))
            nc.scalar.activation(xt, m.banks(6, 2).rearrange("p (a b) -> p a b", b=T), ACT.Copy).then_inc(*x_ready.up())
            act.wait_ge(*o_done.at(GT))
            nc.scalar.activation(rd, m.banks(6, 2).rearrange("p (a b) -> p a b", b=T), ACT.Copy)

        @block.vector
        def _(dve):
            tt_ = nc.vector.tensor_tensor
            nc.vector.memset(state[:, 0, :, :], 0.0)
            dve.wait_ge(*chunk_maps.at(1))
            for c in range(3):
                w = m.chunk_w[:, :, c:c + 1].broadcast_to([P, GT, HD])
                to = state[:, 1, :, :] if c == 0 else gain[:, c, :, :]
                last = tt_(to, m.ps[:, 1 + c, 0:GT * HD].rearrange("p (j n) -> p j n", n=HD), w, ALU.mult)
                if c == 0:
                    last.then_inc(*states.up())
            for c in (1, 2):
                last = tt_(trans[:, c - 1, :, :], m.ps[:, 3 + c, 0:GT * HD].rearrange("p (j n) -> p j n", n=HD),
                           bcast(m.const("eye_pair"), GT), ALU.add)
            done(dve, last, maps_ready)
            for c in (1, 2):
                dve.wait_ge(*carried.at(c))
                for hh in range(2):
                    r = slice(HD * hh, HD * hh + HD)
                    last = tt_(state[r, c + 1, :, :], m.ps[r, hh, 0:GT * HD].rearrange("p (j n) -> p j n", n=HD),
                               m.chunk_w[r, :, c:c + 1].broadcast_to([HD, GT, HD]), ALU.mult)
                done(dve, last, m.dve_step)
                tt_(state[:, c + 1, :, :], state[:, c + 1, :, :], gain[:, c, :, :], ALU.add).then_inc(*states.up())
            dve.wait_ge(*u_done.at(1))
            for hh in range(2):
                for j in range(GT):
                    last = tt_(un[:, :, j, hh, :], m.ps[:, 2 + hh, j * 2 * HD:(j + 1) * 2 * HD].rearrange("p (t n) -> p t n", n=HD),
                               z[j][:, 1, :, hh, :], ALU.add)
            last.then_inc(*u_ready.up())
            for j in range(GT):
                dve.wait_ge(*products.at(j + 1))
                if j:
                    dve.wait_ge(*o_done.at(j))
                for q in range(2):
                    last = tt_(by_head(low[:, q, :, :]), m.ps[:, 2 * q:2 * q + 2, 0:T].rearrange("p h (t n) -> p h t n", n=P),
                               mask4(incl[q]), ALU.mult)
                last.then_inc(*evacuated.up())
    m.end()


def gates_stage(m, w_gates, u):
    nc = m.nc
    w = m.flat(S_AT, KT * 2 * NH).rearrange("p (k n) -> p k n", k=KT)
    load = Load(m, "small_weights_landed")
    ready = m.sig("gates_ready")
    with nc.Block() as block:
        @block.sync
        def _(sp):
            load.start(sp, w, w_gates.rearrange("(k p) n -> p k n", p=P))

        @block.tensor
        def _(pe):
            pe.wait_ge(*load.all())
            for b in range(2):
                for k in range(KT):
                    mm = nc.tensor.matmul(m.ps[0:NH, b, 0:T], w[:, k, b * NH:(b + 1) * NH], u[:, k, :],
                                          start=(k == 0), stop=(k == KT - 1))
            mm.then_inc(*ready.up())

        @block.scalar
        def _(act):
            act.wait_ge(*ready.at(1))
            nc.scalar.activation(m.gates, m.ps[0:NH, 0:2, 0:T], ACT.Copy)
    m.end()


def lower_bounds_stage(m, logits, one_less, log_odds, log_lb):
    nc = m.nc
    t = m.flat(S_AT, 8 * GT).rearrange("p (a b) -> p a b", b=GT)
    e, top, s, inv, lb = t[:, 0:2, :], t[:, 2, :], t[:, 3, :], t[:, 4, :], t[:, 5, :]
    shifted, exps, bounds, logs = m.sig("shifted"), m.sig("decay_ready"), m.sig("lora_in"), m.sig("log_part")
    with nc.Block() as block:
        @block.scalar
        def _(act):
            act.wait_ge(*shifted.at(1))
            nc.scalar.activation(e, e, ACT.Exp).then_inc(*exps.up())
            act.wait_ge(*bounds.at(1))
            nc.scalar.activation(log_odds, one_less, ACT.Ln)
            nc.scalar.activation(log_lb, s, ACT.Ln).then_inc(*logs.up())

        @block.vector
        def _(dve):
            tt, step = nc.vector.tensor_tensor, m.dve_step
            done(dve, tt(top, logits[0], logits[1], ALU.max), step)
            tt(e[:, 0, :], logits[0], top, ALU.subtract)
            done(dve, tt(e[:, 1, :], logits[1], top, ALU.subtract), shifted)
            dve.wait_ge(*exps.at(1))
            done(dve, tt(s, e[:, 0, :], e[:, 1, :], ALU.add), step)
            done(dve, nc.vector.reciprocal(inv, s), step)
            tt(e[:, 0, :], e[:, 0, :], inv, ALU.mult)
            done(dve, tt(e[:, 1, :], e[:, 1, :], inv, ALU.mult), step)
            done(dve, tt(lb, e[:, 0, :], e[:, 1, :], ALU.add), step)
            done(dve, tt(lb, lb, e[:, 0, :], ALU.subtract), step)
            nc.vector.tensor_scalar(s, lb, 2.0 ** -63, None, ALU.max)
            done(dve, nc.vector.tensor_scalar(one_less, lb, -1.0, 1.0, ALU.mult, ALU.add), bounds)
            dve.wait_ge(*logs.at(1))
            tt(log_odds, log_odds, log_lb, ALU.subtract)
    m.end()


def first_block(m, a):
    col = vector_columns(LAYER_VECTORS)

    def vec(layer, name):
        o, n = col[name]
        return m.par[:, layer, o:o + n]

    def proj(layer, c0, n, dst):
        return Linear(m, [a["w_in"][layer]], D, c0, n, lambda k: m.u[:, k, :], dst)

    one_less, log_odds, log_lb = (m.bounds[:, n, :] for n in range(3))
    lower_bounds_stage(m, [vec(0, "hgrn_lb_logits"), vec(1, "hgrn_lb_logits")], one_less, log_odds, log_lb)
    starts = (0, 2048, 4096, 6160)
    for l in range(2):
        first = l == 0
        ret, hgrn, mls = (proj(l, starts[n], 2048, m.a(P_AT, 16)) for n in range(3))
        rwk = proj(l, starts[3], 1792, m.a(P_AT, 14))
        rms_stage(m, m.h, vec(l, "norm_pre_mix"), m.u, prefetch=ret)
        ret.run(hgrn)
        retention_stage(m)
        head_norm_stage(m, m.a(P_AT, 4), m.a(MIX_AT, 4), m.a(P_AT + 12, 4))
        hgrn.run(mls)
        hgrn_stage(m, dict(one_less_lb=one_less, log_odds=log_odds, log_lb=log_lb), first)
        head_norm_stage(m, m.a(P_AT, 4), m.a(MIX_AT + 4, 4), m.a(P_AT + 12, 4), vec(l, "hgrn_norm_w"))
        mls.run(rwk)
        gates_stage(m, a["w_in"][l][:, 6144:6160], m.u)
        mlstm_stage(m, dict(conv_w=vec(l, "mlstm_conv_w"), conv_b=vec(l, "mlstm_conv_b"), i_bias=vec(l, "mlstm_i_bias"),
                            f_bias=vec(l, "mlstm_f_bias")), m.gates)
        head_norm_stage(m, m.a(P_AT, 4), m.a(MIX_AT + 8, 4), m.a(P_AT + 12, 4), vec(l, "mlstm_norm_w"))
        out = Linear(m, [a["w_out"][l]], D, 0, D, lambda k: m.arena[:, MIX_AT + k, :], m.a(P_AT, 16))
        rwk.run(out)
        small = {n: a["rwkv_" + n][l] for n in ("w_up", "a_up", "g_up")}
        if not first:
            small.update({n: a["rwkv_" + n][0] for n in ("v_down", "v_up")})
        rwkv_inputs_stage(m, {n: vec(l, "rwkv_" + n) for n in ("mu", "w0", "a0", "k_k", "k_a", "r_k", "v0")}, small, first)
        rwkv_solve_stage(m)
        rwkv_output_stage(m)
        head_norm_stage(m, m.a(P_AT, 4), m.a(MIX_AT + 12, 4), m.a(S_AT + 32, 4), vec(l, "rwkv_ln_w"), vec(l, "rwkv_ln_b"), m.a(MIX_AT + 12, 4), 64e-5, True)
        gate_up = Linear(m, [a["w_ffn_gate"][l], a["w_ffn_up"][l]], D, 0, DFF, lambda k: m.u[:, k, :], m.a(0, FT), "gate")
        down = Linear(m, [a["w_ffn_down"][l]], DFF, 0, D, lambda k: m.arena[:, k, :], m.a(FT, KT))
        out.run(gate_up)
        rms_stage(m, m.a(P_AT, 16), vec(l, "norm_post_mix"), None, add_to=m.h)
        rms_stage(m, m.h, vec(l, "norm_pre_ffn"), m.u)
        gate_up.run(down)
        down.run()
        rms_stage(m, m.a(FT, KT), vec(l, "norm_post_ffn"), None, add_to=m.h, scratch=0)



G4 = 4
NCMP = 15
BR = ("ks", "kw")


def trig_stage(m, positions):
    nc = m.nc
    pos = m.flat(S_AT, T)
    pos_i = pos.bitcast(I32)
    ang, n, mag = m.a(S_AT + 1, 2), m.a(S_AT + 3, 2), m.a(S_AT + 5, 2)
    freq = m.flat(S_AT + 7, 2)
    trig = m.v_first[:, :, :].rearrange("p (b c) t -> p b c t", b=2)
    load = Load(m, "tables_landed")
    reduced, quarter, mags = m.sig("shifted"), m.sig("lora_in"), m.sig("squares")
    two_pi = 2 * np.pi
    c1 = 6.28125
    c2 = float(np.float32(np.round((two_pi - c1) * 2 ** 21) / 2 ** 21))
    c3 = float(two_pi - c1 - c2)
    magic = 1.5 * 2 ** 23
    with nc.Block() as block:
        @block.sync
        def _(sp):
            load.start(sp, pos_i, positions.broadcast_to([P, T]))
            load.start(sp, freq, m.const_dram("inv_freq"))

        @block.vector
        def _(dve):
            step = m.dve_step
            dve.wait_ge(*load.all())
            done(dve, nc.vector.tensor_copy(mag[:, 0, :], pos_i), step)
            for b in range(2):
                last = nc.vector.tensor_scalar(ang[:, b, :], mag[:, 0, :], freq[:, b:b + 1], None, ALU.mult)
            done(dve, last, step)
            done(dve, nc.vector.tensor_scalar(n, ang, 1.0 / two_pi, magic, ALU.mult, ALU.add), step)
            done(dve, nc.vector.tensor_scalar(n, n, -magic, None, ALU.add), step)
            for c in (c1, c2, c3):
                done(dve, nc.vector.scalar_tensor_tensor(ang, n, -c, ang, ALU.mult, ALU.add), step)
            done(dve, nc.vector.tensor_scalar(ang, ang, 3.1415925, -3.1415925, ALU.min, ALU.max), reduced)
            dve.wait_ge(*mags.at(1))
            nc.vector.tensor_scalar(mag, mag, -1.0, float(np.pi / 2), ALU.mult, ALU.add).then_inc(*quarter.up())

        @block.scalar
        def _(act):
            act.wait_ge(*reduced.at(1))
            nc.scalar.activation(mag, ang, ACT.Abs).then_inc(*mags.up())
            for b in range(2):
                nc.scalar.activation(trig[:, b, 1, :], ang[:, b, :], ACT.Sin)
            act.wait_ge(*quarter.at(1))
            for b in range(2):
                nc.scalar.activation(trig[:, b, 0, :], mag[:, b, :], ACT.Sin)
    m.end()


def ada_stage(m, row, b_ada, ada):
    nc = m.nc
    n = 48
    turned = m.sig("v_turned")
    with nc.Block() as block:
        @block.tensor
        def _(pe):
            for k in range(n):
                mm = nc.tensor.transpose(m.ps[:, 0, k:k + 1], row[:, k * P:(k + 1) * P], m.const("ident")[0:1, 0:1])
            mm.then_inc(*turned.up())

        @block.vector
        def _(dve):
            dve.wait_ge(*turned.at(1))
            nc.vector.tensor_tensor(ada, m.ps[:, 0, 0:n], b_ada, ALU.add)
    m.end()


def scales_stage(m, g_pre, g_post, ada):
    nc = m.nc
    with nc.Block() as block:
        @block.vector
        def _(dve):
            nc.vector.scalar_tensor_tensor(ada[:, 16:32], ada[:, 16:32], 1.0, g_pre, ALU.add, ALU.mult)
            nc.vector.tensor_tensor(ada[:, 32:48], ada[:, 32:48], g_post, ALU.mult)
    m.end()


def compress_stage(m, w, kcd, vc, gates):
    nc = m.nc
    w1 = [m.flat(20, KT * T).rearrange("p (k n) -> p k n", k=KT), m.flat(36, KT * T).rearrange("p (k n) -> p k n", k=KT)]
    x2 = [m.a(52, G4), m.a(56, G4)]
    nb = G4 * NCMP
    blk = [m.flat(60, KT * nb).rearrange("p (j c) -> p j c", j=KT),
           m.tmp[:, 0, :, :].rearrange("p a b -> p (a b)")[:, 0:KT * nb].rearrange("p (j c) -> p j c", j=KT)]
    rest = m.flat(64, 4 * T)
    hid = [rest[:, n * 2 * nb:(n + 1) * 2 * nb].rearrange("p (h c) -> p h c", h=2) for n in range(2)]
    pe_v = [rest[:, 240 + n * KT:240 + (n + 1) * KT] for n in range(2)]
    w2k = rest[:, 280:280 + 2 * P].rearrange("p (h n) -> p h n", h=2)
    w2v = rest[:, 540:540 + 2 * HD].rearrange("p (h n) -> p h n", h=2)
    kc = rest[:, 670:670 + nb]
    wg = m.flat(P_AT + 16 + 4 + 32, KT * 48).rearrange("p (k n) -> p k n", k=KT)
    moved, weights, gate_w = Load(m, "rows_moved"), Load(m, "small_weights_landed"), Load(m, "gate_weights_landed")
    laid, hidden, hid_ready, out, kc_ready, rotated = (m.sig(n) for n in ("blocks_laid", "products", "gates_ready", "scores",
                                                                           "evacuated", "rotated"))
    gate_logits = m.sig("o_done")
    trig = m.v_first[:, 0:2, :]
    with nc.Block() as block:
        @block.sync
        def _(sp):
            for n in range(2):
                for g in range(G4):
                    src = m.arena[HD * (g % 2):HD * (g % 2) + HD, 8 + 2 * n + g // 2, :]
                    moved.start(sp, x2[n][0:HD, g, :], src)
                    moved.start(sp, x2[n][HD:P, g, 0:T - 1], src[:, 1:T])
            for n, (v1, v2, pe_) in enumerate((("w_ck1_2", "w_ck2_2", "pe_ck_2"), ("w_cv1_2", "w_cv2_2", "pe_cv_2"))):
                weights.start(sp, w1[n], w[v1][0].rearrange("(k p) n -> p k n", p=P))
                weights.start(sp, pe_v[n], w[pe_])
                w2 = w[v2][0].rearrange("(k p) n -> p k n", p=P)
                if n == 0:
                    weights.start(sp, w2k[:, :, 0:HD], w2)
                    weights.start(sp, w2k[:, :, HD:P], w2)
                else:
                    weights.start(sp, w2v, w2)
            sp.wait_ge(*laid.at(1))
            gate_w.start(sp, wg, w["w_in_2"][0][:, 2560:2608].rearrange("(k p) n -> p k n", p=P))

        @block.vector
        def _(dve):
            dve.wait_ge(*moved.all())
            dve.wait_ge(*weights.all())
            for n in range(2):
                for g in range(G4):
                    view = x2[n][:, g, :].rearrange("p (c b two) -> p b c two", b=8, two=2)
                    for half in range(2):
                        last = nc.vector.tensor_tensor(blk[n][:, half * 8:half * 8 + 8, g * NCMP:(g + 1) * NCMP],
                                                       view[:, :, half:half + NCMP, 0],
                                                       pe_v[n][:, half * 8:half * 8 + 8].unsqueeze(2).broadcast_to([P, 8, NCMP]),
                                                       ALU.add)
            last.then_inc(*laid.up())
            dve.wait_ge(*rotated.at(1))
            cos, sin = (trig[:, n, 31:T:16].unsqueeze(1).broadcast_to([P, G4, NCMP]) for n in range(2))
            kc4, kcd4 = kc.rearrange("p (g c) -> p g c", g=G4), kcd.rearrange("p (g c) -> p g c", g=G4)
            nc.vector.tensor_tensor(kcd4, m.ps[:, 5, 0:nb].rearrange("p (g c) -> p g c", g=G4), sin, ALU.mult)
            done(dve, nc.vector.tensor_tensor(kc4, kc4, cos, ALU.mult), m.dve_step)
            nc.vector.tensor_tensor(kcd, kcd, kc, ALU.add)

        @block.tensor
        def _(pe):
            pe.wait_ge(*laid.at(1))
            for n in range(2):
                for half in range(2):
                    for j in range(KT):
                        mm = nc.tensor.matmul(m.ps[:, 2 * n + half, 0:nb], w1[n][:, j, half * P:(half + 1) * P], blk[n][:, j, :],
                                              start=(j == 0), stop=(j == KT - 1))
            mm.then_inc(*hidden.up())
            pe.wait_ge(*hid_ready.at(1))
            for half in range(2):
                mm = nc.tensor.matmul(m.ps[:, 4, 0:nb], w2k[:, half, :], hid[0][:, half, :], start=(half == 0), stop=(half == 1))
            mm.then_inc(*out.up())
            for g in range(G4):
                for half in range(2):
                    mm = nc.tensor.matmul(m.ps[0:NCMP, 6, g * HD:(g + 1) * HD], hid[1][:, half, g * NCMP:(g + 1) * NCMP],
                                          w2v[:, half, :], start=(half == 0), stop=(half == 1))
            mm.then_inc(*out.up())
            pe.wait_ge(*kc_ready.at(1))
            nc.tensor.matmul(m.ps[:, 5, 0:nb], m.const("rot_a"), kc, start=True, stop=True).then_inc(*rotated.up())
            pe.wait_ge(*gate_w.all())
            for tt in range(2):
                for k in range(KT):
                    mm = nc.tensor.matmul(m.ps[:, 7, tt * 48:tt * 48 + 48], m.u[:, k, tt * P:(tt + 1) * P], wg[:, k, :],
                                          start=(k == 0), stop=(k == KT - 1))
            mm.then_inc(*gate_logits.up())

        @block.scalar
        def _(act):
            act.wait_ge(*hidden.at(1))
            for n in range(2):
                last = nc.scalar.activation(hid[n], m.ps[:, 2 * n:2 * n + 2, 0:nb], ACT.Gelu_apprx_tanh)
            last.then_inc(*hid_ready.up())
            act.wait_ge(*out.at(1))
            nc.scalar.activation(kc, m.ps[:, 4, 0:nb], ACT.Copy).then_inc(*kc_ready.up())
            act.wait_ge(*out.at(2))
            nc.scalar.activation(vc, m.ps[0:NCMP, 6, 0:G4 * HD], ACT.Copy)
            act.wait_ge(*gate_logits.at(1))
            nc.scalar.activation(gates, m.ps[:, 7, 0:96].rearrange("p (a b) -> p a b", a=2), ACT.Sigmoid)
    m.end()


def rope_stage(m, tiles, rot, trig, turn, keys=None):
    nc = m.nc
    cos, sin = trig[:, 0, :], trig[:, 1, :]
    jobs = [("q", t) for t in tiles] + [("k", k) for k in (keys or [])]
    rotated, scaled, ready = m.sig("rotated"), m.sig("scaled"), m.sig("qk_ready")
    turned, stored = m.sig("v_turned"), m.sig("v_ready")
    with nc.Block() as block:
        @block.tensor
        def _(pe):
            for n, (kind, t) in enumerate(jobs):
                bank = n % 4
                if n >= 4:
                    pe.wait_ge(*ready.at(n - 3))
                if kind == "q":
                    mm = nc.tensor.matmul(m.ps[:, bank, 0:T], rot, m.arena[:, t, :], start=True, stop=True)
                else:
                    nc.tensor.matmul(m.ps[:, bank, 0:T], t[2], m.arena[:, t[0], :], start=True, stop=True)
                    mm = nc.tensor.matmul(m.ps[:, bank, T:2 * T], t[1], m.arena[:, t[0], :], start=True, stop=True)
                mm.then_inc(*rotated.up())
            n = 0
            for src, dst in turn:
                width = len(src) * P
                for tt in range(2):
                    if n >= 2:
                        pe.wait_ge(*stored.at(n - 1))
                    for x, t in enumerate(src):
                        mm = nc.tensor.transpose(m.ps[:, 4 + 2 * (n % 2) + x // 4, x % 4 * P:x % 4 * P + P],
                                                 m.arena[:, t, tt * P:(tt + 1) * P], m.const("ident"))
                    mm.then_inc(*turned.up())
                    n += 1

        @block.scalar
        def _(act):
            n = 0
            for src, dst in turn:
                width = len(src) * P
                for tt in range(2):
                    act.wait_ge(*turned.at(n + 1))
                    nc.scalar.activation(dst[:, tt, :], m.banks(4 + 2 * (n % 2), 2)[:, 0:width], ACT.Copy).then_inc(*stored.up())
                    n += 1

        @block.vector
        def _(dve):
            tmp = m.tmp[:, 0, :, :]
            for n, (kind, t) in enumerate(jobs):
                bank = n % 4
                dve.wait_ge(*rotated.at(n + 1))
                part = nc.vector.tensor_tensor(tmp[:, bank, :], m.ps[:, bank, 0:T], sin, ALU.mult)
                x = m.arena[:, t, :] if kind == "q" else t[3]
                src = x if kind == "q" else m.ps[:, bank, T:2 * T]
                done(dve, nc.vector.tensor_tensor(x, src, cos, ALU.mult), m.dve_step)
                done(dve, nc.vector.tensor_tensor(x, x, tmp[:, bank, :], ALU.add), ready)
    m.end()


def attention_stage(m, units, masks, scale, s_at, pt_at, cmp=None):
    nc = m.nc
    N = 4
    sbuf = [m.flat(s_at + 4 * b, N * T) for b in range(2)]
    pts = [m.flat(pt_at + 4 * b, N * T) for b in range(2)]
    small = m.tmp[:, 0, 0, :]
    scores, read, tops, exps, probs, turned, stored, o_done, o_read = (
        m.sig(n) for n in ("scores", "scores_read", "row_max", "exps", "weights", "v_turned", "v_ready", "o_done", "o_read"))
    load = Load(m, "tables_landed")

    def shape(b, L):
        return sbuf[b][:, 0:N * L].rearrange("p (i s) -> p i s", i=N)

    def stats(u, k, n):
        o = (u % 2) * 64 + k
        return small[:, o:o + n]

    def cbuf(u):
        return m.tmp[:, 0, 1, (u % 2) * 32:(u % 2) * 32 + 2 * NCMP].rearrange("p (h c) -> p h c", h=2)

    def cpt(u):
        return m.tmp[0:NCMP, 0, 2, :] if u % 2 == 0 else m.tmp[0:NCMP, 0, 3, :]

    with nc.Block() as block:
        @block.sync
        def _(sp):
            for dst, src in masks["loads"]:
                load.start(sp, dst, src)

        @block.tensor
        def _(pe):
            def score(u):
                tt, items, _, _ = units[u]
                L = (tt + 1) * P
                if u:
                    pe.wait_ge(*read.at(u))
                for x, (q, keys, bank) in enumerate(items):
                    mm = nc.tensor.matmul(m.ps[:, bank, x % 2 * T:x % 2 * T + L], q, keys(L), start=True, stop=True)
                if cmp is not None:
                    for hh in range(2):
                        mm = nc.tensor.matmul(m.ps[:, 2 + hh, 0:NCMP], *cmp["scores"](u, hh), start=True, stop=True)
                mm.then_inc(*scores.up())

            score(0)
            for u, (tt, items, outs, _) in enumerate(units):
                L = (tt + 1) * P
                if u + 1 < len(units):
                    score(u + 1)
                pe.wait_ge(*probs.at(u + 1))
                if u:
                    pe.wait_ge(*stored.at(u))
                for x in range(N):
                    for st in range(tt + 1):
                        c = (x * (tt + 1) + st) * P
                        mm = nc.tensor.transpose(m.ps[:, 4 + c // 512, c % 512:c % 512 + P], shape(u % 2, L)[:, x, st * P:(st + 1) * P],
                                                 m.const("ident"))
                if cmp is not None:
                    for hh in range(2):
                        mm = nc.tensor.transpose(m.ps[0:NCMP, 6, hh * P:(hh + 1) * P], cbuf(u)[:, hh, :], m.const("ident"))
                mm.then_inc(*turned.up())
                pe.wait_ge(*stored.at(u + 1))
                if u:
                    pe.wait_ge(*o_read.at(u))
                for rows, col, parts in outs:
                    todo = [(v(st), pts[u % 2][:, (x * (tt + 1) + st) * P:(x * (tt + 1) + st + 1) * P])
                            for v, x in parts for st in range(tt + 1)]
                    if cmp is not None:
                        hh = rows.start // HD
                        todo.append((cmp["values"](u), cpt(u)[:, hh * P:(hh + 1) * P]))
                    for n, (l, r) in enumerate(todo):
                        mm = nc.tensor.matmul(m.ps[rows, 7, col:col + P], l, r, start=(n == 0), stop=(n == len(todo) - 1))
                mm.then_inc(*o_done.up())

        @block.scalar
        def _(act):
            def finish(u):
                tt, _, _, dst = units[u]
                L = (tt + 1) * P
                act.wait_ge(*turned.at(u + 1))
                if u >= 2:
                    act.wait_ge(*o_done.at(u - 1))
                ins = nc.scalar.activation(pts[u % 2][:, 0:N * L], m.banks(4, 2)[:, 0:N * L], ACT.Copy)
                if cmp is not None:
                    ins = nc.scalar.activation(cpt(u), m.ps[0:NCMP, 6, 0:2 * P], ACT.Copy)
                ins.then_inc(*stored.up())

            def put(u):
                act.wait_ge(*o_done.at(u + 1))
                dst = units[u][3]
                n = dst.shape[1]
                nc.scalar.activation(dst, m.ps[:, 7, 0:n * P].rearrange("p (a b) -> p a b", b=P), ACT.Copy).then_inc(*o_read.up())

            for u, (tt, items, _, _) in enumerate(units):
                L = (tt + 1) * P
                s = shape(u % 2, L)
                act.wait_ge(*tops.at(u + 1))
                for x in range(N):
                    ins = nc.scalar.activation(s[:, x, :], s[:, x, :], ACT.Exp, bias=stats(u, x, 1), accum_out=stats(u, 8 + x, 1))
                if cmp is not None:
                    for hh in range(2):
                        ins = nc.scalar.activation(cbuf(u)[:, hh, :], cbuf(u)[:, hh, :], ACT.Exp, bias=stats(u, 4 + hh, 1))
                ins.then_inc(*exps.up())
                if u:
                    finish(u - 1)
                    put(u - 1)
            finish(len(units) - 1)
            put(len(units) - 1)

        @block.vector
        def _(dve):
            step = m.dve_step
            dve.wait_ge(*load.all())

            def first(u):
                tt, items, _, _ = units[u]
                L = (tt + 1) * P
                s = shape(u % 2, L)
                dve.wait_ge(*scores.at(u + 1))
                if u >= 2:
                    dve.wait_ge(*turned.at(u - 1))
                for b in range(2):
                    ins = nc.vector.scalar_tensor_tensor(s[:, 2 * b:2 * b + 2, :],
                                                         m.ps[:, b, :].rearrange("p (i s) -> p i s", i=2)[:, :, 0:L], scale,
                                                         bcast(masks["add"][tt][:, 0:L], 2), ALU.mult, ALU.add)
                if cmp is not None:
                    ins = nc.vector.scalar_tensor_tensor(cbuf(u), m.ps[:, 2:4, 0:NCMP], scale,
                                                         bcast(cmp["mask"][tt][:, 0:NCMP], 2), ALU.mult, ALU.add)
                done(dve, ins, read)
                ins = nc.vector.tensor_reduce(stats(u, 0, N), s, AX.X, ALU.max, negate=True)
                if cmp is not None:
                    ins = nc.vector.tensor_reduce(stats(u, 4, 2), cbuf(u), AX.X, ALU.max, negate=True)
                ins.then_inc(*tops.up())

            def second(u):
                tt, items, _, _ = units[u]
                L = (tt + 1) * P
                s = shape(u % 2, L)
                dve.wait_ge(*exps.at(u + 1))
                if cmp is not None:
                    c = cbuf(u)
                    done(dve, nc.vector.tensor_tensor(c, c, bcast(cmp["mask"][tt][:, NCMP:2 * NCMP], 2), ALU.mult), step)
                    done(dve, nc.vector.tensor_reduce(stats(u, 12, 2), c, AX.X, ALU.add), step)
                    done(dve, nc.vector.tensor_scalar(stats(u, 12, 2), stats(u, 12, 2), 1.0, None, ALU.max), step)
                k = 6 if cmp is not None else 4
                done(dve, nc.vector.reciprocal(stats(u, 16, k), stats(u, 8, k)), step)
                if cmp is not None:
                    j = u // 2
                    g = cmp["gates"][:, tt, 6 * j:6 * j + 6].rearrange("p (h b) -> p h b", b=3)
                    nc.vector.tensor_tensor(stats(u, 24, 4).rearrange("p (h b) -> p h b", h=2),
                                            stats(u, 16, 4).rearrange("p (h b) -> p h b", h=2), g[:, :, 1:3], ALU.mult)
                    done(dve, nc.vector.tensor_tensor(stats(u, 28, 2), stats(u, 20, 2), g[:, :, 0], ALU.mult), step)
                    nc.vector.tensor_tensor(c, c, stats(u, 28, 2).unsqueeze(2).broadcast_to([P, 2, NCMP]), ALU.mult)
                r = stats(u, 24 if cmp is not None else 16, N)
                nc.vector.tensor_tensor(s, s, r.unsqueeze(2).broadcast_to([P, N, L]), ALU.mult).then_inc(*probs.up())

            first(0)
            for u in range(len(units)):
                if u + 1 < len(units):
                    first(u + 1)
                second(u)
    m.end()


def add_stage(m, dst, x):
    nc = m.nc
    with nc.Block() as block:
        @block.vector
        def _(dve):
            nc.vector.tensor_tensor(dst, dst, x, ALU.add)
    m.end()


def second_block(m, a):
    w_in = a["w_in_2"][0]
    col = vector_columns(SECOND_VECTORS)
    b_ada, g_pre, g_post, c = (m.par[:, 0, o:o + n] for o, n in col.values())
    ada = m.par[:, 1, 0:48]
    load = Load(m, "vectors_landed")
    row = m.arena[0:1, :, :].rearrange("p a b -> p (a b)")[:, 0:3 * D]
    w_ada = Linear(m, [a["w_ada_2"][0]], D, 0, 3 * D, lambda k: c[:, k:k + 1], row, "row")
    with m.nc.Block() as block:
        @block.sync
        def _(sp):
            load.start(sp, m.par[:, 0, 0:96], a["second_vectors"])
            w_ada.prefetch(sp)
            sp.wait_ge(*load.all())

    def proj(c0, n, dst, kind="copy", func=None, src=None):
        return Linear(m, [w_in], D, c0, n, lambda k: m.u[:, k, :], dst, kind, func, src)

    qkv = proj(0, 2560, m.a(0, 20))
    w_ada.run(qkv)
    ada_stage(m, row, b_ada, ada)
    scales_stage(m, g_pre, g_post, ada)
    rms_stage(m, m.h, ada[:, 16:32], m.u, shift=ada[:, 0:16])
    trig_stage(m, a["positions_2"])
    oa, ob = m.a(52, 8), m.a(58, 8)
    za = proj(2608, 1024, oa, "mul", ACT.Silu, oa)
    qkv.run(za)
    nb = G4 * NCMP
    kcd, vc = m.tmp[:, 1, 0, 0:nb], m.tmp[0:NCMP, 1, 1, :]
    gates = m.tmp[:, 1, 2, 0:96].rearrange("p (a b) -> p a b", a=2)
    compress_stage(m, a, kcd, vc, gates)
    trig = m.v_first[:, :, :].rearrange("p (b c) t -> p b c t", b=2)
    keys = [(12 + 4 * b + g // 2, m.const(f"dup{g % 2}"), m.const(f"rot_dup{g % 2}"), m.arena[:, 20 + 4 * b + g, :])
            for b in range(2) for g in range(G4)]
    vt = [m.flat(28 + 2 * b, 512).rearrange("p (a b) -> p a b", a=2) for b in range(2)]
    rope_stage(m, range(8), m.const("rot_a"), trig[:, 0, :, :], [((14, 15), vt[0]), ((18, 19), vt[1])], keys)
    units = []
    for j in range(8):
        g = j // 2
        for tt in range(2):
            items, outs = [], []
            for hh in range(2):
                r = slice(HD * hh, HD * hh + HD)
                for b in range(2):
                    items.append((m.arena[r, j, tt * P:(tt + 1) * P], lambda L, r=r, b=b, g=g: m.arena[r, 20 + 4 * b + g, 0:L], hh))
                outs.append((r, 0, [(lambda st, b=b, g=g: vt[b][:, st, g * HD:(g + 1) * HD], 2 * hh + b) for b in range(2)]))
            units.append((tt, items, outs, m.arena[:, 52 + j:53 + j, tt * P:(tt + 1) * P]))
    masks = m.flat(32, 2 * T + 60)
    cmask = [masks[:, 2 * T + 30 * tt:2 * T + 30 * tt + 30] for tt in range(2)]
    add = [masks[:, tt * T:(tt + 1) * T] for tt in range(2)]

    def cmp_scores(u, hh):
        j, tt, r = u // 2, u % 2, slice(HD * hh, HD * hh + HD)
        return m.arena[r, j, tt * P:(tt + 1) * P], kcd[r, j // 2 * NCMP:(j // 2 + 1) * NCMP]

    attention_stage(m, units, dict(add=add, loads=[(x, m.const_dram(f"{n}{tt}")) for n, xs in (("causal", add), ("cmp", cmask))
                                                   for tt, x in enumerate(xs)]),
                    HD ** -0.5, 36, 44,
                    dict(scores=cmp_scores, values=lambda u: vc[:, u // 4 * HD:(u // 4 + 1) * HD], mask=cmask, gates=gates))
    ya, yb = m.a(0, 16), m.a(16, 16)
    br_a = Linear(m, [a["w_br_a_2"][0]], 1024, 0, D, lambda k: m.arena[:, 52 + k, :], ya)
    ma = proj(7728, D, ya, "mul", ACT.Sigmoid, ya)
    qkv_b = proj(3632, 3072, m.a(16, 24))
    za.run(br_a)
    br_a.run(ma)
    ma.run(qkv_b)
    zb = proj(6704, 1024, ob, "mul", ACT.Silu, ob)
    qkv_b.run(zb)
    vtb = m.flat(40, 2048).rearrange("p (a b) -> p a b", a=2)
    rope_stage(m, range(16, 32), m.const("rot_b"), trig[:, 1, :, :], [(tuple(range(32, 40)), vtb)])
    addb = [m.flat(56, T), m.flat(57, T)]
    units = []
    for n in range(2):
        for tt in range(2):
            items = [(m.arena[:, 16 + 4 * n + x, tt * P:(tt + 1) * P], lambda L, h=4 * n + x: m.arena[:, 24 + h, 0:L], x // 2)
                     for x in range(4)]
            outs = [(slice(0, P), x * P, [(lambda st, h=4 * n + x: vtb[:, st, h * P:(h + 1) * P], x)]) for x in range(4)]
            units.append((tt, items, outs, m.arena[:, 58 + 4 * n:62 + 4 * n, tt * P:(tt + 1) * P]))
    attention_stage(m, units, dict(add=addb, loads=[(addb[tt], m.const_dram(f"dilated{tt}")) for tt in range(2)]),
                    P ** -0.5, 48, 32)
    br_b = Linear(m, [a["w_br_b_2"][0]], 1024, 0, D, lambda k: m.arena[:, 58 + k, :], yb)
    mb = proj(9776, D, yb, "mul", ACT.Sigmoid, yb)
    out = Linear(m, [a["w_out_2"][0]], D, 0, D, lambda k: m.arena[:, k, :], m.a(16, 16))
    zb.run(br_b)
    br_b.run(mb)
    mb.run(out)
    add_stage(m, ya, yb)
    out.run()
    rms_stage(m, m.a(16, 16), ada[:, 32:48], None, add_to=m.h)

IN_PLACE = ("w_in", "w_out", "w_ffn_gate", "w_ffn_up", "w_ffn_down", "rwkv_w_up", "rwkv_a_up", "rwkv_g_up",
            "rwkv_v_down", "rwkv_v_up", "w_ada_2", "w_in_2", "w_ck1_2", "w_ck2_2", "w_cv1_2", "w_cv2_2", "w_br_a_2",
            "w_br_b_2", "w_out_2", "positions_2")


def pack(inputs, names, layer=None):
    cols = []
    for name, n in names.items():
        v = np.asarray(inputs[name])
        if layer is not None:
            v = v[0] if v.shape[0] == 1 else v[layer]
        v = v.reshape(-1)
        if v.size < P:
            v = np.concatenate([v, np.zeros(P - v.size, v.dtype)])
        cols.append(v.reshape(n, P).T)
    return np.concatenate(cols, 1)


def feature_major(x):
    return np.ascontiguousarray(x.T.reshape(-1, P, x.shape[0]).transpose(1, 0, 2))


def program(nc, a, out):
    with ExitStack() as ctx:
        m = Model(nc, ctx, a["consts"])
        inputs_landed, out_stored = Load(m, "inputs_landed"), Load(m, "out_stored")
        with nc.Block() as block:
            @block.sync
            def _(sp):
                inputs_landed.start(sp, m.h[:, :, :], a["x"])
                inputs_landed.start(sp, m.par[:, :, 0:LAYER_N - 1], a["layer_vectors"])
                inputs_landed.start(sp, m.cs[:, :], a["consts"][:, 0:sum(m.const_at[k][1] for k in m.small)])
                sp.wait_ge(*inputs_landed.all())
        first_block(m, a)
        second_block(m, a)
        with nc.Block() as block:
            @block.sync
            def _(sp):
                out_stored.start(sp, out, m.h[:, :, :])
                sp.wait_ge(*out_stored.all())


def kernel(**inputs):
    import concourse.bacc as bacc
    from concourse.bass_utils import run_bass_kernel_spmd

    nc = bacc.Bacc("TRN2", target_bir_lowering=False, num_devices=1)
    arrays = {name: np.asarray(inputs[name]) for name in IN_PLACE}
    arrays["x"] = feature_major(np.asarray(inputs["x"])[0])
    arrays["layer_vectors"] = np.stack([pack(inputs, LAYER_VECTORS, layer) for layer in range(2)], 1)
    arrays["second_vectors"] = pack(inputs, SECOND_VECTORS)
    for name in ("pe_ck_2", "pe_cv_2"):
        arrays[name] = np.asarray(inputs[name]).reshape(KT, P).T
    arrays["consts"] = constants()[0]
    arrays = {k: np.ascontiguousarray(v) for k, v in arrays.items()}
    aps = {k: nc.dram_tensor(f"in_{k}", v.shape, mybir.dt.from_np(v.dtype), kind="ExternalInput").ap() for k, v in arrays.items()}
    out = nc.dram_tensor("out", (P, KT, T), F32, kind="ExternalOutput").ap()
    program(nc, aps, out)
    res = run_bass_kernel_spmd(nc, [{f"in_{k}": v for k, v in arrays.items()}], core_ids=[0])
    y = np.asarray(res.results[0]["out"])
    return np.ascontiguousarray(y.transpose(2, 1, 0).reshape(1, T, D))
```

```python
from contextlib import ExitStack

import numpy as np
import concourse.bass as bass
from concourse import mybir

F32 = mybir.dt.float32
F32R = mybir.dt.float32r
I32 = mybir.dt.int32
ALU = mybir.AluOpType
ACT = mybir.ActivationFunctionType
AX = mybir.AxisListType

P = 128
T = 256
D = 2048
KT = D // P
GW = 512
GT = GW // P
HD = 64
NH = GW // HD
DFF = 5632
FT = DFF // P
CW = 512
CB = CW // P
SK = 4
RING = 4
BODY = 8
NEG = -1e30
EPS = 1e-6


class Signal:

    def __init__(self, ctx, nc, name):
        self.sem = ctx.enter_context(nc.semaphore(name))
        self.base = 0
        self.seen = 0

    def up(self, times=1):
        self.seen += times
        return self.sem, 1

    def at(self, k):
        return self.sem, self.base + k

    def now(self):
        return self.sem, self.base + self.seen

    def close(self):
        self.base += self.seen
        self.seen = 0


def done(eng, ins, sig):
    ins.then_inc(*sig.up())
    eng.wait_ge(*sig.now())


class Core:

    def __init__(self, nc, ctx):
        self.nc, self.ctx = nc, ctx
        self.signals = {}
        self.loads = {}
        self.slabs = 0
        self.ring = self.sb("weight_ring", [P, RING, SK * CW])
        self.w_hi, self.w_lo = (self.sb(f"w_{n}", [P, 2, SK * CW], F32R) for n in ("hi", "lo"))
        self.x_hi, self.x_lo = (self.sb(f"x_{n}", [P, KT, T], F32R) for n in ("hi", "lo"))
        self.ps = ctx.enter_context(nc.psum_tensor("ps", [P, 8, 512], F32))
        self.free = [self.sig("psum_free_0"), self.sig("psum_free_1")]
        self.landed = [ctx.enter_context(nc.semaphore(f"slab_landed_{i}")) for i in range(RING)]
        self.slab_used, self.hi_ready, self.lo_ready = (ctx.enter_context(nc.semaphore(n)) for n in ("slab_used", "slab_high_ready", "slab_low_ready"))
        self.x_hi_ready, self.x_lo_ready = self.sig("x_high_ready"), self.sig("x_low_ready")
        self.factor_ready = self.sig("factor_ready")
        self.tmp = self.sb("tmp", [P, 2, CW // P, T])
        self.act_step = self.sig("act_step")
        self.dve_step = self.sig("dve_step")
        self.pool_step = self.sig("pool_step")

    def sb(self, name, shape, dt=F32):
        return self.ctx.enter_context(self.nc.sbuf_tensor(name, shape, dt))

    def sig(self, name):
        if name not in self.signals:
            self.signals[name] = Signal(self.ctx, self.nc, name)
        return self.signals[name]

    def end(self):
        for s in self.signals.values():
            s.close()


class Load:

    def __init__(self, core, name):
        if name not in core.loads:
            core.loads[name] = [core.ctx.enter_context(core.nc.semaphore(name)), 0]
        self.rec = core.loads[name]

    def start(self, eng, dst, src):
        self.rec[1] += 16
        eng.dma_start(dst, src).then_inc(self.rec[0], 16)

    def all(self):
        return self.rec[0], self.rec[1]


class Stream:

    def __init__(self, core, total, turn):
        self.core = core
        self.turn = turn
        self.n_slabs = total
        self.prefetched = 0
        self.split = 0
        self.start = None

    def reached(self, eng, signal, g, i=None):
        eng.wait_ge(signal, self.start + g + 1 + (0 if i is None else i * self.turn))

    def landed(self, eng, g, i=None):
        n = self.start + g
        eng.wait_ge(self.core.landed[n % RING], 16 * (n // RING + 1) + (0 if i is None else i * (16 * self.turn // RING)))

    def place(self, sp, g, i=None):
        n = (self.start + g) % RING
        dst = self.core.ring[:, n, :]
        sp.dma_start(*self.ends(dst, g, i)).then_inc(self.core.landed[n], 16)

    def prefetch(self, sp, n=None):
        if self.start is None:
            self.start = self.core.slabs
        n = min(RING if n is None else n, self.n_slabs)
        for g in range(self.prefetched, n):
            self.place(sp, g)
        self.prefetched = max(self.prefetched, n)

    def load_slab(self, sp, g, i=None):
        if i is None and g < self.prefetched:
            return
        self.reached(sp, self.core.lo_ready, g - RING, i)
        self.place(sp, g, i)

    def load_next(self, sp, after, n):
        if after is None:
            return
        for g in range(min(n, after.n_slabs)):
            self.reached(sp, self.core.lo_ready, self.n_slabs - RING + g)
            after.place(sp, g)
            after.prefetched = g + 1

    def high(self, act, g, i=None):
        core = self.core
        if g >= 2:
            self.reached(act, core.slab_used, g - 2, i)
        self.landed(act, g, i)
        core.nc.scalar.activation(core.w_hi[:, g % 2, :], core.ring[:, (self.start + g) % RING, :], ACT.Copy)\
            .then_inc(core.hi_ready, 1)

    def low(self, dve, g, i=None):
        core = self.core
        self.reached(dve, core.hi_ready, g, i)
        core.nc.vector.tensor_tensor(core.w_lo[:, g % 2, :], core.ring[:, (self.start + g) % RING, :],
                                     core.w_hi[:, g % 2, :].bitcast(F32), ALU.subtract).then_inc(core.lo_ready, 1)

    def used(self, eng, g, i=None):
        self.reached(eng, self.core.slab_used, g, i)

    def split_next(self, eng, split, after):
        if after is not None:
            if split == "high":
                self.used(eng, self.n_slabs - 2)
                after.high(eng, 0)
            else:
                after.low(eng, 0)

    def product(self, out, w, x, first, last):
        core, mm = self.core, self.core.nc.tensor.matmul
        w_slot, cols = w
        hi, lo = core.w_hi[:, w_slot, cols], core.w_lo[:, w_slot, cols]
        mm(out, hi, core.x_hi[:, x, :], start=first, stop=False)
        mm(out, hi, core.x_lo[:, x, :], start=False, stop=False)
        return mm(out, lo, core.x_hi[:, x, :], start=False, stop=last)

    def begin(self, after):
        if self.start is None:
            self.start = self.core.slabs
        if after is not None:
            after.start = self.start + self.n_slabs

    def finish(self, after):
        self.core.slabs = self.start + self.n_slabs
        if after is not None:
            after.split = 1


class Linear(Stream):

    def __init__(self, core, mats, k, col0, cols, dst, kind="copy", func=ACT.Copy, src=None, x0=0, tail=None):
        self.x0, self.tail = x0, tail
        self.mats, self.dst, self.kind, self.func, self.src_tiles = mats, dst, kind, func, src
        self.kt = k // P
        self.slabs = self.kt // SK
        self.body = BODY // self.slabs
        self.col0 = col0
        self.m = len(mats)
        full, self.last = divmod(cols, CW)
        self.n_chunks = full * self.m
        assert not (self.m == 2 and self.last)
        self.trips = self.n_chunks // self.body
        self.total = self.n_chunks + (1 if self.last else 0)
        self.ahead_trips = self.trips if self.trips * BODY + 2 <= self.total * self.slabs else self.trips - 1
        super().__init__(core, self.total * self.slabs, BODY)

    def width(self, q):
        return CW if q < self.n_chunks else self.last

    def ends(self, dst, g, i):
        q, s = divmod(g, self.slabs)
        rows = self.mats[q % self.m][s * SK * P:(s + 1) * SK * P, :].rearrange("(k p) n -> p k n", p=P)
        col = self.col0 + q // self.m * CW
        n = self.width(q)
        dst = dst.rearrange("p (k n) -> p k n", k=SK)[:, :, 0:n]
        if i is None:
            return dst, rows[:, :, col:col + n]
        return dst, rows[:, :, bass.ds(i * (self.body // self.m * CW) + col, n)]

    def ahead(self, eng, part, epilogue, after):
        split = dict(high=self.high, low=self.low)[part]
        for g in range(self.split, 2):
            split(eng, g)

        def step(g, i):
            if g + 2 < self.n_slabs:
                split(eng, g + 2, i)
            elif g == self.n_slabs - 2:
                self.split_next(eng, part, after)
            if g % self.slabs == self.slabs - 1:
                epilogue(eng, g // self.slabs, i)

        if self.ahead_trips > 0:
            with eng.Fori(0, self.ahead_trips) as i:
                for g in range(BODY):
                    step(g, i)
        for g in range(max(self.ahead_trips, 0) * BODY, self.n_slabs):
            step(g, None)

    def where(self, q, i):
        turn = q // 2 + (0 if i is None else i * (self.body // 2))
        at = q // self.m * CB + (0 if i is None else i * (self.body // self.m * CB))
        return q % 2, turn, at

    def act_epilogue(self, act, q, i):
        core, nc = self.core, self.core.nc
        par, turn, at = self.where(q, i)
        n = self.width(q) // P
        ps = core.ps[:, CB * par:CB * par + n, 0:T]
        free = core.free[par]
        if self.kind == "copy":
            self.used(act, (q + 1) * self.slabs - 1, i)
            dst = self.dst[:, bass.ds(at, n), :] if self.tail is None or q < self.n_chunks else self.tail
            nc.scalar.activation(dst, ps, self.func).then_inc(free.sem, 1)
        elif self.kind == "mul":
            self.used(act, (q + 1) * self.slabs - 1, i)
            act.wait_ge(free.sem, free.base + 1 + turn)
            nc.scalar.activation(core.tmp[:, par, 0:n, :], ps, self.func).then_inc(core.factor_ready.sem, 1)
        elif self.kind == "gate" and q % 2 == 0:
            self.used(act, (q + 1) * self.slabs - 1, i)
            act.wait_ge(core.free[1].sem, core.free[1].base + 1 + turn)
            nc.scalar.activation(core.tmp[:, 0, 0:n, :], ps, ACT.Silu).then_inc(free.sem, 1)

    def dve_epilogue(self, dve, q, i):
        core, nc = self.core, self.core.nc
        if self.kind == "copy" or (self.kind == "gate" and q % 2 == 0):
            return
        par, turn, at = self.where(q, i)
        n = self.width(q) // P
        dst = self.dst[:, bass.ds(at, n), :]
        if self.kind == "mul":
            dve.wait_ge(core.factor_ready.sem, core.factor_ready.base + q + 1 + (0 if i is None else i * self.body))
            nc.vector.tensor_tensor(dst, self.src_tiles[:, bass.ds(at, n), :], core.tmp[:, par, 0:n, :], ALU.mult)\
                .then_inc(core.free[par].sem, 1)
        elif self.kind == "times":
            self.used(dve, (q + 1) * self.slabs - 1, i)
            nc.vector.tensor_tensor(dst, self.src_tiles[:, bass.ds(at, n), :], core.ps[:, CB * par:CB * par + n, 0:T],
                                    ALU.mult).then_inc(core.free[par].sem, 1)
        else:
            dve.wait_ge(core.free[0].sem, core.free[0].base + turn + 2)
            self.used(dve, (q + 1) * self.slabs - 1, i)
            nc.vector.tensor_tensor(dst, core.tmp[:, 0, 0:n, :], core.ps[:, CB:CB + n, 0:T], ALU.mult)\
                .then_inc(core.free[1].sem, 1)

    def run(self, after=None, ahead=RING, pool=None):
        core, nc = self.core, self.core.nc
        slabs, trips = self.slabs, self.trips
        self.begin(after)
        with nc.Block() as block:
            @block.sync
            def _(sp):
                self.prefetch(sp)
                load_trips = (self.n_chunks * slabs - RING) // BODY
                if load_trips > 0:
                    with sp.Fori(0, load_trips) as i:
                        for g in range(RING, RING + BODY):
                            self.load_slab(sp, g, i)
                for g in range(RING + max(load_trips, 0) * BODY, self.n_slabs):
                    self.load_slab(sp, g)
                self.load_next(sp, after, ahead)

            @block.tensor
            def _(pe):
                def chunk(q, i):
                    par, turn, _ = self.where(q, i)
                    pe.wait_ge(core.free[par].sem, core.free[par].base + turn + 1)
                    for s in range(slabs):
                        g = q * slabs + s
                        self.reached(pe, core.lo_ready, g, i)
                        for k in range(SK):
                            kk = s * SK + k
                            first, last = kk == 0, kk == self.kt - 1
                            for m in range(self.width(q) // P):
                                w = (g % 2, slice(k * CW + m * P, k * CW + m * P + P))
                                mm = self.product(core.ps[:, CB * par + m, 0:T], w, self.x0 + kk, first, last)
                        mm.then_inc(core.slab_used, 1)

                if trips:
                    with pe.Fori(0, trips) as i:
                        for q in range(self.body):
                            chunk(q, i)
                for q in range(trips * self.body, self.total):
                    chunk(q, None)

            @block.scalar
            def _(act):
                act.sem_inc(core.free[0].sem, 1)
                act.sem_inc(core.free[1].sem, 1)
                self.ahead(act, "high", self.act_epilogue, after)

            @block.vector
            def _(dve):
                self.ahead(dve, "low", self.dve_epilogue, after)

            if pool is not None:
                block.gpsimd(pool)

        core.free[0].base += (self.total + 1) // 2 + 1
        core.free[1].base += self.total // 2 + 1
        if self.kind == "mul":
            core.factor_ready.base += self.total
        self.finish(after)


class Down(Stream):

    SLABS = FT // 2
    HEAD = 2
    TRIPS = (FT // 2 - 2 * 2 - 2) // 4

    def __init__(self, core, w, x, dst):
        self.w, self.x, self.dst = w, x, dst
        super().__init__(core, 2 * self.SLABS, 4)

    def ends(self, dst, g, i):
        h, s = divmod(g, self.SLABS)
        rows = self.w.rearrange("(k p) n -> p k n", p=P)
        return (dst.rearrange("p (k n) -> p k n", k=2),
                rows[:, bass.ds(2 * s + (0 if i is None else i * 8), 2), h * 1024:(h + 1) * 1024])

    def x_tiles(self, g, i):
        return self.x[:, bass.ds(2 * (g % self.SLABS) + (0 if i is None else i * 8), 2), :]

    def x_high(self, act, g, i=None):
        core = self.core
        core.nc.scalar.activation(core.x_hi[:, 2 * (g % 4):2 * (g % 4) + 2, :], self.x_tiles(g, i), ACT.Copy)\
            .then_inc(core.x_hi_ready.sem, 1)

    def x_low(self, dve, g, i=None):
        core = self.core
        dve.wait_ge(core.x_hi_ready.sem, core.x_hi_ready.base + g + 1 + (0 if i is None else i * 4))
        at = slice(2 * (g % 4), 2 * (g % 4) + 2)
        core.nc.vector.tensor_tensor(core.x_lo[:, at, :], self.x_tiles(g, i), core.x_hi[:, at, :].bitcast(F32), ALU.subtract)\
            .then_inc(core.x_lo_ready.sem, 1)

    def turns(self, eng, step):
        for h in range(2):
            base = h * self.SLABS
            for s in range(self.HEAD):
                step(base + s, None)
            with eng.Fori(0, self.TRIPS) as i:
                for s in range(self.HEAD, self.HEAD + 4):
                    step(base + s, i)
            for s in range(self.HEAD + 4 * self.TRIPS, self.SLABS):
                step(base + s, None)

    def run(self, after=None, ahead=RING):
        core, nc = self.core, self.core.nc
        evacuated = [core.sig("banks_read_0"), core.sig("banks_read_1")]
        last = self.SLABS - 1
        self.begin(after)

        with nc.Block() as block:
            @block.sync
            def _(sp):
                self.prefetch(sp)

                def step(g, i):
                    if g + RING < self.n_slabs:
                        self.reached(sp, core.lo_ready, g, i)
                        self.place(sp, g + RING, i)

                self.turns(sp, step)
                self.load_next(sp, after, ahead)

            @block.tensor
            def _(pe):
                def slab(g, i):
                    self.reached(pe, core.lo_ready, g, i)
                    pe.wait_ge(core.x_lo_ready.sem, core.x_lo_ready.base + g + 1 + (0 if i is None else i * 4))
                    s = g % self.SLABS
                    for k in range(2):
                        for m in range(8):
                            if g == self.SLABS and k == 0 and m % 4 == 0:
                                pe.wait_ge(*evacuated[m // 4].at(1))
                            w = (g % 2, slice(k * 1024 + m * P, k * 1024 + m * P + P))
                            mm = self.product(core.ps[:, m, 0:T], w, 2 * (g % 4) + k, s == 0 and k == 0, s == last and k == 1)
                    mm.then_inc(core.slab_used, 1)

                self.turns(pe, slab)

            def ahead(eng, part, split, x_split, epilogue):
                for g in range(2):
                    x_split(eng, g)
                    if g >= self.split:
                        split(eng, g)
                x_split(eng, 2)

                def step(g, i):
                    if g % self.SLABS == last:
                        self.used(eng, g)
                        epilogue(g // self.SLABS)
                    if g + 2 < self.n_slabs:
                        split(eng, g + 2, i)
                    elif g == self.n_slabs - 2:
                        self.split_next(eng, part, after)
                    if g + 3 < self.n_slabs:
                        x_split(eng, g + 3, i)

                self.turns(eng, step)

            @block.scalar
            def _(act):
                def epilogue(h):
                    nc.scalar.activation(self.dst[:, 8 * h:8 * h + 4, :], core.ps[:, 0:4, 0:T], ACT.Copy)\
                        .then_inc(*evacuated[0].up())

                ahead(act, "high", self.high, self.x_high, epilogue)

            @block.vector
            def _(dve):
                def epilogue(h):
                    nc.vector.tensor_copy(self.dst[:, 8 * h + 4:8 * h + 8, :], core.ps[:, 4:8, 0:T]).then_inc(*evacuated[1].up())

                ahead(dve, "low", self.low, self.x_low, epilogue)

        core.x_hi_ready.base += self.n_slabs
        core.x_lo_ready.base += self.n_slabs
        self.finish(after)
        core.end()


def split_stage(core, sources, add=None):
    nc = core.nc
    high, summed = core.sig("x_high"), core.sig("normed")
    src = [x[:, n:n + 4, :] for x in sources for n in range(0, x.shape[1], 4)]
    with nc.Block() as block:
        @block.scalar
        def _(act):
            for q, x in enumerate(src):
                if add is not None:
                    act.wait_ge(*summed.at(q + 1))
                nc.scalar.activation(core.x_hi[:, 4 * q:4 * q + 4, :], x, ACT.Copy).then_inc(*high.up())

        @block.vector
        def _(dve):
            if add is not None:
                for q, x in enumerate(src):
                    nc.vector.tensor_tensor(x, x, add[:, 4 * q:4 * q + 4, :], ALU.add).then_inc(*summed.up())
            for q, x in enumerate(src):
                dve.wait_ge(*high.at(q + 1))
                nc.vector.tensor_tensor(core.x_lo[:, 4 * q:4 * q + 4, :], x, core.x_hi[:, 4 * q:4 * q + 4, :].bitcast(F32),
                                        ALU.subtract)
    core.end()


LEVELS = 8


def constants():
    i = np.arange(P)
    t = np.arange(T)
    head = i // HD
    c = {}
    c["ident"] = np.eye(P)
    c["head_ones"] = (head[:, None] == head[None, :])
    c["ones"] = np.ones((P, P))

    def rotation(width, rot):
        r = np.zeros((P, P))
        for o in range(P):
            d, half = o % width, rot // 2
            if d < half:
                r[o + half, o] = -1
            elif d < rot:
                r[o - half, o] = 1
        return r

    c["rot_ret"] = rotation(HD, HD)
    c["rot_a"] = rotation(HD, 16)
    c["rot_b"] = rotation(P, 32)
    for g in range(2):
        dup = (i[:, None] == g * HD + i[None, :] % HD).astype(np.float64)
        c[f"dup{g}"] = dup
        c[f"rot_dup{g}"] = dup @ rotation(HD, 16)
    c["eye_pair"] = (i[:, None] % HD == np.arange(HD)[None, :])
    small = list(c)
    inv = (10000.0 ** (-np.arange(HD // 2, dtype=np.float32) / np.float32(HD // 2))).astype(np.float32)
    ang = (t.astype(np.float32)[None, :] * inv[i % (HD // 2)][:, None]).astype(np.float32)
    c["ret_cos_sin"] = np.concatenate([np.cos(ang), np.sin(ang)], 1)
    lg = np.log1p(-np.exp2(-5.0 - np.arange(NH)))
    low = np.tile(t[None, :], (P, 1)) - i[:, None]
    causal = (low >= 0)
    dec = np.where(causal[None], np.exp(lg[:, None, None] * np.maximum(low, 0)[None]), 0) * HD ** -0.5
    c["ret_decay"] = np.concatenate([dec, dec[:, :, :P]], 2).transpose(1, 0, 2).reshape(P, -1)
    cm = causal * HD ** -0.5
    c["mlstm_mask"] = np.concatenate([cm, cm[:, :P]], 1)
    s, u = i[:, None], i[None, :]
    levels = [s == u]
    for l in range(LEVELS - 1):
        b = 1 << l
        levels.append((s // (2 * b) == u // (2 * b)) & (s // b % 2 == 0) & (u // b % 2 == 1))
    c["hgrn_levels"] = np.stack(levels, 1).reshape(P, -1)
    chunk = s // 64 == u // 64
    b8 = s // 8 == u // 8
    c["low8"] = chunk & b8 & (u < s)
    c["up8"] = chunk & b8 & (u > s)
    c["low_off"] = chunk & ~b8 & (u < s)
    c["up_strict"] = chunk & (u > s)
    c["up_incl"] = chunk & (u >= s)
    c["up_incl_neg"] = -1.0 * c["up_incl"]
    c["chunk_starts"] = np.tile((t % 64 != 0)[None, :], (P, 1))
    for tt in range(2):
        q = i[:, None] + tt * P
        k = t[None, :]
        c[f"causal{tt}"] = np.where(k <= q, 0, NEG)
        d = q - k
        n = ((d >= 0) & (d <= 128)) * 1.0 + ((d >= 0) & (d % 4 == 0)) + ((d >= 0) & (d % 16 == 0))
        c[f"dilated{tt}"] = np.where(n > 0, np.log(np.maximum(n, 1)), NEG)
        e = np.arange(15)[None, :] * 16 + 31
        c[f"cmp{tt}"] = np.concatenate([np.where(e <= q, 0, NEG), (e <= q) * 1.0], 1)

    def inv2(width):
        rot = width // 4
        v = (500000.0 ** (-np.arange(0, rot, 2) / rot)).astype(np.float32)
        out = np.zeros(P, np.float32)
        for o in range(P):
            if o % width < rot:
                out[o] = v[o % width % (rot // 2)]
        return out

    c["inv_freq"] = np.stack([inv2(HD), inv2(P)], 1)
    c = {k: np.ascontiguousarray(v, dtype=np.float32) for k, v in c.items()}
    at, n = {}, 0
    for k, v in c.items():
        at[k] = (n, v.shape[1])
        n += v.shape[1]
    return np.concatenate(list(c.values()), 1), at, sum(c[k].shape[1] for k in small), small


N_ARENA = 68
P_AT, MIX_AT, S_AT = 0, 16, 32


LAYER_VECTORS = dict(norm_pre_mix=16, norm_post_mix=16, norm_pre_ffn=16, norm_post_ffn=16, hgrn_norm_w=4, mlstm_conv_w=32,
                     mlstm_conv_b=8, mlstm_norm_w=4, rwkv_mu=14, rwkv_w0=4, rwkv_a0=4, rwkv_k_k=4, rwkv_k_a=4, rwkv_r_k=4,
                     rwkv_ln_w=4, rwkv_ln_b=4, rwkv_v0=4, mlstm_i_bias=1, mlstm_f_bias=1, hgrn_lb_logits=4)
LAYER_N = sum(LAYER_VECTORS.values()) + 1
SECOND_VECTORS = dict(b_ada_2=48, g_pre_2=16, g_post_2=16, c_2=16)
SECOND_N = sum(SECOND_VECTORS.values())


def vector_columns(names):
    at, out = 0, {}
    for name, n in names.items():
        out[name] = (at, n)
        at += n
    return out


class Model(Core):
    def __init__(self, nc, ctx, consts):
        super().__init__(nc, ctx)
        _, self.const_at, n_small, self.small = constants()
        self.consts = consts
        self.h = self.sb("h", [P, KT, T])
        self.spare = self.sb("spare", [P, 8, T])
        self.arena = self.sb("arena", [P, N_ARENA, T])
        self.v_first = self.sb("v_first", [P, GT, T])
        self.par = self.sb("vectors", [P, 2, LAYER_N])
        self.par2 = self.sb("second_vectors", [P, SECOND_N + 48])
        self.bounds = self.sb("bounds", [P, 3, GT])
        self.chunk_w = self.sb("chunk_w", [P, 4, 4])
        self.cs = self.sb("small_consts", [P, n_small])

    def second(self, name):
        o, n = dict(vector_columns(SECOND_VECTORS), ada=(SECOND_N, 48))[name]
        return self.par2[:, o:o + n]

    def const(self, name):
        o, n = self.const_at[name]
        return self.cs[:, o:o + n]

    def const_dram(self, name):
        o, n = self.const_at[name]
        return self.consts[:, o:o + n]

    def a(self, t0, n=1):
        return self.arena[:, t0:t0 + n, :]

    def flat(self, t0, n):
        assert n <= (N_ARENA - t0) * T
        return self.arena[:, :, :].rearrange("p a b -> p (a b)")[:, t0 * T:t0 * T + n]

    def token_major(self):
        ring = self.ring[:, (self.slabs + RING - 1) % RING, :]
        spare = self.spare[:, :, :].rearrange("p a b -> p (a b)")
        return [x[:, n * 1024:(n + 1) * 1024].rearrange("p (a b) -> p a b", a=2) for x in (ring, spare) for n in range(2)]

    def banks(self, b, n):
        return self.ps[:, b:b + n, :].rearrange("p a b -> p (a b)")


def bcast(ap, n):
    return ap.unsqueeze(1).broadcast_to([ap.shape[0], n, ap.shape[-1]])


def rms_stage(m, src, weight, add_to=None, prefetch=None, scratch=S_AT):
    nc = m.nc
    sq = m.a(scratch, KT)
    inv = m.tmp[:, 1, 0, :]
    squares = m.sig("squares")
    sums = m.sig("mean_sums")
    var = m.sig("variance")
    root = m.sig("root")
    normed, high = m.sig("normed"), m.sig("x_high")
    with nc.Block() as block:
        if prefetch is not None:
            @block.sync
            def _(sp):
                prefetch.prefetch(sp)

        @block.scalar
        def _(act):
            for q in range(4):
                nc.scalar.activation(sq[:, 4 * q:4 * q + 4, :], src[:, 4 * q:4 * q + 4, :], ACT.Square)\
                    .then_inc(*squares.up())
            act.wait_ge(*var.at(1))
            nc.scalar.activation(inv, inv, ACT.Sqrt).then_inc(*root.up())
            if add_to is None:
                for q in range(4):
                    act.wait_ge(*normed.at(q + 1))
                    nc.scalar.activation(m.x_hi[:, 4 * q:4 * q + 4, :], sq[:, 4 * q:4 * q + 4, :], ACT.Copy).then_inc(*high.up())

        @block.tensor
        def _(pe):
            for k in range(KT):
                if k % 4 == 0:
                    pe.wait_ge(*squares.at(k // 4 + 1))
                mm = nc.tensor.matmul(m.ps[:, 0, 0:T], m.const("ones"), sq[:, k, :], start=(k == 0), stop=(k == KT - 1))
            mm.then_inc(*sums.up())

        @block.vector
        def _(dve):
            dve.wait_ge(*sums.at(1))
            nc.vector.tensor_scalar(inv, m.ps[:, 0, 0:T], 1.0 / D, EPS, ALU.mult, ALU.add).then_inc(*var.up())
            dve.wait_ge(*root.at(1))
            done(dve, nc.vector.reciprocal(inv, inv), m.dve_step)
            for k in range(KT):
                last = nc.vector.scalar_tensor_tensor(sq[:, k, :], src[:, k, :], weight[:, k:k + 1], inv, ALU.mult, ALU.mult)
                if add_to is None and k % 4 == 3:
                    last.then_inc(*normed.up())
            if add_to is not None:
                done(dve, last, m.dve_step)
                nc.vector.tensor_tensor(add_to[:, :, :], add_to[:, :, :], sq, ALU.add)
                return
            for q in range(4):
                at = slice(4 * q, 4 * q + 4)
                dve.wait_ge(*high.at(q + 1))
                nc.vector.tensor_tensor(m.x_lo[:, at, :], sq[:, at, :], m.x_hi[:, at, :].bitcast(F32), ALU.subtract)
    m.end()


def residual_stage(m, src, weight, next_weight, scratch, shift=None):
    nc = m.nc
    sq = m.a(scratch, KT)
    inv = m.tmp[:, 1, 0:2, :]
    squares, sums, var, root = m.sig("squares"), m.sig("mean_sums"), m.sig("variance"), m.sig("root")
    normed, added, high = m.sig("normed"), m.sig("added"), m.sig("x_high")
    quarters = [slice(4 * q, 4 * q + 4) for q in range(4)]
    with nc.Block() as block:
        @block.scalar
        def _(act):
            for n, x in enumerate((src, m.h)):
                for q, at in enumerate(quarters):
                    if n == 1:
                        act.wait_ge(*added.at(q + 1))
                    nc.scalar.activation(sq[:, at, :], x[:, at, :], ACT.Square).then_inc(*squares.up())
                act.wait_ge(*var.at(n + 1))
                nc.scalar.activation(inv[:, n, :], inv[:, n, :], ACT.Sqrt).then_inc(*root.up())
            for q, at in enumerate(quarters):
                act.wait_ge(*normed.at(4 + q + 1))
                nc.scalar.activation(m.x_hi[:, at, :], sq[:, at, :], ACT.Copy).then_inc(*high.up())

        @block.tensor
        def _(pe):
            for n in range(2):
                for k in range(KT):
                    if k % 4 == 0:
                        pe.wait_ge(*squares.at(4 * n + k // 4 + 1))
                    mm = nc.tensor.matmul(m.ps[:, n, 0:T], m.const("ones"), sq[:, k, :], start=(k == 0), stop=(k == KT - 1))
                mm.then_inc(*sums.up())

        @block.vector
        def _(dve):
            for n, (x, w) in enumerate(((src, weight), (m.h, next_weight))):
                dve.wait_ge(*sums.at(n + 1))
                nc.vector.tensor_scalar(inv[:, n, :], m.ps[:, n, 0:T], 1.0 / D, EPS, ALU.mult, ALU.add).then_inc(*var.up())
                dve.wait_ge(*root.at(n + 1))
                done(dve, nc.vector.reciprocal(inv[:, n, :], inv[:, n, :]), m.dve_step)
                for q, at in enumerate(quarters):
                    for k in range(4 * q, 4 * q + 4):
                        last = nc.vector.scalar_tensor_tensor(sq[:, k, :], x[:, k, :], w[:, k:k + 1], inv[:, n, :], ALU.mult, ALU.mult)
                    if n == 1 and shift is not None:
                        done(dve, last, m.dve_step)
                        for k in range(4 * q, 4 * q + 4):
                            last = nc.vector.tensor_scalar(sq[:, k, :], sq[:, k, :], shift[:, k:k + 1], None, ALU.add)
                    last.then_inc(*normed.up())
                    if n == 0:
                        dve.wait_ge(*normed.now())
                        nc.vector.tensor_tensor(m.h[:, at, :], m.h[:, at, :], sq[:, at, :], ALU.add).then_inc(*added.up())
            for q, at in enumerate(quarters):
                dve.wait_ge(*high.at(q + 1))
                nc.vector.tensor_tensor(m.x_lo[:, at, :], sq[:, at, :], m.x_hi[:, at, :].bitcast(F32), ALU.subtract)
    m.end()


def head_norm_stage(m, o, dst, gate, weight=None, bias=None, bonus=None, eps=EPS, center=False):
    nc = m.nc
    sq = m.flat(S_AT, GT * T)
    inv = m.flat(S_AT + 4, GT * T)
    of = o.rearrange("p a b -> p (a b)")
    squares, sums, var, root = m.sig("squares"), m.sig("mean_sums"), m.sig("variance"), m.sig("root")
    centred, mean = m.sig("centred"), m.sig("head_mean")
    with nc.Block() as block:
        @block.tensor
        def _(pe):
            if center:
                for b in range(2):
                    mm = nc.tensor.matmul(m.ps[:, 2 + b, :], m.const("head_ones"), of[:, b * 512:(b + 1) * 512], start=True, stop=True)
                mm.then_inc(*mean.up())
            pe.wait_ge(*squares.at(1))
            for b in range(2):
                mm = nc.tensor.matmul(m.ps[:, b, :], m.const("head_ones"), sq[:, b * 512:(b + 1) * 512], start=True, stop=True)
            mm.then_inc(*sums.up())

        @block.scalar
        def _(act):
            if center:
                act.wait_ge(*centred.at(1))
            nc.scalar.activation(sq, of, ACT.Square).then_inc(*squares.up())
            act.wait_ge(*var.at(1))
            nc.scalar.activation(inv, inv, ACT.Sqrt).then_inc(*root.up())

        @block.vector
        def _(dve):
            if center:
                dve.wait_ge(*mean.at(1))
                nc.vector.scalar_tensor_tensor(of, m.banks(2, 2), -1.0 / HD, of, ALU.mult, ALU.add).then_inc(*centred.up())
            dve.wait_ge(*sums.at(1))
            nc.vector.tensor_scalar(inv, m.banks(0, 2), 1.0 / HD, eps, ALU.mult, ALU.add).then_inc(*var.up())
            dve.wait_ge(*root.at(1))
            done(dve, nc.vector.reciprocal(inv, inv), m.dve_step)
            done(dve, nc.vector.tensor_tensor(of, of, inv, ALU.mult), m.dve_step)
            if weight is not None:
                for j in range(GT):
                    if bias is None:
                        last = nc.vector.tensor_scalar(o[:, j, :], o[:, j, :], weight[:, j:j + 1], None, ALU.mult)
                    else:
                        last = nc.vector.tensor_scalar(o[:, j, :], o[:, j, :], weight[:, j:j + 1], bias[:, j:j + 1], ALU.mult, ALU.add)
                done(dve, last, m.dve_step)
            if bonus is not None:
                done(dve, nc.vector.tensor_tensor(o, o, bonus, ALU.add), m.dve_step)
            nc.vector.tensor_tensor(dst, o, gate, ALU.mult)
    m.end()


def decayed_product(pe, m, h, k, q, out):
    j, r = h // 2, slice(HD * (h % 2), HD * (h % 2) + HD)
    m.nc.tensor.matmul(out[:, 0:T], k[r, j, 0:P], q[r, j, :], start=True, stop=True)
    return m.nc.tensor.matmul(out[:, T:T + P], k[r, j, P:T], q[r, j, P:T], start=True, stop=True)


def weighted_values(pe, m, h, v, w, out, first=True):
    r = slice(HD * (h % 2), HD * (h % 2) + HD)
    m.nc.tensor.matmul(out[r, 0:T], v(0), w[:, 0:T], start=first, stop=False)
    return m.nc.tensor.matmul(out[r, P:T], v(1), w[:, T:T + P], start=False, stop=True)


def transpose_values(pe, m, v, bank):
    for tt in range(2):
        for j in range(GT):
            mm = m.nc.tensor.transpose(m.ps[:, bank + tt, j * P:(j + 1) * P], v[:, j, tt * P:(tt + 1) * P], m.const("ident"))
    return mm


def retention_stage(m):
    nc = m.nc
    q, k, v, g = (m.a(P_AT + 4 * n, GT) for n in range(4))
    qk = m.flat(P_AT, 8 * T)
    decay = m.flat(S_AT, NH * 384).rearrange("p (h n) -> p h n", h=NH)
    cs = m.flat(S_AT + 12, 2 * T)
    rot = m.flat(S_AT + 14, 8 * T)
    vt = m.flat(S_AT + 22, 2 * GW).rearrange("p (a b) -> p a b", a=2)
    pr = m.flat(S_AT + 26, 2 * 384).rearrange("p (a b) -> p a b", a=2)
    tables = Load(m, "tables_landed")
    rotated, scaled, qk_ready = m.sig("rotated"), m.sig("scaled"), m.sig("qk_ready")
    v_turned, v_ready = m.sig("v_turned"), m.sig("v_ready")
    scores, weights, o_done = m.sig("scores"), m.sig("weights"), m.sig("o_done")
    with nc.Block() as block:
        @block.sync
        def _(sp):
            tables.start(sp, cs, m.const_dram("ret_cos_sin"))
            tables.start(sp, decay, m.const_dram("ret_decay").rearrange("p (h n) -> p h n", h=NH))

        @block.tensor
        def _(pe):
            for b in range(4):
                mm = nc.tensor.matmul(m.ps[:, b, :], m.const("rot_ret"), qk[:, b * 512:(b + 1) * 512], start=True, stop=True)
            mm.then_inc(*rotated.up())
            transpose_values(pe, m, v, 4).then_inc(*v_turned.up())
            pe.wait_ge(*qk_ready.at(1))
            pe.wait_ge(*v_ready.at(1))
            for h in range(NH + 1):
                if h < NH:
                    if h >= 2:
                        pe.wait_ge(*weights.at(h - 1))
                    decayed_product(pe, m, h, k, q, m.ps[:, 6 + h % 2, :]).then_inc(*scores.up())
                if h >= 1:
                    g_ = h - 1
                    pe.wait_ge(*weights.at(h))
                    weighted_values(pe, m, g_, lambda st: vt[:, st, g_ * HD:(g_ + 1) * HD], pr[:, g_ % 2, :],
                                    m.ps[:, g_ // 4, (g_ // 2 % 2) * T:(g_ // 2 % 2) * T + T]).then_inc(*o_done.up())

        @block.gpsimd
        def _(pool):
            pool.wait_ge(*tables.all())
            pool.wait_ge(*rotated.at(1))
            nc.gpsimd.tensor_tensor(m.a(P_AT, 8), m.a(P_AT, 8), bcast(cs[:, 0:T], 8), ALU.mult).then_inc(*scaled.up())

        @block.scalar
        def _(act):
            nc.scalar.activation(g, g, ACT.Silu)
            act.wait_ge(*v_turned.at(1))
            nc.scalar.activation(vt, m.ps[:, 4:6, :], ACT.Copy).then_inc(*v_ready.up())
            act.wait_ge(*o_done.at(NH))
            nc.scalar.activation(q, m.banks(0, 2).rearrange("p (a b) -> p a b", b=T), ACT.Copy)

        @block.vector
        def _(dve):
            dve.wait_ge(*rotated.at(1))
            dve.wait_ge(*tables.all())
            done(dve, nc.vector.tensor_tensor(rot.rearrange("p (a b) -> p a b", b=T),
                                              m.banks(0, 4).rearrange("p (a b) -> p a b", b=T),
                                              bcast(cs[:, T:2 * T], 8), ALU.mult), m.dve_step)
            dve.wait_ge(*scaled.at(1))
            nc.vector.tensor_tensor(qk, qk, rot, ALU.add).then_inc(*qk_ready.up())
            for h in range(NH):
                dve.wait_ge(*scores.at(h + 1))
                if h >= 2:
                    dve.wait_ge(*o_done.at(h - 1))
                nc.vector.tensor_tensor(pr[:, h % 2, :], m.ps[:, 6 + h % 2, 0:384], decay[:, h, :], ALU.mult)\
                    .then_inc(*weights.up())
    m.end()


def log_one_plus_exp(act, m, x, out, log_part):
    done(act, m.nc.scalar.activation(out, x, ACT.Abs), m.act_step)
    done(act, m.nc.scalar.activation(out, out, ACT.Exp, scale=-1.0), m.act_step)
    m.nc.scalar.activation(out, out, ACT.Ln, bias=1.0).then_inc(*log_part.up())


def mlstm_stage(m, par, gates):
    nc = m.nc
    q, k, v, o = (m.a(P_AT + 4 * n, GT) for n in range(4))
    qk = m.a(P_AT, 8)
    acc = m.a(S_AT, 8)
    mask = m.flat(S_AT + 8, 384)
    vt = m.flat(S_AT + 10, 2 * GW).rearrange("p (a b) -> p a b", a=2)
    ex = m.flat(S_AT + 14, NH * 384).rearrange("p (h n) -> p h n", h=NH)
    exf = m.flat(S_AT + 14, NH * 384)
    pr = m.flat(S_AT + 26, 2 * 384).rearrange("p (a b) -> p a b", a=2)
    enm = m.flat(S_AT + 29, GT * T)
    rows = m.flat(S_AT + 33, 3 * T).rearrange("p (a b) -> p a b", b=T)
    log_i, log_f = gates[0:NH, 0, :], gates[0:NH, 1, :]
    lt, cum, gain = (rows[0:NH, n, :] for n in range(3))
    at = m.tmp[:, 0, 0, 0:2 * NH].rearrange("p (a b) -> p a b", a=2)
    run_m = m.tmp[0:NH, 0, 1, :]
    tables = Load(m, "tables_landed")
    moved = Load(m, "rows_moved")
    conv, qk_ready = m.sig("conv_done"), m.sig("qk_ready")
    v_turned, v_ready = m.sig("v_turned"), m.sig("v_ready")
    biased, log_part, den_ready = m.sig("gates_biased"), m.sig("log_part"), m.sig("den_ready")
    gates_ready, gates_spread, gates_back = m.sig("gates_ready"), m.sig("gates_spread"), m.sig("gates_back")
    distance, decay, masked = m.sig("distance"), m.sig("decay_ready"), m.sig("decay_masked")
    scores, weights, o_done, least = m.sig("scores"), m.sig("weights"), m.sig("o_done"), m.sig("least_ready")
    ones = m.const("ones")
    with nc.Block() as block:
        @block.sync
        def _(sp):
            moved.start(sp, log_f, m.tmp[NH:2 * NH, 1, 0, :])
            tables.start(sp, mask, m.const_dram("mlstm_mask"))

        @block.tensor
        def _(pe):
            transpose_values(pe, m, v, 6).then_inc(*v_turned.up())
            pe.wait_ge(*gates_ready.at(1))
            for tt in range(2):
                nc.tensor.transpose(m.ps[:, 4, tt * NH:tt * NH + NH], gain[:, tt * P:(tt + 1) * P], m.const("ident")[0:NH, 0:NH])\
                    .then_inc(*gates_spread.up())
            for h in range(NH):
                mm = nc.tensor.matmul(m.ps[:, h // 2, h % 2 * T:h % 2 * T + T],
                                      m.const("ident")[0:NH, h:h + 1].broadcast_to([NH, P]), run_m, start=True, stop=True)
            mm.then_inc(*gates_spread.up())
            pe.wait_ge(*gates_back.at(1))
            for h in range(NH):
                mm = nc.tensor.matmul(m.ps[HD * (h % 2):HD * (h % 2) + HD, 4 + h // 4, h // 2 % 2 * T:h // 2 % 2 * T + T],
                                      m.const("ident")[0:NH, h:h + 1].broadcast_to([NH, HD]), log_i, start=True, stop=True)
            mm.then_inc(*gates_spread.up())
            pe.wait_ge(*v_ready.at(1))
            pe.wait_ge(*qk_ready.at(1))
            for h in range(NH + 1):
                if h < NH:
                    if h >= 2:
                        pe.wait_ge(*weights.at(h - 1))
                    decayed_product(pe, m, h, k, q, m.ps[:, 6 + h % 2, :]).then_inc(*scores.up())
                if h >= 1:
                    g = h - 1
                    pe.wait_ge(*weights.at(h))
                    half = (g // 2 % 2) * T
                    weighted_values(pe, m, g, lambda st: vt[:, st, g * HD:(g + 1) * HD], pr[:, g % 2, :],
                                    m.ps[:, g // 4, half:half + T])
                    weighted_values(pe, m, g, lambda st: ones[:, 0:HD], pr[:, g % 2, :],
                                    m.ps[:, 2 + g // 4, half:half + T]).then_inc(*o_done.up())

        @block.gpsimd
        def _(pool):
            pool.wait_ge(*tables.all())
            pool.wait_ge(*decay.at(1))
            nc.gpsimd.tensor_tensor(ex, ex, bcast(mask, NH), ALU.mult).then_inc(*masked.up())

        @block.scalar
        def _(act):
            act.wait_ge(*v_turned.at(1))
            nc.scalar.activation(vt, m.ps[:, 6:8, :], ACT.Copy).then_inc(*v_ready.up())
            act.wait_ge(*biased.at(1))
            log_one_plus_exp(act, m, log_f, lt, log_part)
            act.wait_ge(*conv.at(1))
            nc.scalar.activation(qk, acc, ACT.Silu).then_inc(*qk_ready.up())
            act.wait_ge(*distance.at(1))
            nc.scalar.activation(exf, exf, ACT.Exp, scale=-1.0).then_inc(*decay.up())
            act.wait_ge(*gates_spread.at(4))
            nc.scalar.activation(enm, m.banks(4, 2), ACT.Exp, scale=-1.0).then_inc(*least.up())
            nc.scalar.activation(o, o, ACT.Sigmoid)
            act.wait_ge(*o_done.at(NH))
            nc.scalar.activation(acc[:, 0:GT, :], m.banks(2, 2).rearrange("p (a b) -> p a b", b=T), ACT.Abs).then_inc(*den_ready.up())

        @block.vector
        def _(dve):
            step = m.dve_step
            cw, cb = par["conv_w"], par["conv_b"]

            def conv_tap(back):
                for j in range(8):
                    w = cw[:, (3 - back) * 8 + j:(3 - back) * 8 + j + 1]
                    if back == 0:
                        last = nc.vector.tensor_scalar(acc[:, j, :], qk[:, j, :], w, cb[:, j:j + 1], ALU.mult, ALU.add)
                    else:
                        last = nc.vector.scalar_tensor_tensor(acc[:, j, back:T], qk[:, j, 0:T - back], w, acc[:, j, back:T],
                                                              ALU.mult, ALU.add)
                done(dve, last, conv if back == 3 else step)

            conv_tap(0)
            dve.wait_ge(*moved.all())
            nc.vector.tensor_scalar(log_i, log_i, par["i_bias"][0:NH, :], None, ALU.add)
            done(dve, nc.vector.tensor_scalar(log_f, log_f, par["f_bias"][0:NH, :], None, ALU.add), biased)
            conv_tap(1)
            dve.wait_ge(*log_part.at(1))
            done(dve, nc.vector.scalar_tensor_tensor(log_f, log_f, 0.0, lt, ALU.min, ALU.subtract), step)
            done(dve, nc.vector.tensor_tensor_scan(cum, m.const("ones")[0:NH, 0:1].broadcast_to([NH, T]), log_f, 0.0,
                                                   ALU.mult, ALU.add), step)
            done(dve, nc.vector.tensor_tensor(gain, log_i, cum, ALU.subtract), step)
            done(dve, nc.vector.tensor_tensor_scan(run_m, gain, gain, 0.0, ALU.max, ALU.max), step)
            nc.vector.tensor_tensor(log_i, cum, run_m, ALU.add).then_inc(*gates_ready.up())
            conv_tap(2)
            dve.wait_ge(*gates_spread.at(2))
            done(dve, nc.vector.tensor_copy(at, m.ps[:, 4, 0:2 * NH].rearrange("p (a b) -> p a b", a=2)), gates_back)
            conv_tap(3)
            dve.wait_ge(*gates_spread.at(3))
            for h in range(NH):
                bank, half = h // 2, h % 2 * T
                nc.vector.tensor_scalar(ex[:, h, 0:T], m.ps[:, bank, half:half + T], at[:, 0, h:h + 1], 0.0, ALU.subtract, ALU.max)
                last = nc.vector.tensor_scalar(ex[:, h, T:T + P], m.ps[:, bank, half + P:half + T], at[:, 1, h:h + 1], 0.0,
                                               ALU.subtract, ALU.max)
            last.then_inc(*distance.up())
            dve.wait_ge(*masked.at(1))
            for h in range(NH):
                dve.wait_ge(*scores.at(h + 1))
                if h >= 2:
                    dve.wait_ge(*o_done.at(h - 1))
                nc.vector.tensor_tensor(pr[:, h % 2, :], m.ps[:, 6 + h % 2, 0:384], ex[:, h, :], ALU.mult)\
                    .then_inc(*weights.up())
            dve.wait_ge(*o_done.at(NH))
            dve.wait_ge(*least.at(1))
            dve.wait_ge(*den_ready.at(1))
            done(dve, nc.vector.tensor_tensor(enm, m.flat(S_AT, GT * T), enm, ALU.max), step)
            done(dve, nc.vector.reciprocal(enm, enm), step)
            nc.vector.tensor_tensor(m.flat(P_AT, GT * T), m.banks(0, 2), enm, ALU.mult)
    m.end()


def hgrn_stage(m, par, first):
    nc = m.nc
    q, f, v, g = (m.a(P_AT + 4 * n, GT) for n in range(4))
    k = m.a(S_AT, GT)
    levels = m.flat(S_AT + 4, LEVELS * P)
    vt = m.flat(P_AT + 8, 2 * GW).rearrange("p (a b) -> p a b", a=2)
    pr = m.flat(S_AT + 8, 2 * 384).rearrange("p (a b) -> p a b", a=2)
    prod = m.flat(S_AT + 11, LEVELS * T)
    dq, dk = m.a(S_AT + 19, LEVELS), m.a(S_AT + 27, LEVELS)
    lt = m.a(S_AT + 19, GT)
    ls = m.a(S_AT + 23, GT)
    tables = Load(m, "tables_landed")
    v_turned, v_ready, k_gate, log_ready = m.sig("v_turned"), m.sig("v_ready"), m.sig("k_gate"), m.sig("log_f_ready")
    log_part, odds_ready = m.sig("log_part"), m.sig("odds_ready")
    distance, decay, damped_q, damped_k = m.sig("distance"), m.sig("decay_ready"), m.sig("damped_q"), m.sig("damped_k")
    scores, summed, weights, off_done, o_done = (m.sig(n) for n in ("scores", "scores_masked", "weights", "off_diagonal", "o_done"))
    with nc.Block() as block:
        @block.sync
        def _(sp):
            tables.start(sp, levels, m.const_dram("hgrn_levels"))

        @block.tensor
        def _(pe):
            transpose_values(pe, m, v, 0).then_inc(*v_turned.up())
            pe.wait_ge(*v_ready.at(1))
            for h in range(NH + 1):
                if h < NH:
                    j, r = h // 2, slice(HD * (h % 2), HD * (h % 2) + HD)
                    if h % 2 == 0:
                        pe.wait_ge(*damped_q.at(j + 1))
                        pe.wait_ge(*damped_k.at(j + 1))
                    if h >= 1:
                        pe.wait_ge(*summed.at(h))
                    for l in range(LEVELS):
                        qq, kk = (q[r, j, :], k[r, j, :]) if l == 0 else (dq[r, l - 1, :], dk[r, l - 1, :])
                        for tt in range(2):
                            at = (2 * l + tt) * P
                            nc.tensor.matmul(m.ps[:, at // 512, at % 512:at % 512 + P], kk[:, tt * P:(tt + 1) * P],
                                             qq[:, tt * P:(tt + 1) * P], start=True, stop=True)
                    if h >= 2:
                        pe.wait_ge(*off_done.at(h - 1))
                    nc.tensor.matmul(m.ps[:, 4 + h % 2, 0:P], dk[r, LEVELS - 1, 0:P], dq[r, LEVELS - 1, P:T],
                                     start=True, stop=True).then_inc(*scores.up())
                if h >= 1:
                    g_ = h - 1
                    pe.wait_ge(*weights.at(h))
                    pe.wait_ge(*off_done.at(h))
                    weighted_values(pe, m, g_, lambda st: vt[:, st, g_ * HD:(g_ + 1) * HD], pr[:, g_ % 2, :],
                                    m.ps[:, 6 + g_ // 4, (g_ // 2 % 2) * T:(g_ // 2 % 2) * T + T]).then_inc(*o_done.up())

        @block.scalar
        def _(act):
            act.wait_ge(*v_turned.at(1))
            nc.scalar.activation(vt, m.ps[:, 0:2, :], ACT.Copy).then_inc(*v_ready.up())
            nc.scalar.activation(k, f, ACT.Sigmoid, scale=-1.0).then_inc(*k_gate.up())
            nc.scalar.activation(g, g, ACT.Sigmoid)
            nc.scalar.activation(q, q, ACT.Silu).then_inc(*k_gate.up())
            log_one_plus_exp(act, m, f, lt, log_part)
            if not first:
                act.wait_ge(*odds_ready.at(1))
                log_one_plus_exp(act, m, f, lt, log_part)

            def off(h):
                act.wait_ge(*scores.at(h + 1))
                if h >= 2:
                    act.wait_ge(*o_done.at(h - 1))
                nc.scalar.activation(pr[:, h % 2, P:T], m.ps[:, 4 + h % 2, 0:P], ACT.Copy).then_inc(*off_done.up())

            for j in range(GT):
                act.wait_ge(*distance.at(j + 1))
                nc.scalar.activation(dq, dq, ACT.Exp).then_inc(*decay.up())
                nc.scalar.activation(dk, dk, ACT.Exp, scale=-1.0).then_inc(*decay.up())
                off(2 * j)
                off(2 * j + 1)
            act.wait_ge(*o_done.at(NH))
            nc.scalar.activation(q, m.banks(6, 2).rearrange("p (a b) -> p a b", b=T), ACT.Copy)

        @block.gpsimd
        def _(pool):
            for j in range(GT):
                pool.wait_ge(*decay.at(2 * j + 1))
                nc.gpsimd.tensor_tensor(dq[:, 0:5, :], dq[:, 0:5, :], bcast(q[:, j, :], 5), ALU.mult).then_inc(*damped_q.up())

        @block.vector
        def _(dve):
            step = m.dve_step
            dve.wait_ge(*k_gate.at(1))
            if not first:
                for j in range(GT):
                    nc.vector.tensor_scalar(k[:, j, :], k[:, j, :], par["one_less_lb"][:, j:j + 1], None, ALU.mult)
            dve.wait_ge(*log_part.at(1))
            done(dve, nc.vector.scalar_tensor_tensor(f, f, 0.0, lt, ALU.min, ALU.subtract), step)
            if not first:
                for j in range(GT):
                    last = nc.vector.tensor_scalar(f[:, j, :], f[:, j, :], par["log_odds"][:, j:j + 1], None, ALU.add)
                done(dve, last, odds_ready)
                dve.wait_ge(*log_part.at(2))
                done(dve, nc.vector.scalar_tensor_tensor(f, f, 0.0, lt, ALU.max, ALU.add), step)
                for j in range(GT):
                    last = nc.vector.tensor_scalar(f[:, j, :], f[:, j, :], par["log_lb"][:, j:j + 1], None, ALU.add)
                done(dve, last, step)
            for j in range(GT):
                last = nc.vector.tensor_tensor_scan(ls[:, j, :], m.const("ones")[:, 0:1].broadcast_to([P, T]), f[:, j, :], 0.0,
                                                    ALU.mult, ALU.add)
            done(dve, last, step)
            done(dve, nc.vector.tensor_copy(f, ls), step)
            dve.wait_ge(*k_gate.at(2))
            done(dve, nc.vector.tensor_scalar(q, q, HD ** -0.5, None, ALU.mult), step)
            dve.wait_ge(*tables.all())
            for j in range(GT):
                if j:
                    dve.wait_ge(*scores.at(2 * j))
                for l in range(LEVELS):
                    b = 1 << l
                    c = f[:, j, :].rearrange("p (n b) -> p n b", b=2 * b)
                    last = nc.vector.tensor_tensor(dk[:, l, :].rearrange("p (n b) -> p n b", b=2 * b), c,
                                                   c[:, :, b - 1:b].broadcast_to([P, T // (2 * b), 2 * b]), ALU.subtract)
                done(dve, last, step)
                done(dve, nc.vector.tensor_scalar(dq, dk, 0.0, None, ALU.min), step)
                nc.vector.tensor_scalar(dk, dk, 0.0, None, ALU.max).then_inc(*distance.up())
                dve.wait_ge(*decay.at(2 * j + 2))
                nc.vector.tensor_tensor(dq[:, 5:LEVELS, :], dq[:, 5:LEVELS, :], bcast(q[:, j, :], LEVELS - 5), ALU.mult)
                nc.vector.tensor_tensor(dk, dk, bcast(k[:, j, :], LEVELS), ALU.mult).then_inc(*damped_k.up())
                for h in (2 * j, 2 * j + 1):
                    dve.wait_ge(*scores.at(h + 1))
                    done(dve, nc.vector.tensor_tensor(prod.rearrange("p (l a t) -> p l a t", l=LEVELS, a=2),
                                                      m.banks(0, 4).rearrange("p (l a t) -> p l a t", l=LEVELS, a=2),
                                                      levels.rearrange("p (l t) -> p l t", l=LEVELS).unsqueeze(2).broadcast_to([P, LEVELS, 2, P]),
                                                      ALU.mult), summed)
                    if h >= 2:
                        dve.wait_ge(*o_done.at(h - 1))
                    w = pr[:, h % 2, :].rearrange("p (a t) -> p a t", t=P)[:, 0:3:2, :]
                    done(dve, nc.vector.tensor_reduce(w, prod.rearrange("p (l a t) -> p a t l", l=LEVELS, a=2), AX.X, ALU.add),
                         weights)
    m.end()


DECAY_SCALE = 0.6065306597126334
CHUNK = 64
NC = T // CHUNK


def rwkv_inputs_stage(m, par, w, first):
    nc = m.nc
    p = m.a(P_AT, 14)
    r, k, v = (m.a(P_AT + 4 * n, GT) for n in range(3))
    wa_in, g_in = m.arena[:, P_AT + 12, :], m.arena[:, P_AT + 13, :]
    starts = m.arena[:, P_AT + 15, :]
    wa_up, g_up = m.flat(S_AT, GW), m.flat(S_AT + 2, GW)
    v_down, v_up = m.flat(S_AT + 4, P).rearrange("p (a b) -> p a b", a=GT), m.flat(S_AT + 5, GW)
    v_low = m.arena[:, S_AT + 7, :]
    diff = m.a(S_AT + 8, 14)
    log_w, a, kk, sq, cum, big_w, g = (m.a(S_AT + n, GT) for n in (8, 12, 16, 20, 24, 28, 32))
    sig_v = m.tmp[:, 0, :, :]
    bonus = m.a(MIX_AT + 12, GT)
    weights = Load(m, "small_weights_landed")
    shifted, lora_in, lora_out, gates = m.sig("shifted"), m.sig("lora_in"), m.sig("lora_out"), m.sig("lora_gates")
    v_mix, kk_raw, squares, sums, root = m.sig("v_mix"), m.sig("kk_raw"), m.sig("squares"), m.sig("mean_sums"), m.sig("root")
    bonus_in, bonus_sum, cum_ready, exps = m.sig("bonus_in"), m.sig("bonus_sum"), m.sig("cum_ready"), m.sig("decay_ready")

    def tile(b, j):
        return m.ps[:, b + j // 2, j % 2 * T:j % 2 * T + T]

    with nc.Block() as block:
        @block.sync
        def _(sp):
            weights.start(sp, wa_up[0:HD, :], w["w_up"])
            weights.start(sp, wa_up[HD:P, :], w["a_up"])
            weights.start(sp, g_up, w["g_up"])
            weights.start(sp, starts, m.const_dram("chunk_starts"))
            if not first:
                weights.start(sp, v_down, w["v_down"].rearrange("(k p) n -> p k n", p=P))
                weights.start(sp, v_up[0:32, :], w["v_up"])

        @block.tensor
        def _(pe):
            pe.wait_ge(*weights.all())
            pe.wait_ge(*lora_in.at(1))
            for j in range(GT):
                nc.tensor.matmul(tile(0, j), wa_up[0:HD, j * P:(j + 1) * P], wa_in[0:HD, :], start=True, stop=True)
            for j in range(GT):
                nc.tensor.matmul(tile(2, j), wa_up[HD:P, j * P:(j + 1) * P], wa_in[HD:P, :], start=True, stop=True)
            for j in range(GT):
                mm = nc.tensor.matmul(tile(4, j), g_up[:, j * P:(j + 1) * P], g_in, start=True, stop=True)
            if not first:
                for j in range(GT):
                    mm = nc.tensor.matmul(m.ps[0:32, 6, 0:T], v_down[:, j, :], v[:, j, :], start=(j == 0), stop=(j == GT - 1))
            mm.then_inc(*lora_out.up())
            if not first:
                pe.wait_ge(*gates.at(2))
                for j in range(GT):
                    mm = nc.tensor.matmul(tile(6, j), v_up[0:32, j * P:(j + 1) * P], v_low[0:32, :], start=True, stop=True)
                mm.then_inc(*lora_out.up())
            pe.wait_ge(*gates.at(1 if first else 2))
            pe.wait_ge(*squares.at(1))
            for b in range(2):
                mm = nc.tensor.matmul(m.ps[:, b, :], m.const("head_ones"), sq[:, 2 * b:2 * b + 2, :], start=True, stop=True)
            mm.then_inc(*sums.up())
            pe.wait_ge(*bonus_in.at(1))
            for b in range(2):
                mm = nc.tensor.matmul(m.ps[:, 2 + b, :], m.const("head_ones"), sq[:, 2 * b:2 * b + 2, :], start=True, stop=True)
            mm.then_inc(*bonus_sum.up())

        @block.scalar
        def _(act):
            act.wait_ge(*shifted.at(1))
            nc.scalar.activation(wa_in[0:HD, :], wa_in[0:HD, :], ACT.Tanh)
            nc.scalar.activation(g_in, g_in, ACT.Sigmoid).then_inc(*lora_in.up())
            act.wait_ge(*lora_out.at(1))
            for j in range(GT):
                nc.scalar.activation(log_w[:, j, :], tile(0, j), ACT.Sigmoid, bias=par["w0"][:, j:j + 1])
            for j in range(GT):
                nc.scalar.activation(a[:, j, :], tile(2, j), ACT.Sigmoid, bias=par["a0"][:, j:j + 1])
            nc.scalar.activation(g, m.banks(4, 2).rearrange("p (a b) -> p a b", b=T), ACT.Copy).then_inc(*gates.up())
            if not first:
                nc.scalar.activation(v_low[0:32, :], m.ps[0:32, 6, 0:T], ACT.Copy).then_inc(*gates.up())
                act.wait_ge(*lora_out.at(2))
                for j in range(GT):
                    last = nc.scalar.activation(sig_v[:, j, :], tile(6, j), ACT.Sigmoid, bias=par["v0"][:, j:j + 1])
                last.then_inc(*v_mix.up())
            act.wait_ge(*kk_raw.at(1))
            nc.scalar.activation(sq, kk, ACT.Square).then_inc(*squares.up())
            act.wait_ge(*sums.at(1))
            nc.scalar.activation(sq, m.banks(0, 2).rearrange("p (a b) -> p a b", b=T), ACT.Sqrt).then_inc(*root.up())
            act.wait_ge(*cum_ready.at(1))
            nc.scalar.activation(big_w, cum, ACT.Exp).then_inc(*exps.up())
            act.wait_ge(*bonus_sum.at(1))
            nc.scalar.activation(sq, cum, ACT.Exp, scale=-1.0).then_inc(*exps.up())
            nc.scalar.activation(log_w, log_w, ACT.Exp).then_inc(*exps.up())

        @block.vector
        def _(dve):
            step = m.dve_step
            nc.vector.tensor_tensor(diff[:, :, 1:T], p[:, :, 0:T - 1], p[:, :, 1:T], ALU.subtract)
            done(dve, nc.vector.tensor_scalar(diff[:, :, 0:1], p[:, :, 0:1], -1.0, None, ALU.mult), step)
            for j in list(range(12, 14)) + list(range(12)):
                last = nc.vector.scalar_tensor_tensor(p[:, j, :], diff[:, j, :], par["mu"][:, j:j + 1], p[:, j, :], ALU.mult, ALU.add)
            done(dve, last, shifted)
            if first:
                nc.vector.tensor_copy(m.v_first[:, :, :], v)
            dve.wait_ge(*gates.at(1))
            for j in range(GT):
                last = nc.vector.tensor_scalar(kk[:, j, :], k[:, j, :], par["k_k"][:, j:j + 1], None, ALU.mult)
            done(dve, last, kk_raw)
            done(dve, nc.vector.tensor_scalar(log_w, log_w, -DECAY_SCALE, None, ALU.mult), step)
            dve.wait_ge(*weights.all())
            for j in range(GT):
                last = nc.vector.tensor_tensor_scan(cum[:, j, :], starts, log_w[:, j, :], 0.0, ALU.mult, ALU.add)
            done(dve, last, step)
            done(dve, nc.vector.tensor_tensor(log_w, cum, log_w, ALU.subtract), cum_ready)
            dve.wait_ge(*root.at(1))
            done(dve, nc.vector.tensor_scalar(sq, sq, 1e-12, None, ALU.max), step)
            done(dve, nc.vector.reciprocal(sq, sq), step)
            nc.vector.tensor_tensor(kk, kk, sq, ALU.mult)
            t = m.tmp[:, 1, :, :]
            for j in range(GT):
                last = nc.vector.tensor_scalar(t[:, j, :], a[:, j, :], -1.0, par["k_a"][:, j:j + 1], ALU.add, ALU.mult)
            done(dve, last, step)
            done(dve, nc.vector.scalar_tensor_tensor(k, t, 1.0, k, ALU.add, ALU.mult), step)
            for j in range(GT):
                last = nc.vector.scalar_tensor_tensor(sq[:, j, :], r[:, j, :], par["r_k"][:, j:j + 1], k[:, j, :], ALU.mult, ALU.mult)
            last.then_inc(*bonus_in.up())
            nc.vector.tensor_tensor(a, a, kk, ALU.mult)
            if not first:
                dve.wait_ge(*v_mix.at(1))
                done(dve, nc.vector.tensor_tensor(t, m.v_first[:, :, :], v, ALU.subtract), step)
                done(dve, nc.vector.tensor_tensor(t, t, sig_v, ALU.mult), step)
                done(dve, nc.vector.tensor_tensor(v, v, t, ALU.add), step)
            dve.wait_ge(*bonus_sum.at(1))
            done(dve, nc.vector.tensor_tensor(bonus, m.banks(2, 2).rearrange("p (a b) -> p a b", b=T), v, ALU.mult), step)
            dve.wait_ge(*exps.at(1))
            nc.vector.tensor_tensor(r, r, big_w, ALU.mult)
            nc.vector.tensor_copy(m.chunk_w[:, :, :], big_w[:, :, CHUNK - 1:T:CHUNK])
            dve.wait_ge(*exps.at(2))
            nc.vector.tensor_tensor(k, k, sq, ALU.mult)
            nc.vector.tensor_tensor(a, a, sq, ALU.mult)
            dve.wait_ge(*exps.at(3))
            nc.vector.tensor_tensor(kk, kk, log_w, ALU.mult)
    m.end()


def by_head(ap):
    return ap.rearrange("p (h t) n -> p h t n", h=2)


def mask4(ap):
    return ap.unsqueeze(1).unsqueeze(1).broadcast_to([P, 2, 2, P])


def rwkv_solve_stage(m):
    nc = m.nc
    kh, v, bh, kd = m.a(P_AT + 4, GT), m.a(P_AT + 8, GT), m.a(S_AT + 12, GT), m.a(S_AT + 16, GT)
    vt, kht, nbt, kdt = m.token_major()
    masks = m.flat(S_AT, 6 * P).rearrange("p (a b) -> p a b", b=P)
    low8, up8, low_off, up_strict = (masks[:, n, :] for n in range(4))

    def mat(t0):
        return m.flat(t0, 512).rearrange("p (x n) -> p x n", n=P)

    ad, adt, off, akt, a2, a2t = (mat(S_AT + n) for n in (20, 22, 24, 26, 28, 30))
    y, a4 = mat(P_AT + 12), mat(P_AT + 14)
    bt, b_, b2t, b2, b4t, t1 = ad, adt, akt, a2, a2t, y
    x1 = m.tmp[:, 0, 2:4, :].rearrange("p a (x n) -> p (a x) n", n=P)
    rhs = m.tmp[:, 0, 0:2, :].rearrange("p a b -> p (a b)")
    tables = Load(m, "tables_landed")
    turned, token_major, products, evacuated = m.sig("v_turned"), m.sig("v_ready"), m.sig("products"), m.sig("evacuated")

    def item(flat, x):
        hh, tt = divmod(x, 2)
        return flat.rearrange("p (q t h d) -> p q t h d", q=2, t=2, h=2)[:, :, tt, hh, :]

    with nc.Block() as block:
        @block.sync
        def _(sp):
            for n, name in enumerate(("low8", "up8", "low_off", "up_strict", "up_incl", "up_incl_neg")):
                tables.start(sp, masks[:, n, :], m.const_dram(name))

        @block.tensor
        def _(pe):
            for n, x in enumerate((v, kh, bh, kd)):
                transpose_values(pe, m, x, 2 * n).then_inc(*turned.up())
            pe.wait_ge(*token_major.at(4))

            def mats(bank, lhs, right, x, out=None):
                at = m.ps[:, bank, x * P:(x + 1) * P] if out is None else out
                return nc.tensor.matmul(at, lhs, right, start=True, stop=True)

            for j in range(GT):
                n = 10 * j
                if j:
                    pe.wait_ge(*evacuated.at(n))
                for hh in range(2):
                    r = slice(HD * hh, HD * hh + HD)
                    for tt in range(2):
                        x, tk = 2 * hh + tt, slice(tt * P, (tt + 1) * P)
                        for bank, l, rr in ((0, kd, bh), (1, bh, kd), (2, kh, kd)):
                            mm = mats(0, l[r, j, tk], rr[r, j, tk], x, m.ps[:, bank + 3 * hh, tk])
                mm.then_inc(*products.up())
                pe.wait_ge(*evacuated.at(n + 1))
                for x in range(4):
                    hh, tt = divmod(x, 2)
                    mats(0, adt[:, x, :], ad[:, x, :], x)
                    mats(1, ad[:, x, :], adt[:, x, :], x)
                    col = (tt * 2 + hh) * HD
                    head = (2 * j + hh) * HD
                    mm = mats(2, akt[:, x, :], vt[:, tt, head:head + HD], x, m.ps[:, 2, col:col + HD])
                mm.then_inc(*products.up())
                pe.wait_ge(*evacuated.at(n + 2))
                for x in range(4):
                    mats(0, a2t[:, x, :], a2[:, x, :], x)
                    mm = mats(1, a2[:, x, :], y[:, x, :], x)
                mm.then_inc(*products.up())
                pe.wait_ge(*evacuated.at(n + 3))
                for x in range(4):
                    mm = mats(0, a4[:, x, :], x1[:, x, :], x)
                mm.then_inc(*products.up())
                pe.wait_ge(*evacuated.at(n + 4))
                for x in range(4):
                    mats(0, off[:, x, :], t1[:, x, :], x)
                    mats(1, t1[:, x, :], off[:, x, :], x)
                    mm = mats(2, t1[:, x, :], item(rhs, x), x, item(m.ps[:, 2, :], x))
                mm.then_inc(*products.up())
                pe.wait_ge(*evacuated.at(n + 5))
                for x in range(4):
                    mats(0, b_[:, x, :], bt[:, x, :], x)
                    mm = mats(1, bt[:, x, :], b_[:, x, :], x)
                mm.then_inc(*products.up())
                pe.wait_ge(*evacuated.at(n + 6))
                for x in range(4):
                    mm = mats(0, b2[:, x, :], b2t[:, x, :], x)
                mm.then_inc(*products.up())
                z = m.flat(S_AT + 3 + 2 * j, 512)
                for q, l in enumerate((b4t, b2t, bt)):
                    pe.wait_ge(*evacuated.at(n + 7 + q))
                    for x in range(4):
                        mm = mats(0, l[:, x, :], item(z, x), x, item(m.ps[:, 0, :], x))
                    mm.then_inc(*products.up())

        @block.scalar
        def _(act):
            for n, x in enumerate((vt, kht, nbt, kdt)):
                act.wait_ge(*turned.at(n + 1))
                nc.scalar.activation(x, m.ps[:, 2 * n:2 * n + 2, :], ACT.Copy, scale=-1.0 if n == 2 else 1.0)\
                    .then_inc(*token_major.up())

        @block.vector
        def _(dve):
            ps = [m.ps[:, b, :].rearrange("p (x n) -> p x n", n=P) for b in range(3)]
            tt_, cp = nc.vector.tensor_tensor, nc.vector.tensor_copy
            dve.wait_ge(*tables.all())
            dve.wait_ge(*token_major.at(4))
            for j in range(GT):
                n = 10 * j
                z = m.flat(S_AT + 3 + 2 * j, 512)
                dve.wait_ge(*products.at(n + 1))
                for out, bank, mask in ((ad, 0, low8), (off, 0, low_off), (adt, 1, up8), (akt, 2, up_strict)):
                    last = tt_(by_head(out), m.ps[:, bank:bank + 4:3, 0:T].rearrange("p h (t n) -> p h t n", n=P),
                               mask4(mask), ALU.mult)
                done(dve, last, evacuated)
                nc.vector.scalar_tensor_tensor(y, adt, -1.0, bcast(m.const("ident"), 4), ALU.mult, ALU.add)
                cp(rhs[:, 0:T].rearrange("p (t h) -> p t h", t=2), kdt[:, :, j * P:(j + 1) * P])
                dve.wait_ge(*products.at(n + 2))
                cp(a2, ps[0])
                cp(a2t, ps[1])
                done(dve, cp(rhs[:, T:2 * T], m.ps[:, 2, 0:T]), evacuated)
                dve.wait_ge(*products.at(n + 3))
                cp(a4, ps[0])
                done(dve, tt_(x1, y, ps[1], ALU.add), evacuated)
                dve.wait_ge(*products.at(n + 4))
                tt_(t1, x1, ps[0], ALU.add).then_inc(*evacuated.up())
                dve.wait_ge(*products.at(n + 5))
                cp(bt, ps[0])
                cp(b_, ps[1])
                done(dve, cp(z, m.ps[:, 2, :]), evacuated)
                dve.wait_ge(*products.at(n + 6))
                cp(b2t, ps[0])
                done(dve, cp(b2, ps[1]), evacuated)
                dve.wait_ge(*products.at(n + 7))
                cp(b4t, ps[0]).then_inc(*evacuated.up())
                for q in range(3):
                    dve.wait_ge(*products.at(n + 8 + q))
                    done(dve, tt_(z, z, m.ps[:, 0, :], ALU.subtract if q == 2 else ALU.add), evacuated)
    m.end()


def rwkv_output_stage(m):
    nc = m.nc
    rd, kh, bh = m.a(P_AT, GT), m.a(P_AT + 4, GT), m.a(S_AT + 12, GT)
    vt, kht, nbt, _ = m.token_major()
    incl = [m.flat(S_AT, 6 * P)[:, n * P:(n + 1) * P] for n in (4, 5)]
    trans = m.flat(S_AT + 20, 512).rearrange("p (c j n) -> p c j n", c=2, n=HD)
    state = m.flat(S_AT + 22, NC * T).rearrange("p (c j n) -> p c j n", c=NC, n=HD)
    gain = m.tmp[:, 1, 0:3, :].rearrange("p c (j n) -> p c j n", n=HD)
    xt = m.tmp[:, 0, :, :]
    un = m.flat(S_AT + 28, GT * T).rearrange("p (t j h n) -> p t j h n", t=2, j=GT, h=2)
    unf = m.flat(S_AT + 28, GT * T).rearrange("p (t n) -> p t n", t=2)
    low = m.flat(P_AT + 12, 1024).rearrange("p (q x n) -> p q x n", q=2, n=P)
    z = [m.flat(S_AT + 3 + 2 * j, 512).rearrange("p (q t h d) -> p q t h d", q=2, t=2, h=2) for j in range(GT)]
    zt = [m.flat(S_AT + 3 + 2 * j, 512).rearrange("p (q t n) -> p q t n", q=2, t=2) for j in range(GT)]
    chunk_maps, maps_ready, carried, states = m.sig("chunk_maps"), m.sig("maps_ready"), m.sig("carried"), m.sig("states")
    turned, x_ready, u_done, u_ready = m.sig("v_turned"), m.sig("v_ready"), m.sig("u_done"), m.sig("u_ready")
    products, evacuated, o_done = m.sig("products"), m.sig("evacuated"), m.sig("o_done")
    with nc.Block() as block:
        @block.tensor
        def _(pe):
            for c, bank in ((0, 1), (1, 2), (2, 3)):
                tt, rr = c // 2, slice(CHUNK * (c % 2), CHUNK * (c % 2) + CHUNK)
                for h in range(NH):
                    j, hh = divmod(h, 2)
                    o, cols = slice(HD * hh, HD * hh + HD), slice(h * HD, (h + 1) * HD)
                    out = m.ps[o, bank, j * HD:(j + 1) * HD]
                    nc.tensor.matmul(out, kht[rr, tt, cols], vt[rr, tt, cols], start=True, stop=False)
                    mm = nc.tensor.matmul(out, nbt[rr, tt, cols], z[j][rr, 1, tt, hh, :], start=False, stop=True)
                if c:
                    for h in range(NH):
                        j, hh = divmod(h, 2)
                        o, cols = slice(HD * hh, HD * hh + HD), slice(h * HD, (h + 1) * HD)
                        mm = nc.tensor.matmul(m.ps[o, 3 + c, j * HD:(j + 1) * HD], z[j][rr, 0, tt, hh, :], nbt[rr, tt, cols],
                                              start=True, stop=True)
            mm.then_inc(*chunk_maps.up())
            for j in range(GT):
                for tt in range(2):
                    mm = nc.tensor.transpose(m.ps[:, 6 + j // 2, (j % 2 * 2 + tt) * P:(j % 2 * 2 + tt + 1) * P],
                                             zt[j][:, 0, tt, :], m.const("ident"))
            mm.then_inc(*turned.up())
            for c in (1, 2):
                pe.wait_ge(*maps_ready.at(1))
                pe.wait_ge(*states.at(c))
                for hh in range(2):
                    r = slice(HD * hh, HD * hh + HD)
                    for j in range(GT):
                        mm = nc.tensor.matmul(m.ps[r, hh, j * HD:(j + 1) * HD], trans[r, c - 1, j, :], state[r, c, j, :],
                                              start=True, stop=True)
                mm.then_inc(*carried.up())
            pe.wait_ge(*states.at(3))
            pe.wait_ge(*x_ready.at(1))
            for hh in range(2):
                r = slice(HD * hh, HD * hh + HD)
                for c in range(NC):
                    tt, rr = c // 2, slice(CHUNK * (c % 2), CHUNK * (c % 2) + CHUNK)
                    for j in range(GT):
                        mm = nc.tensor.matmul(m.ps[rr, 2 + hh, (j * 2 + tt) * HD:(j * 2 + tt + 1) * HD],
                                              xt[r, j, c * CHUNK:(c + 1) * CHUNK], state[r, c, j, :], start=True, stop=True)
            mm.then_inc(*u_done.up())
            for j in range(GT):
                if j:
                    pe.wait_ge(*evacuated.at(j))
                else:
                    pe.wait_ge(*u_ready.at(1))
                for hh in range(2):
                    r = slice(HD * hh, HD * hh + HD)
                    for tt in range(2):
                        tk = slice(tt * P, (tt + 1) * P)
                        for q, l in enumerate((kh, bh)):
                            mm = nc.tensor.matmul(m.ps[:, 2 * q + hh, tk], l[r, j, tk], rd[r, j, tk], start=True, stop=True)
                mm.then_inc(*products.up())
                pe.wait_ge(*evacuated.at(j + 1))
                for hh in range(2):
                    r, cols = slice(HD * hh, HD * hh + HD), slice((2 * j + hh) * HD, (2 * j + hh + 1) * HD)
                    for tt in range(2):
                        x = 2 * hh + tt
                        at = j % 2 * T + tt * P
                        out = m.ps[r, 6 + j // 2, :]
                        nc.tensor.matmul(out[:, at:at + P], vt[:, tt, cols], low[:, 0, x, :], start=True, stop=False)
                        nc.tensor.matmul(out[:, at:at + P], unf[:, tt, cols], low[:, 1, x, :], start=False, stop=False)
                        for cc in range(2):
                            c = 2 * tt + cc
                            mm = nc.tensor.matmul(out[:, at + cc * CHUNK:at + (cc + 1) * CHUNK], state[r, c, j, :],
                                                  rd[r, j, c * CHUNK:(c + 1) * CHUNK], start=False, stop=(cc == 1))
                mm.then_inc(*o_done.up())

        @block.scalar
        def _(act):
            act.wait_ge(*turned.at(1))
            nc.scalar.activation(xt, m.banks(6, 2).rearrange("p (a b) -> p a b", b=T), ACT.Copy).then_inc(*x_ready.up())
            act.wait_ge(*o_done.at(GT))
            nc.scalar.activation(rd, m.banks(6, 2).rearrange("p (a b) -> p a b", b=T), ACT.Copy)

        @block.vector
        def _(dve):
            tt_ = nc.vector.tensor_tensor
            nc.vector.memset(state[:, 0, :, :], 0.0)
            dve.wait_ge(*chunk_maps.at(1))
            for c in range(3):
                w = m.chunk_w[:, :, c:c + 1].broadcast_to([P, GT, HD])
                to = state[:, 1, :, :] if c == 0 else gain[:, c, :, :]
                last = tt_(to, m.ps[:, 1 + c, 0:GT * HD].rearrange("p (j n) -> p j n", n=HD), w, ALU.mult)
                if c == 0:
                    last.then_inc(*states.up())
            for c in (1, 2):
                last = tt_(trans[:, c - 1, :, :], m.ps[:, 3 + c, 0:GT * HD].rearrange("p (j n) -> p j n", n=HD),
                           bcast(m.const("eye_pair"), GT), ALU.add)
            done(dve, last, maps_ready)
            for c in (1, 2):
                dve.wait_ge(*carried.at(c))
                for hh in range(2):
                    r = slice(HD * hh, HD * hh + HD)
                    last = tt_(state[r, c + 1, :, :], m.ps[r, hh, 0:GT * HD].rearrange("p (j n) -> p j n", n=HD),
                               m.chunk_w[r, :, c:c + 1].broadcast_to([HD, GT, HD]), ALU.mult)
                done(dve, last, m.dve_step)
                tt_(state[:, c + 1, :, :], state[:, c + 1, :, :], gain[:, c, :, :], ALU.add).then_inc(*states.up())
            dve.wait_ge(*u_done.at(1))
            for hh in range(2):
                for j in range(GT):
                    last = tt_(un[:, :, j, hh, :], m.ps[:, 2 + hh, j * 2 * HD:(j + 1) * 2 * HD].rearrange("p (t n) -> p t n", n=HD),
                               z[j][:, 1, :, hh, :], ALU.add)
            last.then_inc(*u_ready.up())
            for j in range(GT):
                dve.wait_ge(*products.at(j + 1))
                if j:
                    dve.wait_ge(*o_done.at(j))
                for q in range(2):
                    last = tt_(by_head(low[:, q, :, :]), m.ps[:, 2 * q:2 * q + 2, 0:T].rearrange("p h (t n) -> p h t n", n=P),
                               mask4(incl[q]), ALU.mult)
                last.then_inc(*evacuated.up())
    m.end()


def lower_bounds_stage(m, logits, one_less, log_odds, log_lb):
    nc = m.nc
    t = m.flat(S_AT, 8 * GT).rearrange("p (a b) -> p a b", b=GT)
    e, top, s, inv, lb = t[:, 0:2, :], t[:, 2, :], t[:, 3, :], t[:, 4, :], t[:, 5, :]
    shifted, exps, bounds, logs = m.sig("shifted"), m.sig("decay_ready"), m.sig("lora_in"), m.sig("log_part")
    with nc.Block() as block:
        @block.scalar
        def _(act):
            act.wait_ge(*shifted.at(1))
            nc.scalar.activation(e, e, ACT.Exp).then_inc(*exps.up())
            act.wait_ge(*bounds.at(1))
            nc.scalar.activation(log_odds, one_less, ACT.Ln)
            nc.scalar.activation(log_lb, s, ACT.Ln).then_inc(*logs.up())

        @block.vector
        def _(dve):
            tt, step = nc.vector.tensor_tensor, m.dve_step
            done(dve, tt(top, logits[0], logits[1], ALU.max), step)
            tt(e[:, 0, :], logits[0], top, ALU.subtract)
            done(dve, tt(e[:, 1, :], logits[1], top, ALU.subtract), shifted)
            dve.wait_ge(*exps.at(1))
            done(dve, tt(s, e[:, 0, :], e[:, 1, :], ALU.add), step)
            done(dve, nc.vector.reciprocal(inv, s), step)
            tt(e[:, 0, :], e[:, 0, :], inv, ALU.mult)
            done(dve, tt(e[:, 1, :], e[:, 1, :], inv, ALU.mult), step)
            done(dve, tt(lb, e[:, 0, :], e[:, 1, :], ALU.add), step)
            done(dve, tt(lb, lb, e[:, 0, :], ALU.subtract), step)
            nc.vector.tensor_scalar(s, lb, 2.0 ** -63, None, ALU.max)
            done(dve, nc.vector.tensor_scalar(one_less, lb, -1.0, 1.0, ALU.mult, ALU.add), bounds)
            dve.wait_ge(*logs.at(1))
            tt(log_odds, log_odds, log_lb, ALU.subtract)
    m.end()


def first_block(m, a, after):
    col = vector_columns(LAYER_VECTORS)

    def vec(layer, name):
        o, n = col[name]
        return m.par[:, layer, o:o + n]

    def proj(layer, c0, n, dst, tail=None):
        return Linear(m, [a["w_in"][layer]], D, c0, n, dst, tail=tail)

    one_less, log_odds, log_lb = (m.bounds[:, n, :] for n in range(3))
    lower_bounds_stage(m, [vec(0, "hgrn_lb_logits"), vec(1, "hgrn_lb_logits")], one_less, log_odds, log_lb)
    starts = (0, 2048, 4096, 6160)
    following = None
    for l in range(2):
        first = l == 0
        ret, hgrn = (proj(l, starts[n], 2048, m.a(P_AT, 16)) for n in range(2))
        mls = proj(l, starts[2], 2048 + P, m.a(P_AT, 16), tail=m.tmp[:, 1, 0:1, :])
        rwk = proj(l, starts[3], 1792, m.a(P_AT, 14))
        if first:
            rms_stage(m, m.h, vec(0, "norm_pre_mix"), prefetch=ret)
        else:
            ret = following
        ret.run(hgrn)
        retention_stage(m)
        head_norm_stage(m, m.a(P_AT, 4), m.a(MIX_AT, 4), m.a(P_AT + 12, 4))
        hgrn.run(mls)
        hgrn_stage(m, dict(one_less_lb=one_less, log_odds=log_odds, log_lb=log_lb), first)
        head_norm_stage(m, m.a(P_AT, 4), m.a(MIX_AT + 4, 4), m.a(P_AT + 12, 4), vec(l, "hgrn_norm_w"))
        mls.run(rwk)
        mlstm_stage(m, dict(conv_w=vec(l, "mlstm_conv_w"), conv_b=vec(l, "mlstm_conv_b"), i_bias=vec(l, "mlstm_i_bias"),
                            f_bias=vec(l, "mlstm_f_bias")), m.tmp[0:NH, 1, 0:2, :])
        head_norm_stage(m, m.a(P_AT, 4), m.a(MIX_AT + 8, 4), m.a(P_AT + 12, 4), vec(l, "mlstm_norm_w"))
        out = Linear(m, [a["w_out"][l]], D, 0, D, m.a(P_AT, 16))
        rwk.run(out, RING - 1)
        small = {n: a["rwkv_" + n][l] for n in ("w_up", "a_up", "g_up")}
        if not first:
            small.update({n: a["rwkv_" + n][0] for n in ("v_down", "v_up")})
        rwkv_inputs_stage(m, {n: vec(l, "rwkv_" + n) for n in ("mu", "w0", "a0", "k_k", "k_a", "r_k", "v0")}, small, first)
        rwkv_solve_stage(m)
        rwkv_output_stage(m)
        head_norm_stage(m, m.a(P_AT, 4), m.a(MIX_AT + 12, 4), m.a(S_AT + 32, 4), vec(l, "rwkv_ln_w"), vec(l, "rwkv_ln_b"), m.a(MIX_AT + 12, 4), 64e-5, True)
        gate_up = Linear(m, [a["w_ffn_gate"][l], a["w_ffn_up"][l]], D, 0, DFF, m.a(0, FT), "gate")
        down = Down(m, a["w_ffn_down"][l], m.a(0, FT), m.a(FT, KT))
        split_stage(m, [m.a(MIX_AT, 16)])
        out.run(gate_up)
        residual_stage(m, m.a(P_AT, 16), vec(l, "norm_post_mix"), vec(l, "norm_pre_ffn"), S_AT)
        ada_program, ada_sums = ada_products(m, a["w_ada_2"][0], l)
        gate_up.run(down, pool=ada_program)
        ada_stage(m, ada_sums, l)
        following = proj(1, 0, 2048, m.a(P_AT, 16)) if first else after
        down.run(following)
        if first:
            residual_stage(m, m.a(FT, KT), vec(0, "norm_post_ffn"), vec(1, "norm_pre_mix"), 0)
        else:
            ada = m.second("ada")
            scales_stage(m, m.second("g_pre_2"), m.second("g_post_2"), ada)
            residual_stage(m, m.a(FT, KT), vec(1, "norm_post_ffn"), ada[:, 16:32], 0, shift=ada[:, 0:16])



G4 = 4
NCMP = 15
BR = ("ks", "kw")


def trig_stage(m, positions):
    nc = m.nc
    pos = m.flat(S_AT, T)
    pos_i = pos.bitcast(I32)
    ang, n, mag = m.a(S_AT + 1, 2), m.a(S_AT + 3, 2), m.a(S_AT + 5, 2)
    freq = m.flat(S_AT + 7, 2)
    trig = m.v_first[:, :, :].rearrange("p (b c) t -> p b c t", b=2)
    load = Load(m, "tables_landed")
    reduced, quarter, mags = m.sig("shifted"), m.sig("lora_in"), m.sig("squares")
    two_pi = 2 * np.pi
    c1 = 6.28125
    c2 = float(np.float32(np.round((two_pi - c1) * 2 ** 21) / 2 ** 21))
    c3 = float(two_pi - c1 - c2)
    magic = 1.5 * 2 ** 23
    with nc.Block() as block:
        @block.sync
        def _(sp):
            load.start(sp, pos_i, positions.broadcast_to([P, T]))
            load.start(sp, freq, m.const_dram("inv_freq"))

        @block.vector
        def _(dve):
            step = m.dve_step
            dve.wait_ge(*load.all())
            done(dve, nc.vector.tensor_copy(mag[:, 0, :], pos_i), step)
            for b in range(2):
                last = nc.vector.tensor_scalar(ang[:, b, :], mag[:, 0, :], freq[:, b:b + 1], None, ALU.mult)
            done(dve, last, step)
            done(dve, nc.vector.tensor_scalar(n, ang, 1.0 / two_pi, magic, ALU.mult, ALU.add), step)
            done(dve, nc.vector.tensor_scalar(n, n, -magic, None, ALU.add), step)
            for c in (c1, c2, c3):
                done(dve, nc.vector.scalar_tensor_tensor(ang, n, -c, ang, ALU.mult, ALU.add), step)
            done(dve, nc.vector.tensor_scalar(ang, ang, 3.1415925, -3.1415925, ALU.min, ALU.max), reduced)
            dve.wait_ge(*mags.at(1))
            nc.vector.tensor_scalar(mag, mag, -1.0, float(np.pi / 2), ALU.mult, ALU.add).then_inc(*quarter.up())

        @block.scalar
        def _(act):
            act.wait_ge(*reduced.at(1))
            nc.scalar.activation(mag, ang, ACT.Abs).then_inc(*mags.up())
            for b in range(2):
                nc.scalar.activation(trig[:, b, 1, :], ang[:, b, :], ACT.Sin)
            act.wait_ge(*quarter.at(1))
            for b in range(2):
                nc.scalar.activation(trig[:, b, 0, :], mag[:, b, :], ACT.Sin)
    m.end()


def ada_products(m, w, half):
    nc = m.nc
    sums = m.flat(FT, 3 * D // 2)
    buf = m.spare[:, :, :].rearrange("p (b a) c -> p b (a c)", b=2).rearrange("p b (k n) -> p b k n", k=2)
    c = m.second("c_2")
    landed = [Load(m, f"ada_weights_landed_{n}") for n in range(2)]
    step = m.pool_step
    rows = w.rearrange("(k p) n -> p k n", p=P)
    pairs, chunks = KT // 2, 3 * D // CW // 2
    count = [x.rec[1] for x in landed]

    def program(pool):
        def fetch(n):
            i, s = divmod(n, pairs)
            i += half * chunks
            landed[n % 2].start(pool, buf[:, n % 2, :, :], rows[:, 2 * s:2 * s + 2, i * CW:(i + 1) * CW])

        fetch(0)
        for n in range(chunks * pairs):
            i, s = divmod(n, pairs)
            out = sums[:, i * CW:(i + 1) * CW]
            if n + 1 < chunks * pairs:
                fetch(n + 1)
            pool.wait_ge(landed[n % 2].rec[0], count[n % 2] + 16 * (n // 2 + 1))
            for k in range(2):
                to = out if s + k == 0 else buf[:, n % 2, k, :]
                ins = nc.gpsimd.tensor_scalar(to, buf[:, n % 2, k, :], c[:, 2 * s + k:2 * s + k + 1], None, ALU.mult)
                ins.then_inc(*step.up())
            pool.wait_ge(*step.now())
            for k in range(0 if s else 1, 2):
                done(pool, nc.gpsimd.tensor_tensor(out, out, buf[:, n % 2, k, :], ALU.add), step)

    return program, sums


def ada_stage(m, sums, half):
    nc = m.nc
    at = slice(24 * half, 24 * half + 24)
    summed = m.sig("v_turned")
    with nc.Block() as block:
        @block.tensor
        def _(pe):
            for k in range(24):
                mm = nc.tensor.matmul(m.ps[:, 0, k:k + 1], sums[:, k * P:(k + 1) * P], m.const("ones")[:, 0:1], start=True, stop=True)
            mm.then_inc(*summed.up())

        @block.vector
        def _(dve):
            dve.wait_ge(*summed.at(1))
            nc.vector.tensor_tensor(m.second("ada")[:, at], m.ps[:, 0, 0:24], m.second("b_ada_2")[:, at], ALU.add)
    m.end()


def scales_stage(m, g_pre, g_post, ada):
    nc = m.nc
    with nc.Block() as block:
        @block.vector
        def _(dve):
            nc.vector.scalar_tensor_tensor(ada[:, 16:32], ada[:, 16:32], 1.0, g_pre, ALU.add, ALU.mult)
            nc.vector.tensor_tensor(ada[:, 32:48], ada[:, 32:48], g_post, ALU.mult)
    m.end()


def compress_stage(m, w, kcd, vc, logits, gates):
    nc = m.nc
    w1 = [m.flat(20, KT * T).rearrange("p (k n) -> p k n", k=KT), m.flat(36, KT * T).rearrange("p (k n) -> p k n", k=KT)]
    x2 = [m.a(52, G4), m.a(56, G4)]
    nb = G4 * NCMP
    blk = [m.flat(60, KT * nb).rearrange("p (j c) -> p j c", j=KT),
           m.tmp[:, 0, :, :].rearrange("p a b -> p (a b)")[:, 0:KT * nb].rearrange("p (j c) -> p j c", j=KT)]
    rest = m.flat(64, 4 * T)
    hid = [rest[:, n * 2 * nb:(n + 1) * 2 * nb].rearrange("p (h c) -> p h c", h=2) for n in range(2)]
    pe_v = [rest[:, 240 + n * KT:240 + (n + 1) * KT] for n in range(2)]
    w2k = rest[:, 280:280 + 2 * P].rearrange("p (h n) -> p h n", h=2)
    w2v = rest[:, 540:540 + 2 * HD].rearrange("p (h n) -> p h n", h=2)
    kc = rest[:, 670:670 + nb]
    moved, weights = Load(m, "rows_moved"), Load(m, "small_weights_landed")
    laid, hidden, hid_ready, out, kc_ready, rotated = (m.sig(n) for n in ("blocks_laid", "products", "gates_ready", "scores",
                                                                           "evacuated", "rotated"))
    gate_logits = m.sig("o_done")
    trig = m.v_first[:, 0:2, :]
    with nc.Block() as block:
        @block.sync
        def _(sp):
            for n in range(2):
                for g in range(G4):
                    src = m.arena[HD * (g % 2):HD * (g % 2) + HD, 8 + 2 * n + g // 2, :]
                    moved.start(sp, x2[n][0:HD, g, :], src)
                    moved.start(sp, x2[n][HD:P, g, 0:T - 1], src[:, 1:T])
            for n, (v1, v2, pe_) in enumerate((("w_ck1_2", "w_ck2_2", "pe_ck_2"), ("w_cv1_2", "w_cv2_2", "pe_cv_2"))):
                weights.start(sp, w1[n], w[v1][0].rearrange("(k p) n -> p k n", p=P))
                weights.start(sp, pe_v[n], w[pe_])
                w2 = w[v2][0].rearrange("(k p) n -> p k n", p=P)
                if n == 0:
                    weights.start(sp, w2k[:, :, 0:HD], w2)
                    weights.start(sp, w2k[:, :, HD:P], w2)
                else:
                    weights.start(sp, w2v, w2)

        @block.vector
        def _(dve):
            dve.wait_ge(*moved.all())
            dve.wait_ge(*weights.all())
            for n in range(2):
                for g in range(G4):
                    view = x2[n][:, g, :].rearrange("p (c b two) -> p b c two", b=8, two=2)
                    for half in range(2):
                        last = nc.vector.tensor_tensor(blk[n][:, half * 8:half * 8 + 8, g * NCMP:(g + 1) * NCMP],
                                                       view[:, :, half:half + NCMP, 0],
                                                       pe_v[n][:, half * 8:half * 8 + 8].unsqueeze(2).broadcast_to([P, 8, NCMP]),
                                                       ALU.add)
            last.then_inc(*laid.up())
            dve.wait_ge(*rotated.at(1))
            cos, sin = (trig[:, n, 31:T:16].unsqueeze(1).broadcast_to([P, G4, NCMP]) for n in range(2))
            kc4, kcd4 = kc.rearrange("p (g c) -> p g c", g=G4), kcd.rearrange("p (g c) -> p g c", g=G4)
            nc.vector.tensor_tensor(kcd4, m.ps[:, 5, 0:nb].rearrange("p (g c) -> p g c", g=G4), sin, ALU.mult)
            done(dve, nc.vector.tensor_tensor(kc4, kc4, cos, ALU.mult), m.dve_step)
            nc.vector.tensor_tensor(kcd, kcd, kc, ALU.add)

        @block.tensor
        def _(pe):
            for tt in range(2):
                mm = nc.tensor.transpose(m.ps[:, 7, tt * 48:tt * 48 + 48], logits[:, tt * P:(tt + 1) * P],
                                         m.const("ident")[0:48, 0:48])
            mm.then_inc(*gate_logits.up())
            pe.wait_ge(*laid.at(1))
            for n in range(2):
                for half in range(2):
                    for j in range(KT):
                        mm = nc.tensor.matmul(m.ps[:, 2 * n + half, 0:nb], w1[n][:, j, half * P:(half + 1) * P], blk[n][:, j, :],
                                              start=(j == 0), stop=(j == KT - 1))
            mm.then_inc(*hidden.up())
            pe.wait_ge(*hid_ready.at(1))
            for half in range(2):
                mm = nc.tensor.matmul(m.ps[:, 4, 0:nb], w2k[:, half, :], hid[0][:, half, :], start=(half == 0), stop=(half == 1))
            mm.then_inc(*out.up())
            for g in range(G4):
                for half in range(2):
                    mm = nc.tensor.matmul(m.ps[0:NCMP, 6, g * HD:(g + 1) * HD], hid[1][:, half, g * NCMP:(g + 1) * NCMP],
                                          w2v[:, half, :], start=(half == 0), stop=(half == 1))
            mm.then_inc(*out.up())
            pe.wait_ge(*kc_ready.at(1))
            nc.tensor.matmul(m.ps[:, 5, 0:nb], m.const("rot_a"), kc, start=True, stop=True).then_inc(*rotated.up())

        @block.scalar
        def _(act):
            act.wait_ge(*hidden.at(1))
            for n in range(2):
                last = nc.scalar.activation(hid[n], m.ps[:, 2 * n:2 * n + 2, 0:nb], ACT.Gelu_apprx_tanh)
            last.then_inc(*hid_ready.up())
            act.wait_ge(*out.at(1))
            nc.scalar.activation(kc, m.ps[:, 4, 0:nb], ACT.Copy).then_inc(*kc_ready.up())
            act.wait_ge(*out.at(2))
            nc.scalar.activation(vc, m.ps[0:NCMP, 6, 0:G4 * HD], ACT.Copy)
            act.wait_ge(*gate_logits.at(1))
            nc.scalar.activation(gates, m.ps[:, 7, 0:96].rearrange("p (a b) -> p a b", a=2), ACT.Sigmoid)
    m.end()


def rope_stage(m, tiles, rot, trig, turn, keys=None):
    nc = m.nc
    cos, sin = trig[:, 0, :], trig[:, 1, :]
    jobs = [("q", t) for t in tiles] + [("k", k) for k in (keys or [])]
    rotated, scaled, ready = m.sig("rotated"), m.sig("scaled"), m.sig("qk_ready")
    turned, stored = m.sig("v_turned"), m.sig("v_ready")
    with nc.Block() as block:
        @block.tensor
        def _(pe):
            for n, (kind, t) in enumerate(jobs):
                bank = n % 4
                if n >= 4:
                    pe.wait_ge(*ready.at(n - 3))
                if kind == "q":
                    mm = nc.tensor.matmul(m.ps[:, bank, 0:T], rot, m.arena[:, t, :], start=True, stop=True)
                else:
                    nc.tensor.matmul(m.ps[:, bank, 0:T], t[2], m.arena[:, t[0], :], start=True, stop=True)
                    mm = nc.tensor.matmul(m.ps[:, bank, T:2 * T], t[1], m.arena[:, t[0], :], start=True, stop=True)
                mm.then_inc(*rotated.up())
            n = 0
            for src, dst in turn:
                width = len(src) * P
                for tt in range(2):
                    if n >= 2:
                        pe.wait_ge(*stored.at(n - 1))
                    for x, t in enumerate(src):
                        mm = nc.tensor.transpose(m.ps[:, 4 + 2 * (n % 2) + x // 4, x % 4 * P:x % 4 * P + P],
                                                 m.arena[:, t, tt * P:(tt + 1) * P], m.const("ident"))
                    mm.then_inc(*turned.up())
                    n += 1

        @block.scalar
        def _(act):
            n = 0
            for src, dst in turn:
                width = len(src) * P
                for tt in range(2):
                    act.wait_ge(*turned.at(n + 1))
                    nc.scalar.activation(dst[:, tt, :], m.banks(4 + 2 * (n % 2), 2)[:, 0:width], ACT.Copy).then_inc(*stored.up())
                    n += 1

        @block.vector
        def _(dve):
            tmp = m.tmp[:, 0, :, :]
            for n, (kind, t) in enumerate(jobs):
                bank = n % 4
                dve.wait_ge(*rotated.at(n + 1))
                part = nc.vector.tensor_tensor(tmp[:, bank, :], m.ps[:, bank, 0:T], sin, ALU.mult)
                x = m.arena[:, t, :] if kind == "q" else t[3]
                src = x if kind == "q" else m.ps[:, bank, T:2 * T]
                done(dve, nc.vector.tensor_tensor(x, src, cos, ALU.mult), m.dve_step)
                done(dve, nc.vector.tensor_tensor(x, x, tmp[:, bank, :], ALU.add), ready)
    m.end()


def attention_stage(m, units, masks, scale, s_at, pt_at, cmp=None):
    nc = m.nc
    N = 4
    sbuf = [m.flat(s_at + 4 * b, N * T) for b in range(2)]
    pts = [m.flat(pt_at + 4 * b, N * T) for b in range(2)]
    small = m.tmp[:, 0, 0, :]
    scores, read, tops, exps, probs, turned, stored, o_done, o_read = (
        m.sig(n) for n in ("scores", "scores_read", "row_max", "exps", "weights", "v_turned", "v_ready", "o_done", "o_read"))
    load = Load(m, "tables_landed")

    def shape(b, L):
        return sbuf[b][:, 0:N * L].rearrange("p (i s) -> p i s", i=N)

    def stats(u, k, n):
        o = (u % 2) * 64 + k
        return small[:, o:o + n]

    def cbuf(u):
        return m.tmp[:, 0, 1, (u % 2) * 32:(u % 2) * 32 + 2 * NCMP].rearrange("p (h c) -> p h c", h=2)

    def cpt(u):
        return m.tmp[0:NCMP, 0, 2, :] if u % 2 == 0 else m.tmp[0:NCMP, 0, 3, :]

    with nc.Block() as block:
        @block.sync
        def _(sp):
            for dst, src in masks["loads"]:
                load.start(sp, dst, src)

        @block.tensor
        def _(pe):
            def score(u):
                tt, items, _, _ = units[u]
                L = (tt + 1) * P
                if u:
                    pe.wait_ge(*read.at(u))
                for x, (q, keys, bank) in enumerate(items):
                    mm = nc.tensor.matmul(m.ps[:, bank, x % 2 * T:x % 2 * T + L], q, keys(L), start=True, stop=True)
                if cmp is not None:
                    for hh in range(2):
                        mm = nc.tensor.matmul(m.ps[:, 2 + hh, 0:NCMP], *cmp["scores"](u, hh), start=True, stop=True)
                mm.then_inc(*scores.up())

            score(0)
            for u, (tt, items, outs, _) in enumerate(units):
                L = (tt + 1) * P
                if u + 1 < len(units):
                    score(u + 1)
                pe.wait_ge(*probs.at(u + 1))
                if u:
                    pe.wait_ge(*stored.at(u))
                for x in range(N):
                    for st in range(tt + 1):
                        c = (x * (tt + 1) + st) * P
                        mm = nc.tensor.transpose(m.ps[:, 4 + c // 512, c % 512:c % 512 + P], shape(u % 2, L)[:, x, st * P:(st + 1) * P],
                                                 m.const("ident"))
                if cmp is not None:
                    for hh in range(2):
                        mm = nc.tensor.transpose(m.ps[0:NCMP, 6, hh * P:(hh + 1) * P], cbuf(u)[:, hh, :], m.const("ident"))
                mm.then_inc(*turned.up())
                pe.wait_ge(*stored.at(u + 1))
                if u:
                    pe.wait_ge(*o_read.at(u))
                for rows, col, parts in outs:
                    todo = [(v(st), pts[u % 2][:, (x * (tt + 1) + st) * P:(x * (tt + 1) + st + 1) * P])
                            for v, x in parts for st in range(tt + 1)]
                    if cmp is not None:
                        hh = rows.start // HD
                        todo.append((cmp["values"](u), cpt(u)[:, hh * P:(hh + 1) * P]))
                    for n, (l, r) in enumerate(todo):
                        mm = nc.tensor.matmul(m.ps[rows, 7, col:col + P], l, r, start=(n == 0), stop=(n == len(todo) - 1))
                mm.then_inc(*o_done.up())

        @block.scalar
        def _(act):
            def finish(u):
                tt, _, _, dst = units[u]
                L = (tt + 1) * P
                act.wait_ge(*turned.at(u + 1))
                if u >= 2:
                    act.wait_ge(*o_done.at(u - 1))
                ins = nc.scalar.activation(pts[u % 2][:, 0:N * L], m.banks(4, 2)[:, 0:N * L], ACT.Copy)
                if cmp is not None:
                    ins = nc.scalar.activation(cpt(u), m.ps[0:NCMP, 6, 0:2 * P], ACT.Copy)
                ins.then_inc(*stored.up())

            def put(u):
                act.wait_ge(*o_done.at(u + 1))
                dst = units[u][3]
                n = dst.shape[1]
                nc.scalar.activation(dst, m.ps[:, 7, 0:n * P].rearrange("p (a b) -> p a b", b=P), ACT.Copy).then_inc(*o_read.up())

            for u, (tt, items, _, _) in enumerate(units):
                L = (tt + 1) * P
                s = shape(u % 2, L)
                act.wait_ge(*tops.at(u + 1))
                for x in range(N):
                    ins = nc.scalar.activation(s[:, x, :], s[:, x, :], ACT.Exp, bias=stats(u, x, 1), accum_out=stats(u, 8 + x, 1))
                if cmp is not None:
                    for hh in range(2):
                        ins = nc.scalar.activation(cbuf(u)[:, hh, :], cbuf(u)[:, hh, :], ACT.Exp, bias=stats(u, 4 + hh, 1))
                ins.then_inc(*exps.up())
                if u:
                    finish(u - 1)
                    put(u - 1)
            finish(len(units) - 1)
            put(len(units) - 1)

        @block.vector
        def _(dve):
            step = m.dve_step
            dve.wait_ge(*load.all())

            def first(u):
                tt, items, _, _ = units[u]
                L = (tt + 1) * P
                s = shape(u % 2, L)
                dve.wait_ge(*scores.at(u + 1))
                if u >= 2:
                    dve.wait_ge(*turned.at(u - 1))
                for b in range(2):
                    ins = nc.vector.scalar_tensor_tensor(s[:, 2 * b:2 * b + 2, :],
                                                         m.ps[:, b, :].rearrange("p (i s) -> p i s", i=2)[:, :, 0:L], scale,
                                                         bcast(masks["add"][tt][:, 0:L], 2), ALU.mult, ALU.add)
                if cmp is not None:
                    ins = nc.vector.scalar_tensor_tensor(cbuf(u), m.ps[:, 2:4, 0:NCMP], scale,
                                                         bcast(cmp["mask"][tt][:, 0:NCMP], 2), ALU.mult, ALU.add)
                done(dve, ins, read)
                ins = nc.vector.tensor_reduce(stats(u, 0, N), s, AX.X, ALU.max, negate=True)
                if cmp is not None:
                    ins = nc.vector.tensor_reduce(stats(u, 4, 2), cbuf(u), AX.X, ALU.max, negate=True)
                ins.then_inc(*tops.up())

            def second(u):
                tt, items, _, _ = units[u]
                L = (tt + 1) * P
                s = shape(u % 2, L)
                dve.wait_ge(*exps.at(u + 1))
                if cmp is not None:
                    c = cbuf(u)
                    done(dve, nc.vector.tensor_tensor(c, c, bcast(cmp["mask"][tt][:, NCMP:2 * NCMP], 2), ALU.mult), step)
                    done(dve, nc.vector.tensor_reduce(stats(u, 12, 2), c, AX.X, ALU.add), step)
                    done(dve, nc.vector.tensor_scalar(stats(u, 12, 2), stats(u, 12, 2), 1.0, None, ALU.max), step)
                k = 6 if cmp is not None else 4
                done(dve, nc.vector.reciprocal(stats(u, 16, k), stats(u, 8, k)), step)
                if cmp is not None:
                    j = u // 2
                    g = cmp["gates"][:, tt, 6 * j:6 * j + 6].rearrange("p (h b) -> p h b", b=3)
                    nc.vector.tensor_tensor(stats(u, 24, 4).rearrange("p (h b) -> p h b", h=2),
                                            stats(u, 16, 4).rearrange("p (h b) -> p h b", h=2), g[:, :, 1:3], ALU.mult)
                    done(dve, nc.vector.tensor_tensor(stats(u, 28, 2), stats(u, 20, 2), g[:, :, 0], ALU.mult), step)
                    nc.vector.tensor_tensor(c, c, stats(u, 28, 2).unsqueeze(2).broadcast_to([P, 2, NCMP]), ALU.mult)
                r = stats(u, 24 if cmp is not None else 16, N)
                nc.vector.tensor_tensor(s, s, r.unsqueeze(2).broadcast_to([P, N, L]), ALU.mult).then_inc(*probs.up())

            first(0)
            for u in range(len(units)):
                if u + 1 < len(units):
                    first(u + 1)
                second(u)
    m.end()


def add_stage(m, dst, x):
    nc = m.nc
    with nc.Block() as block:
        @block.vector
        def _(dve):
            nc.vector.tensor_tensor(dst, dst, x, ALU.add)
    m.end()


def second_projection(m, a):
    return Linear(m, [a["w_in_2"][0]], D, 0, 2560 + P, m.a(0, 20), tail=m.tmp[:, 1, 3:4, :])


def second_block(m, a, qkv):
    w_in = a["w_in_2"][0]
    ada = m.second("ada")

    def proj(c0, n, dst, kind="copy", func=ACT.Copy, src=None, tail=None):
        return Linear(m, [w_in], D, c0, n, dst, kind, func, src, tail=tail)

    trig_stage(m, a["positions_2"])
    oa, ob = m.a(52, 8), m.a(58, 8)
    za = proj(2608, 1024, m.a(0, 8), "mul", ACT.Silu, oa)
    qkv.run(za)
    nb = G4 * NCMP
    kcd, vc = m.tmp[:, 1, 0, 0:nb], m.tmp[0:NCMP, 1, 1, :]
    gates = m.tmp[:, 1, 2, 0:96].rearrange("p (a b) -> p a b", a=2)
    compress_stage(m, a, kcd, vc, m.tmp[0:48, 1, 3, :], gates)
    trig = m.v_first[:, :, :].rearrange("p (b c) t -> p b c t", b=2)
    keys = [(12 + 4 * b + g // 2, m.const(f"dup{g % 2}"), m.const(f"rot_dup{g % 2}"), m.arena[:, 20 + 4 * b + g, :])
            for b in range(2) for g in range(G4)]
    vt = [m.flat(28 + 2 * b, 512).rearrange("p (a b) -> p a b", a=2) for b in range(2)]
    rope_stage(m, range(8), m.const("rot_a"), trig[:, 0, :, :], [((14, 15), vt[0]), ((18, 19), vt[1])], keys)
    units = []
    for j in range(8):
        g = j // 2
        for tt in range(2):
            items, outs = [], []
            for hh in range(2):
                r = slice(HD * hh, HD * hh + HD)
                for b in range(2):
                    items.append((m.arena[r, j, tt * P:(tt + 1) * P], lambda L, r=r, b=b, g=g: m.arena[r, 20 + 4 * b + g, 0:L], hh))
                outs.append((r, 0, [(lambda st, b=b, g=g: vt[b][:, st, g * HD:(g + 1) * HD], 2 * hh + b) for b in range(2)]))
            units.append((tt, items, outs, m.arena[:, 52 + j:53 + j, tt * P:(tt + 1) * P]))
    masks = m.flat(32, 2 * T + 60)
    cmask = [masks[:, 2 * T + 30 * tt:2 * T + 30 * tt + 30] for tt in range(2)]
    add = [masks[:, tt * T:(tt + 1) * T] for tt in range(2)]

    def cmp_scores(u, hh):
        j, tt, r = u // 2, u % 2, slice(HD * hh, HD * hh + HD)
        return m.arena[r, j, tt * P:(tt + 1) * P], kcd[r, j // 2 * NCMP:(j // 2 + 1) * NCMP]

    attention_stage(m, units, dict(add=add, loads=[(x, m.const_dram(f"{n}{tt}")) for n, xs in (("causal", add), ("cmp", cmask))
                                                   for tt, x in enumerate(xs)]),
                    HD ** -0.5, 36, 44,
                    dict(scores=cmp_scores, values=lambda u: vc[:, u // 4 * HD:(u // 4 + 1) * HD], mask=cmask, gates=gates))
    qkv_b = proj(3632, 3072, m.a(16, 24))
    za.run(qkv_b)
    zb = proj(6704, 1024, ob, "mul", ACT.Silu, ob)
    qkv_b.run(zb)
    vtb = m.flat(40, 2048).rearrange("p (a b) -> p a b", a=2)
    rope_stage(m, range(16, 32), m.const("rot_b"), trig[:, 1, :, :], [(tuple(range(32, 40)), vtb)])
    addb = [m.flat(56, T), m.flat(57, T)]
    units = []
    for n in range(2):
        for tt in range(2):
            items = [(m.arena[:, 16 + 4 * n + x, tt * P:(tt + 1) * P], lambda L, h=4 * n + x: m.arena[:, 24 + h, 0:L], x // 2)
                     for x in range(4)]
            outs = [(slice(0, P), x * P, [(lambda st, h=4 * n + x: vtb[:, st, h * P:(h + 1) * P], x)]) for x in range(4)]
            units.append((tt, items, outs, m.arena[:, 58 + 4 * n:62 + 4 * n, tt * P:(tt + 1) * P]))
    attention_stage(m, units, dict(add=addb, loads=[(addb[tt], m.const_dram(f"dilated{tt}")) for tt in range(2)]),
                    P ** -0.5, 48, 32)
    ya, yb = m.a(8, 16), m.a(24, 16)
    ma, mb = proj(7728, D, ya, func=ACT.Sigmoid), proj(9776, D, yb, func=ACT.Sigmoid)
    br_a = Linear(m, [a["w_br_a_2"][0]], 1024, 0, D, ya, "times", src=ya)
    br_b = Linear(m, [a["w_br_b_2"][0]], 1024, 0, D, yb, "times", src=yb, x0=8)
    out = Linear(m, [a["w_out_2"][0]], D, 0, D, m.a(40, 16))
    zb.run(ma)
    ma.run(mb)
    mb.run(br_a)
    split_stage(m, [m.a(0, 8), ob])
    br_a.run(br_b)
    br_b.run(out)
    split_stage(m, [ya], add=yb)
    out.run()
    rms_stage(m, m.a(40, 16), ada[:, 32:48], add_to=m.h, scratch=0)

IN_PLACE = ("w_in", "w_out", "w_ffn_gate", "w_ffn_up", "w_ffn_down", "rwkv_w_up", "rwkv_a_up", "rwkv_g_up",
            "rwkv_v_down", "rwkv_v_up", "w_ada_2", "w_in_2", "w_ck1_2", "w_ck2_2", "w_cv1_2", "w_cv2_2", "w_br_a_2",
            "w_br_b_2", "w_out_2", "positions_2")


def pack(inputs, names, layer=None):
    cols = []
    for name, n in names.items():
        v = np.asarray(inputs[name])
        if layer is not None:
            v = v[0] if v.shape[0] == 1 else v[layer]
        v = v.reshape(-1)
        if v.size < P:
            v = np.concatenate([v, np.zeros(P - v.size, v.dtype)])
        cols.append(v.reshape(n, P).T)
    return np.concatenate(cols, 1)


def feature_major(x):
    return np.ascontiguousarray(x.T.reshape(-1, P, x.shape[0]).transpose(1, 0, 2))


def program(nc, a, out):
    with ExitStack() as ctx:
        m = Model(nc, ctx, a["consts"])
        inputs_landed, out_stored = Load(m, "inputs_landed"), Load(m, "out_stored")
        with nc.Block() as block:
            @block.sync
            def _(sp):
                inputs_landed.start(sp, m.h[:, :, :], a["x"])
                inputs_landed.start(sp, m.par[:, :, 0:LAYER_N - 1], a["layer_vectors"])
                inputs_landed.start(sp, m.par2[:, 0:SECOND_N], a["second_vectors"])
                inputs_landed.start(sp, m.cs[:, :], a["consts"][:, 0:sum(m.const_at[k][1] for k in m.small)])
                sp.wait_ge(*inputs_landed.all())
        qkv = second_projection(m, a)
        first_block(m, a, qkv)
        second_block(m, a, qkv)
        with nc.Block() as block:
            @block.sync
            def _(sp):
                out_stored.start(sp, out, m.h[:, :, :])
                sp.wait_ge(*out_stored.all())


def kernel(**inputs):
    import concourse.bacc as bacc
    from concourse.bass_utils import run_bass_kernel_spmd

    nc = bacc.Bacc("TRN2", target_bir_lowering=False, num_devices=1)
    arrays = {name: np.asarray(inputs[name]) for name in IN_PLACE}
    arrays["x"] = feature_major(np.asarray(inputs["x"])[0])
    arrays["layer_vectors"] = np.stack([pack(inputs, LAYER_VECTORS, layer) for layer in range(2)], 1)
    arrays["second_vectors"] = pack(inputs, SECOND_VECTORS)
    for name in ("pe_ck_2", "pe_cv_2"):
        arrays[name] = np.asarray(inputs[name]).reshape(KT, P).T
    arrays["consts"] = constants()[0]
    arrays = {k: np.ascontiguousarray(v) for k, v in arrays.items()}
    aps = {k: nc.dram_tensor(f"in_{k}", v.shape, mybir.dt.from_np(v.dtype), kind="ExternalInput").ap() for k, v in arrays.items()}
    out = nc.dram_tensor("out", (P, KT, T), F32, kind="ExternalOutput").ap()
    program(nc, aps, out)
    res = run_bass_kernel_spmd(nc, [{f"in_{k}": v for k, v in arrays.items()}], core_ids=[0])
    y = np.asarray(res.results[0]["out"])
    return np.ascontiguousarray(y.transpose(2, 1, 0).reshape(1, T, D))
```
